# Optimizing a Trainium2 kernel written in Bass

```python
import math
import jax, jax.numpy as jnp
from jax import lax
import numpy as np

D_MODEL = 2048
BATCH = 1
SEQ = 256
DEPTH = 1

ATTN_WIDTH = D_MODEL // 2
SSM_WIDTH = D_MODEL - ATTN_WIDTH
HEAD_DIM = 128
N_HEADS = ATTN_WIDTH // HEAD_DIM
ROT_DIM = HEAD_DIM // 4
ROPE_THETA = 500000.0
DILATED_PATTERNS = ((128, 1), (512, 4), (2048, 16))
ATT_BLOCK = 128
SSM_GROUP = 16
N_SSM_GROUPS = SSM_WIDTH // SSM_GROUP
SSM_STATE = 64
DT_MIN = 1e-3
DT_MAX = 1e-1
D_FF = -(-8 * D_MODEL // (3 * 256)) * 256
IN_WIDTH = 3 * ATTN_WIDTH + SSM_WIDTH
RMS_EPS = 1e-6


def _rmsnorm(t, g):
    tf = t.astype(jnp.float32)
    tf = tf * lax.rsqrt(jnp.mean(tf * tf, axis=-1, keepdims=True) + RMS_EPS)
    return (tf * g.astype(jnp.float32)).astype(t.dtype)

def _rotary_tables(seq):
    pos = jnp.arange(seq, dtype=jnp.float32)
    inv_freq = ROPE_THETA ** (-jnp.arange(0, ROT_DIM, 2, dtype=jnp.float32) / ROT_DIM)
    ang = pos[:, None] * inv_freq[None, :]
    return jnp.cos(ang)[None, :, None, :], jnp.sin(ang)[None, :, None, :]

def _apply_partial_rope(t, cos, sin):
    rot, rest = t[..., :ROT_DIM], t[..., ROT_DIM:]
    x1, x2 = rot[..., :ROT_DIM // 2], rot[..., ROT_DIM // 2:]
    return jnp.concatenate([x1 * cos - x2 * sin, x2 * cos + x1 * sin, rest], axis=-1)

def _dilated_band_attention(q, k, v, dilation, band):
    b, s, h, hd = q.shape
    L = s // dilation
    nb = -(-L // ATT_BLOCK)
    pad = nb * ATT_BLOCK - L

    def to_lattice(t):
        return t.reshape(b, L, dilation, h, hd)

    ql = jnp.pad(to_lattice(q), ((0, 0), (0, pad), (0, 0), (0, 0), (0, 0)))
    kl = jnp.pad(to_lattice(k), ((0, 0), (ATT_BLOCK, pad), (0, 0), (0, 0), (0, 0)))
    vl = jnp.pad(to_lattice(v), ((0, 0), (ATT_BLOCK, pad), (0, 0), (0, 0), (0, 0)))
    qb = ql.reshape(b, nb, ATT_BLOCK, dilation, h, hd)
    kb = kl.reshape(b, nb + 1, ATT_BLOCK, dilation, h, hd)
    vb = vl.reshape(b, nb + 1, ATT_BLOCK, dilation, h, hd)
    kw = jnp.concatenate([kb[:, :-1], kb[:, 1:]], axis=2)
    vw = jnp.concatenate([vb[:, :-1], vb[:, 1:]], axis=2)

    scores = jnp.einsum('bnqrhd,bnkrhd->bnrhqk', qb, kw)
    qi = jnp.arange(ATT_BLOCK)[:, None]
    kj = jnp.arange(2 * ATT_BLOCK)[None, :]
    dist = qi - kj + ATT_BLOCK
    key_idx = jnp.arange(nb)[:, None, None] * ATT_BLOCK + kj[None] - ATT_BLOCK
    valid = (dist >= 0) & (dist <= band) & (key_idx >= 0)
    scores = jnp.where(valid[None, :, None, None], scores, -jnp.inf)
    m = jnp.max(scores, axis=-1)
    p = jnp.exp(scores - m[..., None])
    l = jnp.sum(p, axis=-1)
    o = jnp.einsum('bnrhqk,bnkrhd->bnqrhd', p, vw)

    def from_lattice(t):
        tail = t.shape[5:]
        t = t.reshape((b, nb * ATT_BLOCK, dilation, h) + tail)[:, :L]
        return t.reshape((b, s, h) + tail)

    m = jnp.moveaxis(m, -1, 2)
    l = jnp.moveaxis(l, -1, 2)
    return from_lattice(o), from_lattice(m), from_lattice(l)

def _dilated_attention_mixer(q, k, v, cos, sin):
    b, s, _ = q.shape
    split = lambda t: t.astype(jnp.float32).reshape(b, s, N_HEADS, HEAD_DIM)
    qh = _apply_partial_rope(split(q), cos, sin) * (HEAD_DIM ** -0.5)
    kh = _apply_partial_rope(split(k), cos, sin)
    vh = split(v)
    parts = [_dilated_band_attention(qh, kh, vh, dil, win // dil) for win, dil in DILATED_PATTERNS]
    m_all = jnp.max(jnp.stack([m for _, m, _ in parts], axis=0), axis=0)
    num = 0.0
    den = 0.0
    for o_i, m_i, l_i in parts:
        w_i = jnp.exp(m_i - m_all)
        num = num + w_i[..., None] * o_i
        den = den + w_i * l_i
    out = num / den[..., None]
    return out.reshape(b, s, ATTN_WIDTH).astype(q.dtype)

def _s5_mixer(u, a_re, a_im, log_dt, b_re, b_im, c_re, c_im, d_skip, w_glu, b_glu):
    bsz, s, _ = u.shape
    f32 = jnp.float32
    uf = u.astype(f32).reshape(bsz, s, N_SSM_GROUPS, SSM_GROUP)
    lam = lax.complex(a_re.astype(f32), a_im.astype(f32))
    dt = jnp.exp(log_dt.astype(f32))[:, None]
    a_bar = jnp.exp(lam * dt)
    b_mat = lax.complex(b_re.astype(f32), b_im.astype(f32))
    b_bar = ((a_bar - 1.0) / lam)[..., None] * b_mat
    bu = jnp.einsum('bsgp,gnp->bsgn', uf.astype(jnp.complex64), b_bar)
    a_seq = jnp.broadcast_to(a_bar, bu.shape)

    def combine(e1, e2):
        a1, x1 = e1
        a2, x2 = e2
        return a1 * a2, a2 * x1 + x2

    _, states = lax.associative_scan(combine, (a_seq, bu), axis=1)
    c_mat = lax.complex(c_re.astype(f32), c_im.astype(f32))
    y = jnp.einsum('bsgn,gpn->bsgp', states, c_mat).real + d_skip.astype(f32) * uf
    y = jax.nn.gelu(y.reshape(bsz, s, SSM_WIDTH))
    gate = jax.nn.sigmoid(y @ w_glu.astype(f32) + b_glu.astype(f32))
    return (y * gate).astype(u.dtype)

def first_inputs(seed: int = 0) -> dict:
    key = jax.random.key(seed)
    ks = jax.random.split(key, 20)
    f32 = jnp.float32
    nrm = lambda k, shape, scale: jax.random.normal(k, shape, f32) * scale
    x = jax.random.normal(ks[0], (BATCH, SEQ, D_MODEL), f32)
    norm1_g = 1.0 + nrm(ks[1], (DEPTH, D_MODEL), 0.02)
    w_in = nrm(ks[2], (DEPTH, D_MODEL, IN_WIDTH), D_MODEL ** -0.5)
    a_re = -0.5 + nrm(ks[3], (DEPTH, N_SSM_GROUPS, SSM_STATE), 0.01)
    a_im = (math.pi * jnp.arange(SSM_STATE, dtype=f32))[None, None, :] + nrm(ks[4], (DEPTH, N_SSM_GROUPS, SSM_STATE), 0.01)
    log_dt = jax.random.uniform(ks[5], (DEPTH, N_SSM_GROUPS), f32, math.log(DT_MIN), math.log(DT_MAX))
    b_re = nrm(ks[6], (DEPTH, N_SSM_GROUPS, SSM_STATE, SSM_GROUP), (2 * SSM_GROUP) ** -0.5)
    b_im = nrm(ks[7], (DEPTH, N_SSM_GROUPS, SSM_STATE, SSM_GROUP), (2 * SSM_GROUP) ** -0.5)
    c_re = nrm(ks[8], (DEPTH, N_SSM_GROUPS, SSM_GROUP, SSM_STATE), (2 * SSM_STATE) ** -0.5)
    c_im = nrm(ks[9], (DEPTH, N_SSM_GROUPS, SSM_GROUP, SSM_STATE), (2 * SSM_STATE) ** -0.5)
    d_skip = nrm(ks[10], (DEPTH, N_SSM_GROUPS, SSM_GROUP), 1.0)
    w_glu = nrm(ks[11], (DEPTH, SSM_WIDTH, SSM_WIDTH), SSM_WIDTH ** -0.5)
    b_glu = nrm(ks[12], (DEPTH, SSM_WIDTH), 0.02)
    w_out = nrm(ks[13], (DEPTH, ATTN_WIDTH + SSM_WIDTH, D_MODEL), (ATTN_WIDTH + SSM_WIDTH) ** -0.5)
    norm2_g = 1.0 + nrm(ks[14], (DEPTH, D_MODEL), 0.02)
    w_gate = nrm(ks[15], (DEPTH, D_MODEL, D_FF), D_MODEL ** -0.5)
    w_up = nrm(ks[16], (DEPTH, D_MODEL, D_FF), D_MODEL ** -0.5)
    w_down = nrm(ks[17], (DEPTH, D_FF, D_MODEL), D_FF ** -0.5)
    final_g = 1.0 + nrm(ks[18], (D_MODEL,), 0.02)
    return {"x": x, "norm1_g": norm1_g, "w_in": w_in, "a_re": a_re, "a_im": a_im,
            "log_dt": log_dt, "b_re": b_re, "b_im": b_im, "c_re": c_re, "c_im": c_im,
            "d_skip": d_skip, "w_glu": w_glu, "b_glu": b_glu, "w_out": w_out,
            "norm2_g": norm2_g, "w_gate": w_gate, "w_up": w_up, "w_down": w_down,
            "final_g": final_g}

def first_block(x, norm1_g, w_in, a_re, a_im, log_dt, b_re, b_im, c_re, c_im, d_skip,
              w_glu, b_glu, w_out, norm2_g, w_gate, w_up, w_down, final_g):
    _, s, _ = x.shape
    cos, sin = _rotary_tables(s)
    h = x
    for layer in range(DEPTH):
        hn = _rmsnorm(h, norm1_g[layer])
        proj = hn @ w_in[layer]
        q, k, v, u = jnp.split(proj, [ATTN_WIDTH, 2 * ATTN_WIDTH, 3 * ATTN_WIDTH], axis=-1)
        attn_out = _dilated_attention_mixer(q, k, v, cos, sin)
        ssm_out = _s5_mixer(u, a_re[layer], a_im[layer], log_dt[layer], b_re[layer],
                            b_im[layer], c_re[layer], c_im[layer], d_skip[layer],
                            w_glu[layer], b_glu[layer])
        h = h + jnp.concatenate([attn_out, ssm_out], axis=-1) @ w_out[layer]
        hn = _rmsnorm(h, norm2_g[layer])
        h = h + (jax.nn.silu(hn @ w_gate[layer]) * (hn @ w_up[layer])) @ w_down[layer]
    return _rmsnorm(h, final_g)


N_MEM = 256
LRU_WIDTH = D_MODEL
LRU_BLOCKS = 16
LRU_BLOCK_DIM = LRU_WIDTH // LRU_BLOCKS
CONV_WIDTH = 4
LRU_C = 8.0
N_Q_HEADS = 16
N_KV_HEADS = 4
Q_GROUP = N_Q_HEADS // N_KV_HEADS
WINDOW = 128
BLOCK = 128
N_X_HEADS = 4
X_HEAD_DIM = D_MODEL // N_X_HEADS
D_FF_2 = 4 * D_MODEL
N_BRANCH = 3
ROPE_THETA_2 = 10000.0
EPS = 1e-6
SPLITS = (LRU_WIDTH, LRU_WIDTH, N_Q_HEADS * HEAD_DIM, N_KV_HEADS * HEAD_DIM,
          N_KV_HEADS * HEAD_DIM, N_X_HEADS * X_HEAD_DIM, N_BRANCH * D_MODEL)


def rmsnorm(x, g):
    xf = x.astype(jnp.float32)
    var = jnp.mean(xf * xf, axis=-1, keepdims=True)
    return (xf * lax.rsqrt(var + EPS) * g.astype(jnp.float32)).astype(x.dtype)

def rope(t, positions):
    half = t.shape[-1] // 2
    freqs = ROPE_THETA_2 ** (-jnp.arange(half, dtype=jnp.float32) / half)
    ang = positions.astype(jnp.float32)[..., None] * freqs
    cos = jnp.cos(ang)[:, :, None, :]
    sin = jnp.sin(ang)[:, :, None, :]
    tf = t.astype(jnp.float32)
    t1, t2 = tf[..., :half], tf[..., half:]
    return jnp.concatenate([t1 * cos - t2 * sin, t2 * cos + t1 * sin], axis=-1).astype(t.dtype)

def _lin_combine(c1, c2):
    a1, b1 = c1
    a2, b2 = c2
    return a1 * a2, a2 * b1 + b2

def rglru_direction(xc, w_r, b_r, w_i, b_i, lam, reverse):
    B, S, C = xc.shape
    xb = xc.reshape(B, S, LRU_BLOCKS, LRU_BLOCK_DIM)
    r = jax.nn.sigmoid((jnp.einsum('bshi,hij->bshj', xb, w_r) + b_r).reshape(B, S, C).astype(jnp.float32))
    i = jax.nn.sigmoid((jnp.einsum('bshi,hij->bshj', xb, w_i) + b_i).reshape(B, S, C).astype(jnp.float32))
    log_a = -LRU_C * r * jax.nn.softplus(-lam.astype(jnp.float32))
    a = jnp.exp(log_a)
    u = jnp.sqrt(-jnp.expm1(2.0 * log_a)) * (i * xc.astype(jnp.float32))
    if reverse:
        a, u = jnp.flip(a, axis=1), jnp.flip(u, axis=1)
    _, h = lax.associative_scan(_lin_combine, (a, u), axis=1)
    if reverse:
        h = jnp.flip(h, axis=1)
    return h

def local_attention(q, k, v, sink):
    B, S, _, D = q.shape
    nb = S // BLOCK
    qb = q.reshape(B, nb, BLOCK, N_KV_HEADS, Q_GROUP, D)

    def band(t):
        tp = jnp.pad(t, ((0, 0), (BLOCK, BLOCK), (0, 0), (0, 0))).reshape(B, nb + 2, BLOCK, N_KV_HEADS, D)
        return jnp.concatenate([tp[:, :-2], tp[:, 1:-1], tp[:, 2:]], axis=2)

    kb, vb = band(k), band(v)
    s = jnp.einsum('bnqkgd,bnskd->bnkgqs', qb, kb).astype(jnp.float32) * (D ** -0.5)
    blk = jnp.arange(nb, dtype=jnp.int32)[:, None] * BLOCK
    qpos = blk + jnp.arange(BLOCK, dtype=jnp.int32)[None, :]
    kpos = blk - BLOCK + jnp.arange(3 * BLOCK, dtype=jnp.int32)[None, :]
    rel = kpos[:, None, :] - qpos[:, :, None]
    valid = (jnp.abs(rel) <= WINDOW) & (kpos[:, None, :] >= 0) & (kpos[:, None, :] < S)
    s = jnp.where(valid[None, :, None, None], s, -jnp.inf)
    sink_f = sink.astype(jnp.float32).reshape(N_KV_HEADS, Q_GROUP)[None, None, :, :, None, None]
    m = jnp.maximum(jnp.max(s, axis=-1, keepdims=True), sink_f)
    p = jnp.exp(s - m)
    denom = jnp.sum(p, axis=-1, keepdims=True) + jnp.exp(sink_f - m)
    o = jnp.einsum('bnkgqs,bnskd->bnqkgd', (p / denom).astype(v.dtype), vb)
    return o.reshape(B, S, N_Q_HEADS * D)

def memory_attention(q, mk, mv):
    B, S = q.shape[0], q.shape[1]
    s = jnp.einsum('bshd,bmhd->bhsm', q, mk).astype(jnp.float32) * (X_HEAD_DIM ** -0.5)
    p = jax.nn.softmax(s, axis=-1).astype(mv.dtype)
    return jnp.einsum('bhsm,bmhd->bshd', p, mv).reshape(B, S, N_X_HEADS * X_HEAD_DIM)

def hybrid_layer(x, mem, positions, norm_mix_pre, norm_mix_post, norm_mem, w_in, b_gate,
                 conv_w, conv_b, wr_f, br_f, wi_f, bi_f, lam_f, wr_b, br_b, wi_b, bi_b, lam_b,
                 attn_sink, w_mem_kv, w_br_lru, w_br_attn, w_br_mem, w_out,
                 norm_mlp_pre, norm_mlp_post, w_up, w_down):
    B, S, _ = x.shape
    h = rmsnorm(x, norm_mix_pre)
    proj = h @ w_in
    idx = [int(c) for c in np.cumsum(SPLITS)[:-1]]
    xr, gr, q, k, v, qm, gl = jnp.split(proj, idx, axis=-1)

    xc = lax.conv_general_dilated(xr, conv_w[:, None, :], window_strides=(1,),
                                  padding=[(1, CONV_WIDTH - 2)],
                                  dimension_numbers=('NWC', 'WIO', 'NWC'),
                                  feature_group_count=LRU_WIDTH) + conv_b
    h_lru = (rglru_direction(xc, wr_f, br_f, wi_f, bi_f, lam_f, False)
             + rglru_direction(xc, wr_b, br_b, wi_b, bi_b, lam_b, True))
    y_lru = (h_lru * jax.nn.gelu(gr.astype(jnp.float32))).astype(x.dtype)

    q = rope(q.reshape(B, S, N_Q_HEADS, HEAD_DIM), positions)
    k = rope(k.reshape(B, S, N_KV_HEADS, HEAD_DIM), positions)
    v = v.reshape(B, S, N_KV_HEADS, HEAD_DIM)
    y_attn = local_attention(q, k, v, attn_sink)

    mn = rmsnorm(mem, norm_mem)
    mk, mv = jnp.split(mn @ w_mem_kv, 2, axis=-1)
    M = mem.shape[1]
    y_mem = memory_attention(qm.reshape(B, S, N_X_HEADS, X_HEAD_DIM),
                             mk.reshape(B, M, N_X_HEADS, X_HEAD_DIM),
                             mv.reshape(B, M, N_X_HEADS, X_HEAD_DIM))

    gates = jax.nn.sigmoid((gl + b_gate).astype(jnp.float32)).reshape(B, S, N_BRANCH, D_MODEL)
    merged = (gates[:, :, 0] * (y_lru @ w_br_lru).astype(jnp.float32)
              + gates[:, :, 1] * (y_attn @ w_br_attn).astype(jnp.float32)
              + gates[:, :, 2] * (y_mem @ w_br_mem).astype(jnp.float32)).astype(x.dtype)
    x = x + rmsnorm(merged @ w_out, norm_mix_post)

    hm = rmsnorm(x, norm_mlp_pre)
    u = jnp.square(jax.nn.relu(hm @ w_up))
    x = x + rmsnorm(u @ w_down, norm_mlp_post)
    return x

def second_inputs(seed: int = 0) -> dict:
    key = jax.random.key(seed)
    ks = jax.random.split(key, 40)
    L = DEPTH
    f32 = jnp.float32

    def nrm(k, shape, scale):
        return jax.random.normal(k, shape, f32) * scale

    def gain(k, shape):
        return 1.0 + 0.05 * jax.random.normal(k, shape, f32)

    def lam_init(k):
        a0 = jax.random.uniform(k, (L, LRU_WIDTH), f32, minval=0.9, maxval=0.999)
        return jnp.log(a0) - jnp.log1p(-a0)

    n_in = sum(SPLITS)
    bd = LRU_BLOCK_DIM
    return {
        'x': nrm(ks[0], (BATCH, SEQ, D_MODEL), 1.0),
        'mem': nrm(ks[1], (BATCH, N_MEM, D_MODEL), 1.0),
        'positions': (jnp.arange(SEQ, dtype=jnp.int32)[None, :]
                      + jax.random.randint(ks[2], (BATCH, 1), 0, 1024, dtype=jnp.int32)),
        'norm_mix_pre': gain(ks[3], (L, D_MODEL)),
        'norm_mix_post': gain(ks[4], (L, D_MODEL)),
        'norm_mem': gain(ks[5], (L, D_MODEL)),
        'w_in': nrm(ks[6], (L, D_MODEL, n_in), D_MODEL ** -0.5),
        'b_gate': nrm(ks[7], (L, N_BRANCH * D_MODEL), 0.1),
        'conv_w': nrm(ks[8], (L, CONV_WIDTH, LRU_WIDTH), CONV_WIDTH ** -0.5),
        'conv_b': nrm(ks[9], (L, LRU_WIDTH), 0.02),
        'wr_f': nrm(ks[10], (L, LRU_BLOCKS, bd, bd), bd ** -0.5),
        'br_f': nrm(ks[11], (L, LRU_BLOCKS, bd), 0.02),
        'wi_f': nrm(ks[12], (L, LRU_BLOCKS, bd, bd), bd ** -0.5),
        'bi_f': nrm(ks[13], (L, LRU_BLOCKS, bd), 0.02),
        'lam_f': lam_init(ks[14]),
        'wr_b': nrm(ks[15], (L, LRU_BLOCKS, bd, bd), bd ** -0.5),
        'br_b': nrm(ks[16], (L, LRU_BLOCKS, bd), 0.02),
        'wi_b': nrm(ks[17], (L, LRU_BLOCKS, bd, bd), bd ** -0.5),
        'bi_b': nrm(ks[18], (L, LRU_BLOCKS, bd), 0.02),
        'lam_b': lam_init(ks[19]),
        'attn_sink': nrm(ks[20], (L, N_Q_HEADS), 0.5),
        'w_mem_kv': nrm(ks[21], (L, D_MODEL, 2 * N_X_HEADS * X_HEAD_DIM), D_MODEL ** -0.5),
        'w_br_lru': nrm(ks[22], (L, LRU_WIDTH, D_MODEL), LRU_WIDTH ** -0.5),
        'w_br_attn': nrm(ks[23], (L, N_Q_HEADS * HEAD_DIM, D_MODEL), (N_Q_HEADS * HEAD_DIM) ** -0.5),
        'w_br_mem': nrm(ks[24], (L, N_X_HEADS * X_HEAD_DIM, D_MODEL), (N_X_HEADS * X_HEAD_DIM) ** -0.5),
        'w_out': nrm(ks[25], (L, D_MODEL, D_MODEL), D_MODEL ** -0.5),
        'norm_mlp_pre': gain(ks[26], (L, D_MODEL)),
        'norm_mlp_post': gain(ks[27], (L, D_MODEL)),
        'w_up': nrm(ks[28], (L, D_MODEL, D_FF_2), D_MODEL ** -0.5),
        'w_down': nrm(ks[29], (L, D_FF_2, D_MODEL), D_FF_2 ** -0.5),
    }

def second_block(x, mem, positions, norm_mix_pre, norm_mix_post, norm_mem, w_in, b_gate,
              conv_w, conv_b, wr_f, br_f, wi_f, bi_f, lam_f, wr_b, br_b, wi_b, bi_b, lam_b,
              attn_sink, w_mem_kv, w_br_lru, w_br_attn, w_br_mem, w_out,
              norm_mlp_pre, norm_mlp_post, w_up, w_down):
    for l in range(DEPTH):
        x = hybrid_layer(x, mem, positions, norm_mix_pre[l], norm_mix_post[l], norm_mem[l],
                         w_in[l], b_gate[l], conv_w[l], conv_b[l],
                         wr_f[l], br_f[l], wi_f[l], bi_f[l], lam_f[l],
                         wr_b[l], br_b[l], wi_b[l], bi_b[l], lam_b[l],
                         attn_sink[l], w_mem_kv[l], w_br_lru[l], w_br_attn[l], w_br_mem[l],
                         w_out[l], norm_mlp_pre[l], norm_mlp_post[l], w_up[l], w_down[l])
    return x


def setup_inputs(seed=0):
    out = dict(first_inputs(seed))
    for name, value in second_inputs(seed + 1).items():
        if name != "x":
            out[name + "_2"] = value
    return out


def reference(
    x, norm1_g, w_in, a_re, a_im, log_dt, b_re, b_im, c_re, c_im, d_skip, w_glu, b_glu, w_out,
    norm2_g, w_gate, w_up, w_down, final_g, mem_2, positions_2, norm_mix_pre_2, norm_mix_post_2,
    norm_mem_2, w_in_2, b_gate_2, conv_w_2, conv_b_2, wr_f_2, br_f_2, wi_f_2, bi_f_2, lam_f_2,
    wr_b_2, br_b_2, wi_b_2, bi_b_2, lam_b_2, attn_sink_2, w_mem_kv_2, w_br_lru_2, w_br_attn_2,
    w_br_mem_2, w_out_2, norm_mlp_pre_2, norm_mlp_post_2, w_up_2, w_down_2,
):
    x = first_block(
        x, norm1_g, w_in, a_re, a_im, log_dt, b_re, b_im, c_re, c_im, d_skip, w_glu, b_glu,
        w_out, norm2_g, w_gate, w_up, w_down, final_g,
    )
    return second_block(
        x, mem_2, positions_2, norm_mix_pre_2, norm_mix_post_2, norm_mem_2, w_in_2, b_gate_2,
        conv_w_2, conv_b_2, wr_f_2, br_f_2, wi_f_2, bi_f_2, lam_f_2, wr_b_2, br_b_2, wi_b_2,
        bi_b_2, lam_b_2, attn_sink_2, w_mem_kv_2, w_br_lru_2, w_br_attn_2, w_br_mem_2, w_out_2,
        norm_mlp_pre_2, norm_mlp_post_2, w_up_2, w_down_2,
    )


_drawn_inputs = setup_inputs


def setup_inputs(seed=0):
    import zlib

    import numpy as np

    out = dict(_drawn_inputs(seed))
    spreads = {}
    factors = {'norm1_g': 5.095,
     'a_re': 200.0,
     'log_dt': 2.679,
     'b_re': 12.067,
     'b_im': 12.04,
     'c_re': 11.556,
     'c_im': 12.088,
     'b_glu': 8.0,
     'norm2_g': 2.972,
     'norm_mem_2': 6.925,
     'br_f_2': 200.0,
     'bi_f_2': 190.862,
     'br_b_2': 200.0,
     'bi_b_2': 193.295,
     'attn_sink_2': 176.576,
     'conv_b_2': 8.0,
     'wr_f_2': 4.773,
     'wi_f_2': 2.736,
     'wr_b_2': 4.746,
     'wi_b_2': 2.699,
     'a_im': 3.06,
     'w_br_attn_2': 3.225}
    for name, (base, spread) in spreads.items():
        noise = np.random.default_rng([zlib.crc32(name.encode()), seed]).standard_normal(out[name].shape)
        drawn = base * np.exp(spread * noise) if base else spread * noise
        out[name] = __import__('jax').numpy.asarray(drawn.astype(out[name].dtype))
    for name, factor in factors.items():
        out[name] = (out[name] * factor).astype(out[name].dtype)
    return out
```

```python
import math
from contextlib import ExitStack

import numpy as np
import concourse.bass as bass
from concourse import mybir

D = 2048
T = 256
P = 128
KT = D // P
AW = 1024
HD = 128
H1 = AW // HD
HEADS = H1 + D // HD
STATES = 64 * 64
PAIRS = STATES // P
UT = AW // P
FF1, FF2 = 5632, 8192
GC = 256
UNITS = 4
SLOTS = 8
RING = 4
LAG = 2
M_SCALE = 512 ** -0.5
EPS = 1e-6
SCALE = float(HD) ** -0.5
MAGIC = 12582912.0
TWO_PI = 6.283185
NEG = -1e30

VEC = {}
for _name, _n in (("norm1", 16), ("norm2", 16), ("final", 16), ("mem", 16), ("mix_pre", 16), ("mix_post", 16),
                  ("mlp_pre", 16), ("mlp_post", 16), ("b_glu", 8), ("d_skip", 8), ("a_re", 32), ("a_im", 32),
                  ("log_dt", 32), ("b_gate", 48), ("conv_w", 64), ("conv_b", 16), ("br", 32), ("bi", 32),
                  ("lam", 32), ("sink", 16), ("freq", 1)):
    VEC[_name] = (sum(n for _, n in VEC.values()), _n)
NVEC = sum(n for _, n in VEC.values())


class At:

    def __init__(self, reg, k, c):
        self.reg, self.k, self.c = reg, k, c

    def __call__(self, mul=1, add=0):
        c = mul * self.c + add
        if self.reg is None:
            return c
        e = self.reg if mul * self.k == 1 else self.reg * (mul * self.k)
        return e + c if c > 0 else e - (-c) if c < 0 else e

    def plus(self, n):
        return At(self.reg, self.k, self.c + n)

    def before(self):
        return self.plus(-1)

    def times(self, n):
        return At(self.reg, self.k * n, self.c * n)

    def halved(self):
        return At(self.reg, self.k // 2, self.c // 2)


def wait(eng, sem, value):
    if not isinstance(value, int) or value > 0:
        eng.wait_ge(sem, value)


def ix(value, n=1):
    return slice(value, value + n) if isinstance(value, int) else bass.ds(value, n)


class Gemm:

    bodies_before = 0

    def __init__(self, w, bodies, unroll=1):
        self.w, self.bodies, self.unroll = w, bodies, unroll
        self.kt = w.shape[3] // GC
        self.first = Gemm.bodies_before
        Gemm.bodies_before += bodies

    def stretches(self, eng, peel):
        u = self.unroll
        for c in range(u if peel else 0):
            yield At(None, 0, c), c
        rest = self.bodies // u - (1 if peel else 0)
        start = 1 if peel else 0
        if rest == 1:
            for c in range(u):
                yield At(None, 0, start * u + c), c
        elif rest > 1:
            with eng.Fori(start, self.bodies // u) as r:
                for c in range(u):
                    yield At(r, u, c), c


def program(nc, A, out):
    f32, f32r, i32 = mybir.dt.float32, mybir.dt.float32r, mybir.dt.int32
    ACT, ALU, AX = mybir.ActivationFunctionType, mybir.AluOpType, mybir.AxisListType
    Gemm.bodies_before = 0

    in_u = Gemm(A["w_in_u"], 2, unroll=2)
    in_qk = Gemm(A["w_in_qk"], 4, unroll=2)
    in_v = Gemm(A["w_in_v"], 2, unroll=2)
    mem_k = Gemm(A["w_mem_k"], 4, unroll=2)
    mem_v = Gemm(A["w_mem_v"], 4, unroll=2)
    out_attn = Gemm(A["w_out_attn"], 4, unroll=4)
    glu = Gemm(A["w_glu"], 2, unroll=2)
    out_ssm = Gemm(A["w_out_ssm"], 4)
    ffn1 = []
    for c in range(3):
        up, down = A[f"w_gu{c}"], A[f"w_dn{c}"]
        ffn1.append((Gemm(up, up.shape[0] // 2), Gemm(down, down.shape[0] // 2)))
    lru_in, lru_gate = Gemm(A["w_lru_in"], 4), Gemm(A["w_lru_gate"], 4)
    in_q2 = Gemm(A["w_in_q2"], 4)
    in_k2, in_v2 = Gemm(A["w_in_k2"], 1), Gemm(A["w_in_v2"], 1)
    in_qm = Gemm(A["w_in_qm"], 4)
    branches = [Gemm(A[f"w_branch{n}"], 8, unroll=(1, 2, 2, 1)[n + 1]) for n in range(3)]
    out2 = Gemm(A["w_out2"], 4)
    ffn2 = [(Gemm(A[f"w_up{c}"], 4), Gemm(A[f"w_down{c}"], 4)) for c in range(4)]
    stages = [in_u, in_qk, in_v, mem_k, mem_v, out_attn, glu, out_ssm] + [g for pair in ffn1 for g in pair]
    stages += [lru_in, lru_gate, in_q2, in_k2, in_v2, in_qm] + branches + [out2] + [g for pair in ffn2 for g in pair]

    ctx = ExitStack()
    with ctx:
        def sb(name, shape, dt=f32):
            return ctx.enter_context(nc.sbuf_tensor(name, shape, dt))

        def sem(name):
            return ctx.enter_context(nc.semaphore(name))

        RAW = sb("weights", [P, RING, UNITS * GC])
        HI = sb("weights_hi", [P, RING, UNITS * GC], f32r)
        LO = sb("weights_lo", [P, RING, UNITS * GC], f32r)
        XH = sb("x_hi", [P, KT, T], f32r)
        XL = sb("x_lo", [P, KT, T], f32r)
        UH = sb("u_hi", [P, KT, T], f32r)
        UL = sb("u_lo", [P, KT, T], f32r)
        H = sb("residual", [P, KT, T])
        ZP = sb("projections", [P, 2 * KT, T])
        Q2 = sb("late", [P, 4096])
        WK = sb("work", [P, 4096])
        vecs = sb("vecs", [P, NVEC])
        ident = sb("ident", [P, P])
        ones = sb("ones", [P, P])
        rotate = sb("rotate", [P, P])
        steps = sb("steps", [P, T])
        cos_sin = sb("cos_sin", [P, 2, T])
        masks = sb("masks", [P, 2, 2 * T])
        rms = sb("rms", [P, 2, T])
        rms_col = sb("rms_col", [P, 2, 2])
        acc = sb("squares", [P, 2, T])
        small = sb("small", [P, 24, 32])
        consts = sb("consts", [P, 4])

        def vec(name, a=0, n=None):
            start, size = VEC[name]
            n = size - a if n is None else n
            return vecs[:, start + a:start + a + n] if isinstance(a, int) else vecs[:, bass.ds(a + start, n)]

        def view(buf, at, shape):
            n = int(np.prod(shape))
            v = buf[:, at:at + n]
            return v if len(shape) == 1 else v.rearrange("p (a b) -> p a b", b=shape[1])
        q2, wk = Q2, WK
        fcyc, kcyc, acyc = view(q2, 0, [T]), view(q2, 256, [T]), view(q2, 512, [T])
        sin_t = [view(q2, 768 + 512 * n, [T]) for n in range(2)]
        cos_t = [view(q2, 1024 + 512 * n, [T]) for n in range(2)]
        prod_c, prod_s = view(q2, 1792, [2, T]), view(q2, 2304, [2, T])
        state_g, state_h = view(q2, 2816, [2, T]), view(q2, 3328, [2, T])
        b_stage, c_stage = view(q2, 3840, [2, P]), view(wk, 2816, [2, P])
        qk_rot, rot_tmp = view(wk, 0, [2, T]), view(wk, 512, [2, T])
        probs, probs_t = view(wk, 1024, [2, T]), view(wk, 1536, [2, T])
        v_stage = view(wk, 2048, [2, P])
        u_stage = view(wk, 2304, [T])
        mem_raw = [view(wk, 0, [4, T]), view(wk, 1024, [4, T])]
        b_raw = [view(q2, 0, [PAIRS, 32]), view(q2, 1024, [PAIRS, 32])]
        b_bar = [view(q2, 2048, [PAIRS, 32]), view(q2, 3072, [PAIRS, 32])]
        squares = view(wk, 3072, [4, T])
        mem_stage = [view(wk, 3072, [2, T]), view(wk, 3584, [2, T])]
        b_flat = Q2[:, 0:2048]
        gate_space = masks[:, 1, :].rearrange("p (a t) -> p a t", a=2)
        up_space = view(wk, 0, [2, T])
        xr, gr = ZP[:, 0:KT, :], ZP[:, KT:2 * KT, :]
        qm, merged = ZP[:, 0:KT, :], ZP[:, KT:2 * KT, :]
        q_late = Q2[:, :].rearrange("p (a t) -> p a t", t=T)
        lru_xc = [view(wk, 1792 * n, [T]) for n in range(2)]
        lru_a = [view(wk, 1792 * n + 256, [2, T]) for n in range(2)]
        lru_w = [view(wk, 1792 * n + 768, [2, T]) for n in range(2)]
        lru_i = [view(wk, 1792 * n + 1280, [2, T]) for n in range(2)]
        lru_tmp = view(wk, 3584, [2, T])
        lru_weights = [masks[:, n, :].rearrange("p (m n) -> p m n", m=4) for n in range(2)]
        pos_raw, ang, ang_tmp = wk[:, 0:T], wk[:, 256:512], wk[:, 512:768]
        k2, v2 = view(wk, 0, [4, T]), view(wk, 1024, [2, 4 * P])
        q_rot, scores2 = view(wk, 2048, [T]), view(wk, 2304, [2, T])
        probs2_t, v2_stage = view(wk, 2816, [2, T]), view(wk, 3328, [2, P])
        probs2 = view(wk, 3584, [2, T])
        qm_stage, mk, mv = view(wk, 0, [4, T]), view(wk, 1024, [4, T]), view(wk, 2048, [4, GC])
        m_probs, m_probs_t = view(wk, 3072, [2, T]), view(wk, 3584, [2, T])
        values = ZP[:, 3 * UT:4 * UT, :].rearrange("p a t -> p (a t)").rearrange("p (k c) -> p k c", k=2)
        by_head = ZP[:, :, :].rearrange("p (a b) t -> p b a t", b=H1)

        def heads(h, first, n):
            v = by_head[:, ix(h()), first:first + n, :]
            return v.rearrange("p b a t -> p (b a) t") if n > 1 else v.rearrange("p b a t -> p (b a t)")

        def v_head(h):
            return values[:, :, ix(h(HD), HD)]
        bt_scratch = nc.dram_tensor("b_scratch", [UT, P, 2, P], f32).ap()
        memk_scratch = nc.dram_tensor("memk_scratch", [8, P, 2, T], f32).ap()
        memv_scratch = nc.dram_tensor("memv_scratch", [8, P, 2, T], f32).ap()

        GP = ctx.enter_context(nc.psum_tensor("gemm_psum", [P, 4, 512], f32))
        bank_a = ctx.enter_context(nc.psum_tensor("bank_a", [P, 2, T], f32))
        bank_s = ctx.enter_context(nc.psum_tensor("bank_s", [P, 2, T], f32))
        bank_b = ctx.enter_context(nc.psum_tensor("bank_b", [P, 2, T], f32))
        bank_y = ctx.enter_context(nc.psum_tensor("bank_y", [P, 2, T], f32))

        raw_in = [sem(f"raw_in{n}") for n in range(RING)]
        evac = [sem(f"evac{n}") for n in range(2)]
        x_in = [sem(f"x_in{n}") for n in range(4)]
        mem_in = [sem(f"mem_in{n}") for n in range(4)]
        memkv_out = [sem("memkv_out0"), sem("memkv_out1")]
        lw_in = [sem("lru_weights_in0"), sem("lru_weights_in1")]
        stored = [sem(f"stored{n}") for n in range(4)]
        hi_done, lo_done, mm_done, vecs_in = sem("hi_done"), sem("lo_done"), sem("mm_done"), sem("vecs_in")
        tabs_in, b_in, dve_step, pool_link = sem("tabs_in"), sem("b_in"), sem("dve_step"), sem("pool_link")
        dve_link, act_link, mem_squared, xg_done = sem("dve_link"), sem("act_link"), sem("mem_squared"), sem("xg_done")
        xh_done, xl_done, stat_in, stat_mm = sem("xh_done"), sem("xl_done"), sem("stat_in"), sem("stat_mm")
        stat_root, mg_done, mh_done, ml_done = sem("stat_root"), sem("mg_done"), sem("mh_done"), sem("ml_done")
        theta_done, angle_in, angle_done, bbar_done = sem("theta_done"), sem("angle_in"), sem("angle_done"), sem("bbar_done")
        bt_done, bt_copied, bt_out, cyc_done = sem("bt_done"), sem("bt_copied"), sem("bt_out"), sem("cyc_done")
        frac_done, trig_done, abs_done, cyc_half = sem("frac_done"), sem("trig_done"), sem("abs_done"), sem("cyc_half")
        bu_done, pq_done, gin_done, scan_done = sem("bu_done"), sem("pq_done"), sem("gin_done"), sem("scan_done")
        pq2_done, h_done, y_done, yt_done = sem("pq2_done"), sem("h_done"), sem("y_done"), sem("yt_done")
        bs_in, cs_in, us_done, rot_done = sem("bs_in"), sem("cs_in"), sem("us_done"), sem("rot_done")
        qk_sin, rope_done, scores_done, masked = sem("qk_sin"), sem("rope_done"), sem("scores_done"), sem("masked")
        max_done, nmax_done, exp_done, counted = sem("max_done"), sem("nmax_done"), sem("exp_done"), sem("counted")
        den_done, rden_done, probs_done, pt_done = sem("den_done"), sem("rden_done"), sem("probs_done"), sem("pt_done")
        pt_copied, vs_done, pv_done, oh_done = sem("pt_copied"), sem("vs_done"), sem("pv_done"), sem("oh_done")
        ol_done, yh_done, yl_done, gated = sem("ol_done"), sem("yh_done"), sem("yl_done"), sem("gated")
        gh_done, gl_done, res_done, res_g = sem("gh_done"), sem("gl_done"), sem("res_done"), sem("res_g")
        res_hi, res_lo, res_sq, sq_step = sem("res_hi"), sem("res_lo"), sem("res_sq"), sem("sq_step")
        silu_done, act_g, act_hi, act_lo = sem("silu_done"), sem("act_g"), sem("act_hi"), sem("act_lo")
        pos_in, rotate2_in, turn_done, lam_exp = sem("pos_in"), sem("rotate2_in"), sem("turn_done"), sem("lam_exp")
        lru_consts, angle2, norm_part, conv_step = sem("lru_consts"), sem("angle2"), sem("norm_part"), sem("conv_step")
        conv_done, lru_mm, sig_gates, decays = sem("conv_done"), sem("lru_mm"), sem("sig_gates"), sem("decays")
        w_step, w_done, root_done, u_done = sem("w_step"), sem("w_done"), sem("root_done"), sem("u_done")
        scans_done, dirs_summed, lru_y, lru_hi = sem("scans_done"), sem("dirs_summed"), sem("lru_y"), sem("lru_hi")
        lru_lo, gr_done, mask2_in, k_rot = sem("lru_lo"), sem("gr_done"), sem("mask2_in"), sem("k_rot")
        k_cos, k_roped, mkv_in, qm_staged = sem("k_cos"), sem("k_roped"), sem("mkv_in"), sem("qm_staged")
        op_hi, op_lo, gate_sig, merged_done = sem("op_hi"), sem("op_lo"), sem("gate_sig"), sem("merged_done")
        gate_biased, post_added, pre_hi, pre_lo = sem("gate_biased"), sem("post_added"), sem("pre_hi"), sem("pre_lo")
        up_sq, up_hi, up_lo = sem("up_sq"), sem("up_hi"), sem("up_lo")

        block = ctx.enter_context(nc.Block())

        @block.sync
        def _(sp):
            sp.dma_start(vecs[:, :], A["vecs"]).then_inc(vecs_in, 16)
            for n in range(4):
                sp.dma_start(H[:, 4 * n:4 * n + 4, :], A["x"][:, 4 * n:4 * n + 4, :]).then_inc(x_in[n], 16)
            for g in stages:
                for b, _ in g.stretches(sp, peel=g is in_u):
                    for j in range(SLOTS):
                        wait(sp, lo_done, b(SLOTS, SLOTS * g.first + j - RING + 1))
                        sp.dma_start(RAW[:, j % RING:j % RING + 1, 0:g.kt * GC],
                                     g.w[ix(b(2, j // UNITS)), j % UNITS].rearrange("a p n -> p a n"))\
                          .then_inc(raw_in[j % RING], 16)
            for n in range(4):
                sp.wait_ge(dve_step, n + 1)
                sp.dma_start(out[:, 4 * n:4 * n + 4, :], H[:, 4 * n:4 * n + 4, :]).then_inc(stored[n], 16)
            for n in range(4):
                sp.wait_ge(stored[n], 16)

        @block.tensor
        def _(pe):
            def units(g, b, j, operands, tokens_out=False):
                p = j // UNITS
                wait(pe, lo_done, b(SLOTS, SLOTS * g.first + j + 1))
                if j % UNITS == 0:
                    wait(pe, evac[p], b(1, g.first))
                xh, xl, off = operands
                for n in range(2):
                    for k in range(g.kt):
                        kk = off + (j % UNITS) * g.kt + k
                        first, end = j % UNITS == 0 and k == 0, j % UNITS == UNITS - 1 and k == g.kt - 1
                        o = GP[:, 2 * p + n, 0:T]
                        if tokens_out:
                            cols = slice(k * GC, (k + 1) * GC)
                            wh, wl = HI[:, j % RING, cols], LO[:, j % RING, cols]
                            ah, al = xh[:, kk, n * P:(n + 1) * P], xl[:, kk, n * P:(n + 1) * P]
                            pe.matmul(o, ah, wh, start=first, stop=False)
                            pe.matmul(o, al, wh, start=False, stop=False)
                            mm = pe.matmul(o, ah, wl, start=False, stop=end)
                        else:
                            cols = slice(k * GC + n * P, k * GC + (n + 1) * P)
                            wh, wl = HI[:, j % RING, cols], LO[:, j % RING, cols]
                            pe.matmul(o, wh, xh[:, kk, :], start=first, stop=False)
                            pe.matmul(o, wh, xl[:, kk, :], start=False, stop=False)
                            mm = pe.matmul(o, wl, xh[:, kk, :], start=False, stop=end)
                mm.then_inc(mm_done, 1)

            def ssm_in(q, i):
                wait(pe, pq_done, q(4, i))
                wait(pe, bs_in, q(16, 16))
                wait(pe, us_done, q(1, 1))
                rows = slice(32 * i, 32 * i + 32)
                for n in range(2):
                    mm = pe.matmul(bank_b[:, n, :], b_stage[rows, n, :], u_stage[rows, :],
                                   start=True, stop=True)
                mm.then_inc(bu_done, 1)

            def ssm_out(q, i):
                wait(pe, h_done, q(4, i + 1))
                if i == 0:
                    wait(pe, cs_in, q(16, 16))
                    wait(pe, yt_done, q())
                o = bank_y[32 * i:32 * i + 32, 0, :]
                pe.matmul(o, c_stage[:, 0, 32 * i:32 * i + 32], state_h[:, 0, :], start=True, stop=False)
                pe.matmul(o, c_stage[:, 1, 32 * i:32 * i + 32], state_h[:, 1, :], start=False, stop=True)\
                  .then_inc(y_done, 1)

            def ssm(slot, b, q0):
                q, half = b.halved().plus(q0), b.c % 2
                if slot == 0:
                    ssm_in(q, 2 * half)
                    if half:
                        ssm_out(q, 1)
                    elif not (isinstance(q(), int) and q() == 0):
                        ssm_out(q.before(), 3)
                if slot == 4:
                    ssm_in(q, 2 * half + 1)
                    ssm_out(q, 2 * half)

            def attention(slot, h):
                if slot == 0 and not (isinstance(h(), int) and h() == 0):
                    pv(h.before())
                if slot == 2:
                    wait(pe, ol_done, h())
                    if isinstance(h(), int) and h() == 0:
                        pe.wait_ge(evac[1], in_v.first + in_v.bodies)
                    pe.matmul(bank_a[:, 0, :], rotate[:, :], heads(h, 1, 1), start=True, stop=True)
                    pe.matmul(bank_a[:, 1, :], rotate[:, :], heads(h, 2, 1), start=True, stop=True).then_inc(rot_done, 1)
                if slot == 4:
                    wait(pe, rope_done, h(1, 1))
                    wait(pe, pt_copied, h())
                    for n in range(2):
                        mm = pe.matmul(bank_s[:, n, :], qk_rot[:, 0, n * P:(n + 1) * P], qk_rot[:, 1, :],
                                       start=True, stop=True)
                    mm.then_inc(scores_done, 1)
                if slot == 7:
                    wait(pe, probs_done, h(1, 1))
                    for kt in range(2):
                        for n in range(2):
                            mm = pe.transpose(bank_s[:, kt, n * P:(n + 1) * P], probs[:, n, kt * P:(kt + 1) * P],
                                              ident[:, :])
                    mm.then_inc(pt_done, 1)

            def pv(h):
                wait(pe, vs_done, h(1, 1))
                for kt in range(2):
                    mm = pe.matmul(bank_a[:, 0, :], v_stage[:, kt, :], probs_t[:, kt, :], start=kt == 0, stop=kt == 1)
                mm.then_inc(pv_done, 1)

            def statistics(n, ready, columns, sums=1):
                pe.wait_ge(*ready)
                for s in range(sums):
                    mm = pe.matmul(bank_y[:, s, :], ones[:, :], acc[:, s, :], start=True, stop=True)
                if columns:
                    for tt in range(2):
                        mm = pe.matmul(bank_a[:, 0, tt:tt + 1], acc[:, 0, tt * P:(tt + 1) * P], ones[:, 0:1],
                                       start=True, stop=True)
                mm.then_inc(stat_mm, 1)

            x, u = (XH, XL, 0), (UH, UL, 0)
            for b, _ in in_u.stretches(pe, peel=True):
                for j in range(SLOTS):
                    if b() == 0 and j < 4:
                        pe.wait_ge(xl_done, j + 1)
                    if b() == 0 and j == 4:
                        statistics(0, (stat_in, 1), True)
                    units(in_u, b, j, x)
            pe.wait_ge(tabs_in, 80)
            pe.wait_ge(bbar_done, 1)
            pe.wait_ge(stat_root, 1)
            for q in range(UT):
                bank = (bank_a, bank_s, bank_b, bank_y)[q // 2]
                for n in range(2):
                    mm = pe.transpose(bank[:, q % 2, n * P:(n + 1) * P], b_bar[n][:, 4 * q:4 * q + 4, :], ident[:, :])
            mm.then_inc(bt_done, 1)
            for b, _ in in_qk.stretches(pe, peel=True):
                for j in range(SLOTS):
                    ssm(j, b, 0)
                    units(in_qk, b, j, x)
            for b, _ in in_v.stretches(pe, peel=False):
                for j in range(SLOTS):
                    ssm(j, b, 2)
                    units(in_v, b, j, x, tokens_out=True)
            pe.wait_ge(ml_done, 4)
            pe.wait_ge(stat_in, 2)
            for b, _ in mem_k.stretches(pe, peel=True):
                for j in range(SLOTS):
                    ssm(j, b, 3)
                    attention(j, b)
                    if b() == 0 and isinstance(b(), int) and j == 1:
                        for tt in range(2):
                            mm = pe.matmul(bank_a[:, 0, tt:tt + 1], acc[:, 1, tt * P:(tt + 1) * P], ones[:, 0:1],
                                           start=True, stop=True)
                        mm = pe.matmul(bank_s[:, 0, :], ones[:, :], acc[:, 1, :], start=True, stop=True)
                        mm.then_inc(stat_mm, 1)
                        pe.wait_ge(stat_root, 2)
                    units(mem_k, b, j, u)
            for b, _ in mem_v.stretches(pe, peel=False):
                for j in range(SLOTS):
                    ssm(j, b, 5)
                    attention(j, b.plus(4))
                    units(mem_v, b, j, u, tokens_out=True)
            q7 = At(None, 0, 7)
            for b, c in out_attn.stretches(pe, peel=True):
                for j in range(SLOTS):
                    if j == 0:
                        ssm_in(q7, c)
                        ssm_out(q7, c - 1) if c else ssm_out(q7.before(), 3)
                        if c == 0:
                            pv(q7)
                            pe.wait_ge(ol_done, H1)
                    units(out_attn, b, j, x)
            ssm_out(q7, 3)
            for b, _ in glu.stretches(pe, peel=True):
                for j in range(SLOTS):
                    if b() == 0 and j == 0:
                        pe.wait_ge(yl_done, 1)
                    units(glu, b, j, (XH, XL, UT))
            pe.wait_ge(gl_done, 2)
            for b, _ in out_ssm.stretches(pe, peel=False):
                for j in range(SLOTS):
                    units(out_ssm, b, j, u)
            act_parts = 0
            for n, (up, down) in enumerate(ffn1):
                if n == 0:
                    pe.wait_ge(res_lo, 8)
                    statistics(2, (stat_in, 3), False)
                for b, _ in up.stretches(pe, peel=False):
                    for j in range(SLOTS):
                        units(up, b, j, x)
                act_parts += up.bodies
                pe.wait_ge(act_lo, act_parts)
                for b, _ in down.stretches(pe, peel=False):
                    for j in range(SLOTS):
                        units(down, b, j, u)
            statistics(3, (stat_in, 4), False, sums=2)
            for s in range(2):
                for tt in range(2):
                    mm = pe.matmul(bank_a[:, 0, 2 * s + tt:2 * s + tt + 1], acc[:, s, tt * P:(tt + 1) * P], ones[:, 0:1],
                                   start=True, stop=True)
            mm.then_inc(stat_mm, 1)
            pe.wait_ge(res_lo, 16)

            def lru(slot, b, before):
                if slot == 2:
                    c = b.plus(before)
                    for n in range(2):
                        wait(pe, conv_done, c(2, n + 1))
                        wait(pe, lw_in[n], c(16, 16))
                        banks = ((bank_a, bank_s), (bank_b, bank_y))[n]
                        for m in range(4):
                            mm = pe.matmul(banks[m // 2][:, m % 2, :], lru_weights[n][:, m, :], lru_xc[n],
                                           start=True, stop=True)
                        mm.then_inc(lru_mm, 1)

            pe.wait_ge(stat_root, 5)
            for b, _ in lru_in.stretches(pe, peel=False):
                for j in range(SLOTS):
                    units(lru_in, b, j, x)
            for b, _ in lru_gate.stretches(pe, peel=False):
                for j in range(SLOTS):
                    lru(j, b, 0)
                    units(lru_gate, b, j, x)
            for b, _ in in_q2.stretches(pe, peel=False):
                for j in range(SLOTS):
                    lru(j, b, 4)
                    units(in_q2, b, j, x)
            for g in (in_k2, in_v2):
                for b, _ in g.stretches(pe, peel=True):
                    for j in range(SLOTS):
                        units(g, b, j, x, tokens_out=g is in_v2)
            pe.wait_ge(rotate2_in, 16)
            for b, _ in in_qm.stretches(pe, peel=True):
                for j in range(SLOTS):
                    if j == 2:
                        wait(pe, k_roped, b())
                        pe.matmul(bank_a[:, 0, :], rotate[:, :], k2[:, ix(b()), :].rearrange("p a t -> p (a t)"),
                                  start=True, stop=True).then_inc(k_rot, 1)
                    units(in_qm, b, j, x)

            def local(slot, b):
                for n, slots in ((0, (0, 1, 3, 4)), (1, (4, 5, 7, 8))):
                    h = b.times(2).plus(n)
                    if slot == slots[3] % 8:
                        k = h if n == 0 else h.plus(-2)
                        if not (isinstance(k(), int) and k() < 0):
                            local_pv(k)
                    if slot == slots[0]:
                        pe.matmul(bank_a[:, 0, :], rotate[:, :], q_late[:, ix(h()), :].rearrange("p a t -> p (a t)"),
                                  start=True, stop=True).then_inc(rot_done, 1)
                    if slot == slots[1]:
                        wait(pe, rope_done, h(1, H1 + 1))
                        wait(pe, pt_copied, h(1, H1))
                        kv = k2[:, ix(b.halved()()), :].rearrange("p a t -> p (a t)")
                        for t in range(2):
                            mm = pe.matmul(bank_s[:, t, :], q_rot[:, t * P:(t + 1) * P], kv, start=True, stop=True)
                        mm.then_inc(scores_done, 1)
                    if slot == slots[2]:
                        wait(pe, probs_done, h(1, H1 + 1))
                        for kt in range(2):
                            for t in range(2):
                                mm = pe.transpose(bank_s[:, kt, t * P:(t + 1) * P], probs2[:, t, kt * P:(kt + 1) * P],
                                                  ident[:, :])
                        mm.then_inc(pt_done, 1)

            def local_pv(h):
                wait(pe, pt_copied, h(1, H1 + 1))
                wait(pe, oh_done, h(1, H1))
                for kt in range(2):
                    mm = pe.matmul(bank_b[:, 0, :], v2_stage[:, kt, :], probs2_t[:, kt, :], start=kt == 0, stop=kt == 1)
                mm.then_inc(pv_done, 1)

            def memory(slot, b):
                h, half = b.halved(), b.c % 2
                if slot == 2 and half == 0:
                    wait(pe, qm_staged, h(1, 1))
                    wait(pe, mkv_in, h(64, 64))
                    wait(pe, pt_copied, h(1, HEADS))
                    for t in range(2):
                        for d in range(4):
                            mm = pe.matmul(bank_s[:, t, :], qm_stage[:, d, t * P:(t + 1) * P], mk[:, d, :],
                                           start=d == 0, stop=d == 3)
                    mm.then_inc(scores_done, 1)
                if slot == 7 and half == 0:
                    wait(pe, probs_done, h(1, HEADS + 1))
                    for kt in range(2):
                        for t in range(2):
                            mm = pe.transpose(bank_a[:, kt, t * P:(t + 1) * P], m_probs[:, t, kt * P:(kt + 1) * P],
                                              ident[:, :])
                    mm.then_inc(pt_done, 1)
                if slot == 2 and half == 1:
                    wait(pe, pt_copied, h(1, HEADS + 1))
                    wait(pe, oh_done, h(1, HEADS))
                    for d in range(4):
                        bank = (bank_b, bank_y)[d // 2]
                        for kt in range(2):
                            mm = pe.matmul(bank[:, d % 2, :], mv[:, 2 * (d // 2) + kt, (d % 2) * P:(d % 2 + 1) * P],
                                           m_probs_t[:, kt, :], start=kt == 0, stop=kt == 1)
                    mm.then_inc(pv_done, 1)

            for n, g in enumerate(branches):
                for b, _ in g.stretches(pe, peel=True):
                    for j in range(SLOTS):
                        if n == 0 and j == 0 and isinstance(b(), int) and b() == 0:
                            pe.wait_ge(k_roped, 4)
                        if n == 0:
                            local(j, b)
                        if n == 1:
                            if j == 0 and isinstance(b(), int) and b() == 0:
                                local_pv(At(None, 0, 15))
                            memory(j, b)
                        if j >= 4 and isinstance(b(), int) and b() == 0:
                            pe.wait_ge(lru_lo, 16) if n == 0 else pe.wait_ge(op_lo, 4 * (n - 1) + j - 3)
                        units(g, b, j, x if j < 4 else u)
            for b, _ in out2.stretches(pe, peel=True):
                for j in range(SLOTS):
                    if isinstance(b(), int) and b() == 0 and j < 4:
                        pe.wait_ge(op_lo, 8 + j + 1)
                    units(out2, b, j, x)
            statistics(5, (stat_in, 5), False)
            done = 0
            for n, (up, down) in enumerate(ffn2):
                for b, _ in up.stretches(pe, peel=n == 0):
                    for j in range(SLOTS):
                        if n == 0 and isinstance(b(), int) and b() == 0:
                            if j < 4:
                                pe.wait_ge(pre_lo, j + 1)
                            if j == 4:
                                statistics(6, (stat_in, 6), False)
                        units(up, b, j, x)
                done += 8
                pe.wait_ge(up_lo, done)
                for b, _ in down.stretches(pe, peel=False):
                    for j in range(SLOTS):
                        units(down, b, j, u)
            statistics(7, (stat_in, 7), False)

        def stream(eng, g, split, late, events, tail=None):
            for b, _ in g.stretches(eng, peel=True):
                for j in range(SLOTS):
                    split(g, b, j)
                    if j >= LAG:
                        events(j - LAG, b)
                    elif isinstance(b(), int) and b() == 0:
                        if late:
                            late[0](SLOTS - LAG + j, late[1])
                        if j == LAG - 1 and tail:
                            tail()
                    else:
                        events(SLOTS - LAG + j, b.before())
            return events, At(None, 0, g.bodies - 1)

        @block.scalar
        def _(act):
            links = [0]

            def link(ins):
                links[0] += 1
                ins.then_inc(act_link, 1)
                act.wait_ge(act_link, links[0])

            def upper(g, b, j):
                wait(act, raw_in[j % RING], b(32, 32 * g.first + 16 * (j // RING) + 16))
                wait(act, mm_done, b(SLOTS, SLOTS * g.first + j - RING + 1))
                act.activation(HI[:, j % RING, 0:g.kt * GC], RAW[:, j % RING, 0:g.kt * GC], ACT.Copy)\
                   .then_inc(hi_done, 1)

            def root(n, src, dst, src_col=None, dst_col=None):
                act.wait_ge(stat_mm, n + 1)
                ins = act.activation(dst, src, ACT.Sqrt, scale=1.0 / D, bias=consts[:, 0:1])
                if src_col is not None:
                    ins = act.activation(dst_col, src_col, ACT.Sqrt, scale=1.0 / D, bias=consts[:, 0:1])
                ins.then_inc(stat_root, 1)

            def nothing(slot, b):
                pass

            act.dma_start(ident[:, :], A["ident"]).then_inc(tabs_in, 16)
            act.dma_start(rotate[:, :], A["rotate1"]).then_inc(tabs_in, 16)
            act.dma_start(steps[:, :], A["steps"]).then_inc(tabs_in, 16)
            act.dma_start(cos_sin[:, :, :], A["cos_sin"]).then_inc(tabs_in, 16)
            act.dma_start(masks[:, :, :], A["masks1"]).then_inc(tabs_in, 16)
            for n in range(2):
                act.dma_start(b_raw[n], A[("b_re", "b_im")[n]]).then_inc(b_in, 16)
            for n in range(2):
                act.dma_start(mem_raw[n], A["mem"][:, 4 * n:4 * n + 4, :]).then_inc(mem_in[n], 16)
            for n in range(4):
                act.wait_ge(xg_done, n + 1)
                act.activation(XH[:, 4 * n:4 * n + 4, :], ZP[:, 4 * n:4 * n + 4, :], ACT.Copy).then_inc(xh_done, 1)

            def in_u_events(slot, b):
                if slot == 0 and b() == 0:
                    act.wait_ge(vecs_in, 16)
                    act.activation(small[:, 0, :], vec("log_dt"), ACT.Exp).then_inc(angle_in, 1)
                if slot == 1 and b() == 0:
                    act.wait_ge(theta_done, 1)
                    act.activation(small[:, 3, :], small[:, 1, :], ACT.Exp)
                    link(act.activation(small[:, 7, :], small[:, 6, :], ACT.Abs))
                    act.activation(small[:, 8, :], small[:, 6, :], ACT.Sin, scale=TWO_PI)
                    act.activation(small[:, 9, :], small[:, 7, :], ACT.Sin, scale=-TWO_PI, bias=consts[:, 1:2])\
                       .then_inc(angle_done, 1)
                if slot in (2, 6):
                    n = 2 * b() + slot // 4
                    act.wait_ge(mg_done, n + 1)
                    act.activation(UH[:, 4 * n:4 * n + 4, :], mem_raw[n % 2], ACT.Copy).then_inc(mh_done, 1)
                if slot == 3 and b() == 0:
                    root(0, bank_y[:, 0, :], rms[:, 1, :], bank_a[:, 0, 0:2], rms_col[:, 1, :])

            def tables(s, par):
                wait(act, frac_done, s(1, 1))
                act.activation(acyc, kcyc, ACT.Abs).then_inc(abs_done, 1)
                act.activation(sin_t[par], kcyc, ACT.Sin, scale=-TWO_PI)
                wait(act, abs_done, s(1, 1))
                act.activation(cos_t[par], acyc, ACT.Sin, scale=-TWO_PI, bias=consts[:, 1:2]).then_inc(trig_done, 1)

            def input_staged(q):
                wait(act, bu_done, q(4))
                act.activation(u_stage, ZP[:, ix(q()), :].rearrange("p a t -> p (a t)"), ACT.Copy).then_inc(us_done, 1)

            def ssm(slot, b, q0):
                if slot == 5 and b.c % 2:
                    input_staged(b.halved().plus(q0 + 1))
                if slot in (2, 6):
                    tables(b.times(2).plus(4 * q0 + slot // 4 + 1), (slot // 4 + 1) % 2)

            def attention(slot, h):
                if slot == 1 and not (isinstance(h(), int) and h() == 0):
                    upper_out(h.before())
                if slot == 4:
                    wait(act, nmax_done, h(1, 1))
                    for n in range(2):
                        ins = act.activation(probs[:, n, :], rot_tmp[:, n, :], ACT.Exp, scale=SCALE, bias=small[:, 20, n:n + 1])
                    ins.then_inc(exp_done, 1)
                if slot == 7:
                    wait(act, pt_done, h(1, 1))
                    act.activation(probs_t[:, :, :], bank_s[:, :, :], ACT.Copy).then_inc(pt_copied, 1)
                    act.activation(v_stage[:, :, :], v_head(h), ACT.Copy).then_inc(vs_done, 1)

            def upper_out(h):
                wait(act, pv_done, h(1, 1))
                act.activation(XH[:, ix(h()), :], bank_a[:, 0:1, :], ACT.Copy).then_inc(oh_done, 1)

            def qk_events(slot, b):
                ssm(slot, b, 0)

            def v_events(slot, b):
                ssm(slot, b, 2)

            def mem_out(scratch, g, slot, b):
                p = slot // 4
                wait(act, evac[p], b(1, g.first + 1))
                act.dma_start(scratch[ix(b(2, p))].rearrange("a p k t -> p (a k) t"), mem_stage[p]).then_inc(memkv_out[p], 16)

            def mem_k_events(slot, b):
                ssm(slot, b, 3)
                attention(slot, b)
                if slot in (3, 7):
                    mem_out(memk_scratch, mem_k, slot, b)

            def mem_v_events(slot, b):
                ssm(slot, b, 5)
                attention(slot, b.plus(4))
                if slot in (3, 7):
                    mem_out(memv_scratch, mem_v, slot, b)

            def out_attn_events(slot, b):
                if slot == 1 and b() == 0:
                    upper_out(At(None, 0, 7))
                if slot == 2 and b() < 3:
                    tables(At(None, 0, 29 + b()), (29 + b()) % 2)

            def qk_tail():
                act.wait_ge(bt_done, 1)
                for n, bank in enumerate((bank_a, bank_s, bank_b, bank_y)):
                    ins = act.activation(b_flat[:, 512 * n:512 * n + 512], bank[:, :, :], ACT.Copy)
                ins.then_inc(bt_copied, 1)
                act.wait_ge(bt_copied, 1)
                act.dma_start(bt_scratch.rearrange("q p a n -> p q (a n)"),
                              b_flat.rearrange("p (q n) -> p q n", n=2 * P)).then_inc(bt_out, 16)
                act.wait_ge(bt_out, 16)
                tables(At(None, 0, 0), 0)
                act.wait_ge(evac[1], in_u.first + in_u.bodies)
                input_staged(At(None, 0, 0))

            def mem_stats():
                root(1, bank_s[:, 0, :], rms[:, 1, :], bank_a[:, 0, 0:2], rms_col[:, 1, :])

            late = stream(act, in_u, upper, None, in_u_events)
            late = stream(act, in_qk, upper, late, qk_events, tail=qk_tail)
            late = stream(act, in_v, upper, late, v_events)
            late = stream(act, mem_k, upper, late, mem_k_events, tail=mem_stats)
            late = stream(act, mem_v, upper, late, mem_v_events)
            late = stream(act, out_attn, upper, late, out_attn_events)

            def gelu_y():
                act.wait_ge(yt_done, 8)
                link(act.activation(ZP[:, 0:UT, :], ZP[:, 0:UT, :], ACT.Gelu_apprx_tanh))
                act.activation(XH[:, UT:KT, :], ZP[:, 0:UT, :], ACT.Copy).then_inc(yh_done, 1)

            def glu_events(slot, b):
                if slot in (3, 7):
                    gidx = 2 * b() + slot // 4
                    act.wait_ge(mm_done, SLOTS * (glu.first + b()) + slot + 1)
                    for n in range(2):
                        ins = act.activation(ZP[:, UT + 2 * gidx + n, :], GP[:, 2 * (slot // 4) + n, 0:T], ACT.Sigmoid,
                                             bias=vec("b_glu", 2 * gidx + n, 1))
                    ins.then_inc(evac[slot // 4], 1)
                if slot == 7:
                    act.wait_ge(gated, b() + 1)
                    act.activation(UH[:, 4 * b():4 * b() + 4, :], ZP[:, UT + 4 * b():UT + 4 * b() + 4, :], ACT.Copy)\
                       .then_inc(gh_done, 1)

            late = stream(act, glu, upper, late, glu_events, tail=gelu_y)

            def out_ssm_events(slot, b):
                if slot in (3, 7):
                    tiles = b(4, 2 * (slot // 4))
                    wait(act, res_g, b(2, slot // 4 + 1))
                    act.activation(XH[:, ix(tiles, 2), :], ZP[:, 0:2, :], ACT.Copy).then_inc(res_hi, 1)

            late = stream(act, out_ssm, upper, late, out_ssm_events)
            act.wait_ge(ol_done, H1)
            act.dma_start(rotate[:, :], A["rotate2"]).then_inc(rotate2_in, 16)
            act.dma_start(pos_raw.bitcast(i32), A["positions"]).then_inc(pos_in, 16)

            def final_root(n):
                def f():
                    root(n, bank_y[:, 0, :], rms[:, 1, :])
                return f

            def up_events(g, first):
                def f(slot, b):
                    if slot == 7:
                        tiles = b(2)
                        wait(act, evac[0], b(1, g.first + 1))
                        act.activation(ZP[:, 4:6, :], ZP[:, 2:4, :], ACT.Silu).then_inc(silu_done, 1)
                        wait(act, act_g, b(1, first + 1))
                        act.activation(UH[:, ix(tiles, 2), :], ZP[:, 6:8, :], ACT.Copy).then_inc(act_hi, 1)
                return f

            def last_down_events(slot, b):
                if slot in (3, 7):
                    tiles = b(4, 2 * (slot // 4))
                    wait(act, res_g, b(2, 8 + slot // 4 + 1))
                    act.activation(XH[:, ix(tiles, 2), :], ZP[:, 0:2, :], ACT.Copy).then_inc(res_hi, 1)

            def second_constants():
                act.wait_ge(turn_done, 1)
                link(act.activation(ang_tmp, ang, ACT.Abs))
                act.activation(cos_sin[:, 1, :], ang, ACT.Sin, scale=TWO_PI)
                act.activation(cos_sin[:, 0, :], ang_tmp, ACT.Sin, scale=-TWO_PI, bias=consts[:, 1:2])
                link(act.activation(small[:, 0, :], vec("lam"), ACT.Abs))
                act.activation(small[:, 1, :], small[:, 0, :], ACT.Exp, scale=-1.0).then_inc(lam_exp, 1)

            done = 0
            for n, (up, down) in enumerate(ffn1):
                late = stream(act, up, upper, late, up_events(up, done), tail=final_root(2) if n == 0 else None)
                done += up.bodies
                late = stream(act, down, upper, late, last_down_events if n == 2 else nothing,
                              tail=second_constants if n == 0 else None)

            def block_roots():
                act.wait_ge(stat_mm, 5)
                act.activation(rms[:, 1, :], bank_y[:, 0, :], ACT.Sqrt, scale=1.0 / D, bias=consts[:, 0:1])
                act.activation(rms_col[:, 1, :], bank_a[:, 0, 0:2], ACT.Sqrt, scale=1.0 / D, bias=consts[:, 0:1])\
                   .then_inc(stat_root, 1)
                act.wait_ge(norm_part, 1)
                act.activation(rms[:, 0, :], rms[:, 0, :], ACT.Sqrt, scale=1.0 / D, bias=consts[:, 0:1])
                act.activation(rms_col[:, 0, :], rms_col[:, 0, :], ACT.Sqrt, scale=1.0 / D, bias=consts[:, 0:1])\
                   .then_inc(stat_root, 1)

            def gelu_gate(g, slot, b):
                if slot in (3, 7):
                    p = slot // 4
                    wait(act, evac[p], b(1, g.first + 1))
                    t = gr[:, ix(b(4, 2 * p), 2), :]
                    act.activation(t, t, ACT.Gelu_apprx_tanh).then_inc(gr_done, 1)

            def lru(slot, b, before):
                c = b.plus(before)
                if slot == 2:
                    for n in range(2):
                        wait(act, lru_mm, c(2, n + 1))
                        banks = ((bank_a, bank_s), (bank_b, bank_y))[n]
                        for d in range(2):
                            act.activation(lru_a[n][:, d, :], banks[0][:, d, :], ACT.Sigmoid, bias=vec("br", c(2, 16 * d + n), 1))
                            ins = act.activation(lru_i[n][:, d, :], banks[1][:, d, :], ACT.Sigmoid, bias=vec("bi", c(2, 16 * d + n), 1))
                        ins.then_inc(sig_gates, 1)
                if slot == 3:
                    for n in range(2):
                        wait(act, sig_gates, c(2, n + 1))
                        for d in range(2):
                            ins = act.activation(lru_w[n][:, d, :], lru_a[n][:, d, :], ACT.Tanh, scale=small[:, 15, ix(c(2, 16 * d + n))])
                    ins.then_inc(angle2, 1)
                    wait(act, angle2, c(1, 1))
                    for n in range(2):
                        for d in range(2):
                            ins = act.activation(lru_a[n][:, d, :], lru_a[n][:, d, :], ACT.Exp, scale=small[:, 16, ix(c(2, 16 * d + n))])
                        ins.then_inc(decays, 1)
                if slot == 5:
                    wait(act, w_done, c(2, 2))
                    for n in range(2):
                        act.activation(lru_w[n], lru_w[n], ACT.Sqrt).then_inc(root_done, 1)
                if slot == 7:
                    wait(act, lru_y, c(2, 2))
                    for n in range(2):
                        act.activation(UH[:, ix(c(2, n)), :], lru_a[n][:, 0:1, :], ACT.Copy).then_inc(lru_hi, 1)

            def lru_gate_events(slot, b):
                gelu_gate(lru_gate, slot, b)
                lru(slot, b, 0)

            def q2_events(slot, b):
                lru(slot, b, 4)

            late = stream(act, lru_in, upper, late, nothing, tail=block_roots)
            late = stream(act, lru_gate, upper, late, lru_gate_events)
            late = stream(act, in_q2, upper, late, q2_events)
            late = stream(act, in_k2, upper, late, nothing)
            late = stream(act, in_v2, upper, late, nothing)
            late = stream(act, in_qm, upper, late, nothing)

            def local(slot, b):
                for n, slots in ((0, (1, 3, 4)), (1, (5, 7, 8))):
                    h = b.times(2).plus(n)
                    if slot == slots[2] % 8:
                        k = h if n == 0 else h.plus(-2)
                        if not (isinstance(k(), int) and k() < 0):
                            local_out(k)
                    if slot == slots[0]:
                        wait(act, nmax_done, h(1, H1 + 1))
                        for t in range(2):
                            act.activation(probs2[:, t, :], scores2[:, t, :], ACT.Exp, scale=SCALE, bias=small[:, 20, t:t + 1],
                                           accum_out=small[:, 19, t:t + 1])
                        act.activation(small[:, 19, 2:4], small[:, 20, 0:2], ACT.Exp, bias=vec("sink", h(), 1)).then_inc(exp_done, 1)
                    if slot == slots[1]:
                        wait(act, pt_done, h(1, H1 + 1))
                        act.activation(probs2_t[:, :, :], bank_s[:, :, :], ACT.Copy)
                        act.activation(v2_stage[:, :, :], v2[:, :, ix(b.halved()(HD), HD)], ACT.Copy).then_inc(pt_copied, 1)

            def local_out(h):
                wait(act, pv_done, h(1, H1 + 1))
                act.activation(q_late[:, ix(h()), :], bank_b[:, 0:1, :], ACT.Copy).then_inc(oh_done, 1)

            def gates(g, n, slot, b):
                if slot == 3:
                    wait(act, gate_biased, b(1, 8 * n + 1))
                    act.activation(gate_space, gate_space, ACT.Sigmoid).then_inc(gate_sig, 1)

            def memory(slot, b):
                h, half = b.halved(), b.c % 2
                if slot == 0 and half == 0:
                    wait(act, scores_done, h(1, HEADS))
                    act.activation(qm_stage[:, :, :], qm[:, ix(h(4), 4), :], ACT.Copy).then_inc(qm_staged, 1)
                if slot == 4 and half == 0:
                    wait(act, nmax_done, h(1, HEADS + 1))
                    for t in range(2):
                        ins = act.activation(m_probs[:, t, :], m_probs[:, t, :], ACT.Exp, scale=M_SCALE, bias=small[:, 20, t:t + 1],
                                             accum_out=small[:, 19, t:t + 1])
                    ins.then_inc(exp_done, 1)
                if slot == 0 and half == 1:
                    wait(act, pt_done, h(1, HEADS + 1))
                    act.activation(m_probs_t[:, :, :], bank_a[:, :, :], ACT.Copy).then_inc(pt_copied, 1)
                if slot == 3 and half == 1:
                    wait(act, pv_done, h(1, HEADS + 1))
                    act.activation(qm[:, ix(h(4, 2), 2), :], bank_y[:, :, :], ACT.Copy)
                    act.activation(qm[:, ix(h(4), 2), :], bank_b[:, :, :], ACT.Copy).then_inc(oh_done, 1)

            def operand(n, src, hi):
                def f():
                    if n == 0:
                        local_out(At(None, 0, 15))
                        act.wait_ge(oh_done, H1 + 16)
                    if n == 1:
                        act.wait_ge(oh_done, HEADS + 4)
                    if n == 2:
                        act.wait_ge(merged_done, 16)
                    act.wait_ge(mm_done, SLOTS * (branches[n].first + 8))
                    for c in range(4):
                        act.activation(hi[:, 4 * c:4 * c + 4, :], src[:, 4 * c:4 * c + 4, :], ACT.Copy).then_inc(op_hi, 1)
                return f

            def branch_events(n):
                def f(slot, b):
                    if n == 0:
                        local(slot, b)
                    if n == 1:
                        memory(slot, b)
                    gates(branches[n], n, slot, b)
                return f

            late = stream(act, branches[0], upper, late, branch_events(0))
            late = stream(act, branches[1], upper, late, branch_events(1), tail=operand(0, q_late, UH))
            late = stream(act, branches[2], upper, late, branch_events(2), tail=operand(1, qm, UH))
            late = stream(act, out2, upper, late, nothing, tail=operand(2, merged, XH))

            def mixed():
                root(5, bank_y[:, 0, :], rms[:, 1, :])
                for k in range(KT):
                    if k % 4 == 0:
                        act.wait_ge(post_added, k // 4 + 1)
                    ins = act.activation(XH[:, k, :], H[:, k, :], ACT.Copy, scale=vec("mlp_pre", k, 1))
                    if k % 4 == 3:
                        ins.then_inc(pre_hi, 1)

            def up2_events(first):
                def f(slot, b):
                    if slot in (3, 7):
                        if slot == 3 and first == 0 and isinstance(b(), int) and b() == 0:
                            root(6, bank_y[:, 0, :], rms[:, 1, :])
                        wait(act, up_sq, b(2, first + slot // 4 + 1))
                        act.activation(UH[:, ix(b(4, 2 * (slot // 4)), 2), :], up_space, ACT.Copy).then_inc(up_hi, 1)
                return f

            for n, (up, down) in enumerate(ffn2):
                late = stream(act, up, upper, late, up2_events(8 * n), tail=mixed if n == 0 else None)
                late = stream(act, down, upper, late, nothing)
            root(7, bank_y[:, 0, :], rms[:, 1, :])

        @block.vector
        def _(dve):
            links = [0]

            def link(ins):
                links[0] += 1
                ins.then_inc(dve_link, 1)
                dve.wait_ge(dve_link, links[0])

            def lower(g, b, j):
                wait(dve, hi_done, b(SLOTS, SLOTS * g.first + j + 1))
                cols = slice(0, g.kt * GC)
                dve.tensor_tensor(LO[:, j % RING, cols], RAW[:, j % RING, cols], HI[:, j % RING, cols].bitcast(f32),
                                  ALU.subtract).then_inc(lo_done, 1)

            def taken(g, b, slot):
                wait(dve, mm_done, b(SLOTS, SLOTS * g.first + slot + 1))
                return GP[:, 2 * (slot // 4):2 * (slot // 4) + 2, 0:T]

            def row(v):
                return v.unsqueeze(1).to_broadcast([P, 2, T])

            def col(v, n=T):
                return v.unsqueeze(2).to_broadcast([P, v.shape[1], n])

            dve.memset(consts[:, 0:1], EPS)
            link(dve.memset(consts[:, 1:2], math.pi / 2))
            dve.wait_ge(vecs_in, 16)
            for n in range(4):
                dve.wait_ge(x_in[n], 16)
                s = slice(4 * n, 4 * n + 4)
                dve.tensor_tensor(ZP[:, s, :], H[:, s, :], col(vec("norm1", 4 * n, 4)), ALU.mult).then_inc(xg_done, 1)
                dve.wait_ge(xh_done, n + 1)
                dve.tensor_tensor(XL[:, s, :], ZP[:, s, :], XH[:, s, :].bitcast(f32), ALU.subtract).then_inc(xl_done, 1)

            def reduced(dst, src, tmp):
                link(dve.tensor_scalar(tmp, src, 1.0 / (2 * math.pi), MAGIC, ALU.mult, ALU.add))
                link(dve.tensor_scalar(tmp, tmp, -MAGIC, None, ALU.add))
                for part in (-6.28125, -0.0019350051879882812, -3.019916e-07):
                    link(dve.scalar_tensor_tensor(src, tmp, part, src, ALU.mult, ALU.add))
                link(dve.tensor_scalar(dst, src, 1.0 / (2 * math.pi), None, ALU.mult))
                return dve.tensor_scalar(dst, dst, 0.5, -0.5, ALU.min, ALU.max)

            def s_(n):
                return small[:, n, :]

            def tt(o, a, b, op):
                link(dve.tensor_tensor(o, a, b, op))

            def ssm_params():
                dve.wait_ge(angle_in, 1)
                tt(s_(1), vec("a_re"), s_(0), ALU.mult)
                tt(s_(2), vec("a_im"), s_(0), ALU.mult)
                reduced(s_(6), s_(2), s_(4)).then_inc(theta_done, 1)
                tt(s_(4), vec("a_re"), vec("a_re"), ALU.mult)
                tt(s_(5), vec("a_im"), vec("a_im"), ALU.mult)
                tt(s_(4), s_(4), s_(5), ALU.add)
                link(dve.reciprocal(s_(12), s_(4)))

            def ssm_input():
                dve.wait_ge(angle_done, 1)
                tt(s_(11), s_(3), s_(8), ALU.mult)
                tt(s_(10), s_(3), s_(9), ALU.mult)
                link(dve.tensor_scalar(s_(10), s_(10), -1.0, None, ALU.add))
                tt(s_(4), s_(10), vec("a_re"), ALU.mult)
                tt(s_(5), s_(11), vec("a_im"), ALU.mult)
                tt(s_(4), s_(4), s_(5), ALU.add)
                tt(s_(13), s_(4), s_(12), ALU.mult)
                tt(s_(4), s_(11), vec("a_re"), ALU.mult)
                tt(s_(5), s_(10), vec("a_im"), ALU.mult)
                tt(s_(4), s_(4), s_(5), ALU.subtract)
                tt(s_(14), s_(4), s_(12), ALU.mult)
                dve.wait_ge(b_in, 32)
                re, im = col(s_(13), 32), col(s_(14), 32)
                tt(b_bar[0], b_raw[0], re, ALU.mult)
                tt(b_bar[1], b_raw[1], im, ALU.mult)
                tt(b_bar[0], b_bar[0], b_bar[1], ALU.subtract)
                tt(b_bar[1], b_raw[1], re, ALU.mult)
                tt(b_raw[0], b_raw[0], im, ALU.mult)
                dve.tensor_tensor(b_bar[1], b_bar[1], b_raw[0], ALU.add).then_inc(bbar_done, 1)

            def scaled_out(g, b, slot, dst):
                o = taken(g, b, slot)
                dve.tensor_tensor(dst, o, row(rms[:, 0, :]), ALU.mult).then_inc(evac[slot // 4], 1)

            def in_u_events(slot, b):
                if slot == 1 and b() == 0:
                    ssm_params()
                if slot == 5 and b() == 0:
                    ssm_input()
                if slot in (2, 6):
                    n = 2 * b() + slot // 4
                    dve.wait_ge(mem_in[n], 16)
                    dve.wait_ge(mem_squared, n + 1)
                    dve.tensor_tensor(mem_raw[n % 2], mem_raw[n % 2], col(vec("mem", 4 * n, 4)), ALU.mult).then_inc(mg_done, 1)
                    dve.wait_ge(mh_done, n + 1)
                    dve.tensor_tensor(UL[:, 4 * n:4 * n + 4, :], mem_raw[n % 2], UH[:, 4 * n:4 * n + 4, :].bitcast(f32),
                                      ALU.subtract).then_inc(ml_done, 1)
                if slot in (3, 7):
                    if slot == 3 and b() == 0:
                        dve.wait_ge(stat_root, 1)
                        link(dve.reciprocal(rms[:, 0, :], rms[:, 1, :]))
                        link(dve.reciprocal(rms_col[:, 0, :], rms_col[:, 1, :]))
                    tile0 = 4 * b() + 2 * (slot // 4)
                    scaled_out(in_u, b, slot, ZP[:, tile0:tile0 + 2, :])

            def fractions(s):
                wait(dve, cyc_done, s(1, 1))
                dve.scalar_tensor_tensor(kcyc, kcyc, MAGIC, fcyc, ALU.subtract, ALU.subtract).then_inc(frac_done, 1)

            def rotate_in(s, par):
                wait(dve, bu_done, s(1, 1))
                wait(dve, trig_done, s(1, 1))
                wait(dve, h_done, s())
                dve.tensor_tensor(prod_c, bank_b[:, :, :], row(cos_t[par]), ALU.mult)
                dve.tensor_tensor(prod_s, bank_b[:, :, :], row(sin_t[par]), ALU.mult).then_inc(pq_done, 1)

            def scan_and_rotate_out(s, par):
                wait(dve, gin_done, s(1, 1))
                decay = small[:, 3, ix(s())].to_broadcast([P, T])
                for n in range(2):
                    ins = dve.tensor_tensor_scan(state_g[:, n, :], decay, state_g[:, n, :], 0.0, ALU.mult, ALU.add)
                ins.then_inc(scan_done, 1)
                wait(dve, scan_done, s(1, 1))
                dve.tensor_tensor(prod_c, state_g, row(cos_t[par]), ALU.mult)
                dve.tensor_tensor(prod_s, state_g, row(sin_t[par]), ALU.mult).then_inc(pq2_done, 1)

            def skip_added(q):
                wait(dve, y_done, q(4, 4))
                tile = ZP[:, ix(q()), :].rearrange("p a t -> p (a t)")
                dve.scalar_tensor_tensor(tile, tile, vec("d_skip", q(), 1), bank_y[:, 0, :], ALU.mult, ALU.add)\
                   .then_inc(yt_done, 1)

            def ssm(slot, b, q0):
                s = b.times(2).plus(4 * q0)
                if slot in (0, 4):
                    rotate_in(s.plus(slot // 4), slot // 4)
                if slot in (2, 6):
                    scan_and_rotate_out(s.plus(slot // 4), slot // 4)
                if slot in (1, 5):
                    fractions(s.plus(slot // 4 + 1))
                if slot == 1 and b.c % 2 == 0:
                    q = b.halved().plus(q0 - 1)
                    if not (isinstance(q(), int) and q() < 0):
                        skip_added(q)

            def attention(slot, h):
                if slot == 1 and not (isinstance(h(), int) and h() == 0):
                    lower_out(h.before())
                if slot == 2:
                    wait(dve, rot_done, h(1, 1))
                    dve.tensor_tensor(qk_rot, heads(h, 1, 2), row(cos_sin[:, 0, :]), ALU.mult)
                    dve.tensor_tensor(rot_tmp, bank_a[:, :, :], row(cos_sin[:, 1, :]), ALU.mult).then_inc(qk_sin, 1)
                    wait(dve, qk_sin, h(1, 1))
                    dve.tensor_tensor(qk_rot, qk_rot, rot_tmp, ALU.add).then_inc(rope_done, 1)
                if slot == 4:
                    wait(dve, scores_done, h(1, 1))
                    dve.tensor_tensor(rot_tmp, bank_s[:, :, :], masks[:, 0, :].rearrange("p (a t) -> p a t", a=2), ALU.add)\
                       .then_inc(masked, 1)
                    wait(dve, masked, h(1, 1))
                    dve.tensor_reduce(small[:, 21, 0:2], rot_tmp, AX.X, ALU.max).then_inc(max_done, 1)
                    wait(dve, max_done, h(1, 1))
                    dve.tensor_scalar(small[:, 20, 0:2], small[:, 21, 0:2], -SCALE, None, ALU.mult).then_inc(nmax_done, 1)
                if slot == 5:
                    wait(dve, exp_done, h(1, 1))
                    dve.tensor_tensor(probs, probs, masks[:, 1, :].rearrange("p (a t) -> p a t", a=2), ALU.mult).then_inc(counted, 1)
                    wait(dve, counted, h(1, 1))
                    dve.tensor_reduce(small[:, 19, 0:2], probs, AX.X, ALU.add).then_inc(den_done, 1)
                    wait(dve, den_done, h(1, 1))
                    dve.reciprocal(small[:, 18, 0:2], small[:, 19, 0:2]).then_inc(rden_done, 1)
                    wait(dve, rden_done, h(1, 1))
                    dve.tensor_tensor(probs, probs, col(small[:, 18, 0:2]), ALU.mult).then_inc(probs_done, 1)

            def lower_out(h):
                wait(dve, oh_done, h(1, 1))
                dve.tensor_tensor(XL[:, ix(h()), :], bank_a[:, 0:1, :], XH[:, ix(h()), :].bitcast(f32), ALU.subtract)\
                   .then_inc(ol_done, 1)

            def qk_events(slot, b):
                ssm(slot, b, 0)
                if slot in (3, 7):
                    scaled_out(in_qk, b, slot, ZP[:, ix(b(4, 8 + 2 * (slot // 4)), 2), :])

            def v_events(slot, b):
                ssm(slot, b, 2)
                if slot in (3, 7):
                    o = taken(in_v, b, slot)
                    dve.tensor_tensor(values[:, :, ix(b(2 * GC, GC * (slot // 4)), GC)], o, col(rms_col[:, 0, :]), ALU.mult)\
                       .then_inc(evac[slot // 4], 1)

            def mem_out(g, g0, slot, b, factor):
                p = slot // 4
                o = taken(g, b, slot)
                wait(dve, memkv_out[p], b(16, 16 * (g.first - mem_k.first)))
                dve.tensor_tensor(mem_stage[p], o, factor, ALU.mult).then_inc(evac[p], 1)

            def mem_k_events(slot, b):
                ssm(slot, b, 3)
                attention(slot, b)
                if slot in (3, 7):
                    mem_out(mem_k, 0, slot, b, row(rms[:, 0, :]))

            def mem_v_events(slot, b):
                ssm(slot, b, 5)
                attention(slot, b.plus(4))
                if slot in (3, 7):
                    mem_out(mem_v, 8, slot, b, col(rms_col[:, 0, :]))

            def out_attn_events(slot, b):
                s = At(None, 0, 28 + b())
                if slot == 0:
                    rotate_in(s, b() % 2)
                if slot == 1:
                    if b() == 0:
                        lower_out(At(None, 0, 7))
                        skip_added(At(None, 0, 6))
                    if b() < 3:
                        fractions(s.plus(1))
                if slot == 2:
                    scan_and_rotate_out(s, b() % 2)
                if slot in (3, 7):
                    o = taken(out_attn, b, slot)
                    tiles = slice(4 * b() + 2 * (slot // 4), 4 * b() + 2 * (slot // 4) + 2)
                    dve.tensor_tensor(H[:, tiles, :], H[:, tiles, :], o, ALU.add).then_inc(evac[slot // 4], 1)

            def qk_tail():
                fractions(At(None, 0, 0))

            def mem_stats():
                dve.wait_ge(stat_root, 2)
                link(dve.reciprocal(rms[:, 0, :], rms[:, 1, :]))
                link(dve.reciprocal(rms_col[:, 0, :], rms_col[:, 1, :]))

            def y_lower():
                skip_added(At(None, 0, 7))
                dve.wait_ge(yh_done, 1)
                dve.tensor_tensor(XL[:, UT:KT, :], ZP[:, 0:UT, :], XH[:, UT:KT, :].bitcast(f32), ALU.subtract).then_inc(yl_done, 1)

            def glu_events(slot, b):
                if slot == 7:
                    dve.wait_ge(evac[1], glu.first + b() + 1)
                    t, y = slice(UT + 4 * b(), UT + 4 * b() + 4), slice(4 * b(), 4 * b() + 4)
                    dve.tensor_tensor(ZP[:, t, :], ZP[:, t, :], ZP[:, y, :], ALU.mult).then_inc(gated, 1)
                    dve.wait_ge(gh_done, b() + 1)
                    dve.tensor_tensor(UL[:, y, :], ZP[:, t, :], UH[:, y, :].bitcast(f32), ALU.subtract).then_inc(gl_done, 1)

            def residual(g, b, slot, count, gain, before):
                p = slot // 4
                o = taken(g, b, slot)
                tiles = ix(b(4, 2 * p), 2)
                wait(dve, res_lo, b(2, before + p))
                dve.tensor_tensor(H[:, tiles, :], H[:, tiles, :], o, ALU.add).then_inc(evac[p], 1)
                wait(dve, evac[p], b(1, g.first + 1))
                if before:
                    wait(dve, res_sq, b(2, p + 1))
                    dve.tensor_tensor(H[:, tiles, :], H[:, tiles, :], col(vec("final", b(4, 2 * p), 2)), ALU.mult)\
                       .then_inc(res_done, 1)
                    wait(dve, res_done, b(2, p + 1))
                dve.tensor_tensor(ZP[:, 0:2, :], H[:, tiles, :], col(vec(gain, b(4, 2 * p), 2)), ALU.mult).then_inc(res_g, 1)
                wait(dve, res_hi, b(2, before + p + 1))
                dve.tensor_tensor(XL[:, tiles, :], ZP[:, 0:2, :], XH[:, tiles, :].bitcast(f32), ALU.subtract).then_inc(res_lo, 1)

            def out_ssm_events(slot, b):
                if slot in (3, 7):
                    residual(out_ssm, b, slot, 0, "norm2", 0)

            def rms_ready(n):
                def f():
                    dve.wait_ge(stat_root, n + 1)
                    link(dve.reciprocal(rms[:, 0, :], rms[:, 1, :]))
                return f

            def up_events(g, first):
                def f(slot, b):
                    if slot == 3:
                        o = taken(g, b, 3)
                        dve.tensor_tensor(ZP[:, 2:4, :], o, row(rms[:, 0, :]), ALU.mult).then_inc(evac[0], 1)
                    if slot == 7:
                        o = taken(g, b, 7)
                        dve.tensor_tensor(ZP[:, 6:8, :], o, row(rms[:, 0, :]), ALU.mult).then_inc(evac[1], 1)
                        wait(dve, silu_done, b(1, first + 1))
                        wait(dve, evac[1], b(1, g.first + 1))
                        dve.tensor_tensor(ZP[:, 6:8, :], ZP[:, 6:8, :], ZP[:, 4:6, :], ALU.mult).then_inc(act_g, 1)
                        wait(dve, act_hi, b(1, first + 1))
                        dve.tensor_tensor(UL[:, ix(b(2), 2), :], ZP[:, 6:8, :], UH[:, ix(b(2), 2), :].bitcast(f32),
                                          ALU.subtract).then_inc(act_lo, 1)
                return f

            def down_events(g):
                def f(slot, b):
                    if slot in (3, 7):
                        o = taken(g, b, slot)
                        tiles = ix(b(4, 2 * (slot // 4)), 2)
                        dve.tensor_tensor(H[:, tiles, :], H[:, tiles, :], o, ALU.add).then_inc(evac[slot // 4], 1)
                return f

            def last_down_events(slot, b):
                if slot in (3, 7):
                    residual(ffn1[2][1], b, slot, 0, "mix_pre", 8)

            late = stream(dve, in_u, lower, None, in_u_events)
            late = stream(dve, in_qk, lower, late, qk_events, tail=qk_tail)
            late = stream(dve, in_v, lower, late, v_events)
            late = stream(dve, mem_k, lower, late, mem_k_events, tail=mem_stats)
            late = stream(dve, mem_v, lower, late, mem_v_events)
            late = stream(dve, out_attn, lower, late, out_attn_events)
            late = stream(dve, glu, lower, late, glu_events, tail=y_lower)
            late = stream(dve, out_ssm, lower, late, out_ssm_events)
            def second_constants():
                dve.wait_ge(pos_in, 16)
                link(dve.tensor_copy(ang, pos_raw.bitcast(i32)))
                link(dve.tensor_scalar(ang, ang, vec("freq"), None, ALU.mult))
                link(reduced(ang, ang, ang_tmp))
                dve.wait_ge(ol_done, H1)
                dve.tensor_copy(small[:, 14, 0:1], small[:, 14, 1:2]).then_inc(turn_done, 1)
                dve.wait_ge(lam_exp, 1)
                link(dve.tensor_scalar(s_(2), s_(1), 2.0, None, ALU.add))
                link(dve.reciprocal(s_(2), s_(2)))
                tt(s_(2), s_(2), s_(1), ALU.mult)
                tt(s_(3), s_(2), s_(2), ALU.mult)
                link(dve.tensor_scalar(s_(4), s_(3), 1.0 / 19, 1.0 / 17, ALU.mult, ALU.add))
                for k in range(15, 0, -2):
                    tt(s_(4), s_(4), s_(3), ALU.mult)
                    link(dve.tensor_scalar(s_(4), s_(4), 1.0 / k, None, ALU.add))
                tt(s_(4), s_(4), s_(2), ALU.mult)
                link(dve.tensor_scalar(s_(5), vec("lam"), -1.0, 0.0, ALU.mult, ALU.max))
                link(dve.scalar_tensor_tensor(s_(5), s_(4), 2.0, s_(5), ALU.mult, ALU.add))
                dve.tensor_scalar(s_(15), s_(5), 8.0, None, ALU.mult)
                dve.tensor_scalar(s_(16), s_(5), -8.0, None, ALU.mult).then_inc(lru_consts, 1)

            done = 0
            for n, (up, down) in enumerate(ffn1):
                late = stream(dve, up, lower, late, up_events(up, done), tail=rms_ready(2) if n == 0 else None)
                done += up.bodies
                late = stream(dve, down, lower, late, last_down_events if n == 2 else down_events(down),
                              tail=second_constants if n == 0 else None)

            def block_norms():
                dve.wait_ge(stat_root, 4)
                link(dve.reciprocal(rms[:, 1, :], rms[:, 1, :]))
                link(dve.reciprocal(rms_col[:, 1, :], rms_col[:, 1, :]))
                tt(rms[:, 0, :], rms[:, 1, :], rms[:, 1, :], ALU.mult)
                tt(rms_col[:, 0, :], rms_col[:, 1, :], rms_col[:, 1, :], ALU.mult)
                dve.tensor_tensor(rms[:, 0, :], rms[:, 0, :], bank_y[:, 1, :], ALU.mult)
                dve.tensor_tensor(rms_col[:, 0, :], rms_col[:, 0, :], bank_a[:, 0, 2:4], ALU.mult).then_inc(norm_part, 1)
                dve.wait_ge(stat_root, 5)
                link(dve.reciprocal(rms[:, 0, :], rms[:, 0, :]))
                link(dve.reciprocal(rms_col[:, 0, :], rms_col[:, 0, :]))
                tt(rms[:, 0, :], rms[:, 0, :], rms[:, 1, :], ALU.mult)
                tt(rms_col[:, 0, :], rms_col[:, 0, :], rms_col[:, 1, :], ALU.mult)

            def lru_in_events(slot, b):
                if slot in (3, 7):
                    p = slot // 4
                    tiles = ix(b(4, 2 * p), 2)
                    scaled_out(lru_in, b, slot, xr[:, tiles, :])
                    dve.tensor_tensor(H[:, tiles, :], H[:, tiles, :], row(rms[:, 1, :]), ALU.mult)

            def lru(slot, b, before):
                c = b.plus(before)
                if slot == 0:
                    if not (isinstance(c(), int) and c() == 0):
                        for n in range(2):
                            wait(dve, lru_hi, c(2, n - 1))
                            t = ix(c(2, n - 2))
                            dve.tensor_tensor(UL[:, t, :], lru_a[n][:, 0:1, :], UH[:, t, :].bitcast(f32), ALU.subtract).then_inc(lru_lo, 1)
                    for n in range(2):
                        src = xr[:, ix(c(2, n)), :].rearrange("p a t -> p (a t)")
                        def tap(k):
                            return vec("conv_w", c(2, 16 * k + n), 1)
                        v = lru_xc[n]
                        dve.tensor_scalar(v, src, tap(1), vec("conv_b", c(2, n), 1), ALU.mult, ALU.add).then_inc(conv_step, 1)
                        wait(dve, conv_step, c(6, 3 * n + 1))
                        dve.scalar_tensor_tensor(v[:, 1:T], src[:, 0:T - 1], tap(0), v[:, 1:T], ALU.mult, ALU.add).then_inc(conv_step, 1)
                        wait(dve, conv_step, c(6, 3 * n + 2))
                        dve.scalar_tensor_tensor(v[:, 0:T - 1], src[:, 1:T], tap(2), v[:, 0:T - 1], ALU.mult, ALU.add).then_inc(conv_step, 1)
                        wait(dve, conv_step, c(6, 3 * n + 3))
                        dve.scalar_tensor_tensor(v[:, 0:T - 2], src[:, 2:T], tap(3), v[:, 0:T - 2], ALU.mult, ALU.add).then_inc(conv_done, 1)
                if slot == 4:
                    for n in range(2):
                        wait(dve, decays, c(2, n + 1))
                        wait(dve, w_done, c(2, n))
                        dve.tensor_tensor(lru_tmp, lru_a[n], lru_a[n], ALU.mult).then_inc(w_step, 1)
                        dve.tensor_tensor(lru_i[n], lru_i[n], row(lru_xc[n]), ALU.mult)
                        wait(dve, w_step, c(2, n + 1))
                        dve.scalar_tensor_tensor(lru_w[n], lru_tmp, 1.0, lru_w[n], ALU.add, ALU.mult).then_inc(w_done, 1)
                if slot == 6:
                    for n in range(2):
                        wait(dve, root_done, c(2, n + 1))
                        dve.tensor_tensor(lru_i[n], lru_w[n], lru_i[n], ALU.mult).then_inc(u_done, 1)
                    for n in range(2):
                        wait(dve, u_done, c(2, n + 1))
                        dve.tensor_tensor_scan(lru_w[n][:, 0, :], lru_a[n][:, 0, :], lru_i[n][:, 0, :], 0.0, ALU.mult, ALU.add)
                        dve.tensor_tensor_scan(lru_w[n][:, 1, ::-1], lru_a[n][:, 1, ::-1], lru_i[n][:, 1, ::-1], 0.0, ALU.mult, ALU.add)\
                           .then_inc(scans_done, 1)
                    for n in range(2):
                        wait(dve, scans_done, c(2, n + 1))
                        dve.tensor_tensor(lru_w[n][:, 0, :], lru_w[n][:, 0, :], lru_w[n][:, 1, :], ALU.add).then_inc(dirs_summed, 1)
                    wait(dve, gr_done, c(1, 1) if before == 0 else 8)
                    for n in range(2):
                        wait(dve, dirs_summed, c(2, n + 1))
                        dve.tensor_tensor(lru_a[n][:, 0:1, :], lru_w[n][:, 0:1, :], gr[:, ix(c(2, n)), :], ALU.mult).then_inc(lru_y, 1)

            def lru_gate_events(slot, b):
                lru(slot, b, 0)
                if slot in (3, 7):
                    scaled_out(lru_gate, b, slot, gr[:, ix(b(4, 2 * (slot // 4)), 2), :])

            def q2_events(slot, b):
                lru(slot, b, 4)
                if slot in (3, 7):
                    scaled_out(in_q2, b, slot, q_late[:, ix(b(4, 2 * (slot // 4)), 2), :])

            def last_lru():
                for n in range(2):
                    dve.wait_ge(lru_hi, 15 + n)
                    dve.tensor_tensor(UL[:, 14 + n:15 + n, :], lru_a[n][:, 0:1, :], UH[:, 14 + n:15 + n, :].bitcast(f32), ALU.subtract)\
                       .then_inc(lru_lo, 1)
                dve.wait_ge(lru_lo, 16)

            def k2_events(slot, b):
                if slot in (3, 7):
                    scaled_out(in_k2, b, slot, k2[:, 2 * (slot // 4):2 * (slot // 4) + 2, :])

            def v2_events(slot, b):
                if slot in (3, 7):
                    o, p = taken(in_v2, b, slot), slot // 4
                    dve.tensor_tensor(v2[:, :, GC * p:GC * p + GC], o, col(rms_col[:, 0, :]), ALU.mult).then_inc(evac[p], 1)

            def qm_events(slot, b):
                if slot == 2:
                    wait(dve, k_rot, b(1, 1))
                    k = k2[:, ix(b()), :].rearrange("p a t -> p (a t)")
                    dve.tensor_tensor(k, k, cos_sin[:, 0, :], ALU.mult)
                    dve.tensor_tensor(scores2[:, 0, :], bank_a[:, 0, :], cos_sin[:, 1, :], ALU.mult).then_inc(k_cos, 1)
                    wait(dve, k_cos, b(1, 1))
                    dve.tensor_tensor(k, k, scores2[:, 0, :], ALU.add).then_inc(k_roped, 1)
                if slot in (3, 7):
                    scaled_out(in_qm, b, slot, qm[:, ix(b(4, 2 * (slot // 4)), 2), :])

            def local(slot, b):
                for n, (s0, s1, s2) in ((0, (0, 1, 2)), (1, (4, 5, 6))):
                    h = b.times(2).plus(n)
                    if slot == s0:
                        wait(dve, rot_done, h(1, H1 + 1))
                        dve.tensor_tensor(q_rot, q_late[:, ix(h()), :].rearrange("p a t -> p (a t)"), cos_sin[:, 0, :], ALU.mult)
                        dve.tensor_tensor(scores2[:, 0, :], bank_a[:, 0, :], cos_sin[:, 1, :], ALU.mult).then_inc(qk_sin, 1)
                        wait(dve, qk_sin, h(1, H1 + 1))
                        dve.tensor_tensor(q_rot, q_rot, scores2[:, 0, :], ALU.add).then_inc(rope_done, 1)
                    if slot == s1:
                        wait(dve, scores_done, h(1, H1 + 1))
                        dve.tensor_tensor(scores2, bank_s[:, :, :], masks[:, 0, :].rearrange("p (a t) -> p a t", a=2), ALU.add)\
                           .then_inc(masked, 1)
                        wait(dve, masked, h(1, H1 + 1))
                        dve.tensor_reduce(small[:, 21, 0:2], scores2, AX.X, ALU.max).then_inc(max_done, 1)
                        wait(dve, max_done, h(1, H1 + 1))
                        dve.scalar_tensor_tensor(small[:, 18, 0:2], small[:, 21, 0:2], SCALE, vec("sink", h(), 1).to_broadcast([P, 2]),
                                                 ALU.mult, ALU.max).then_inc(counted, 1)
                        wait(dve, counted, h(1, H1 + 1))
                        dve.tensor_scalar(small[:, 20, 0:2], small[:, 18, 0:2], -1.0, None, ALU.mult).then_inc(nmax_done, 1)
                    if slot == s2:
                        wait(dve, exp_done, h(1, H1 + 1))
                        dve.tensor_tensor(small[:, 17, 0:2], small[:, 19, 0:2], small[:, 19, 2:4], ALU.add).then_inc(den_done, 1)
                        wait(dve, den_done, h(1, H1 + 1))
                        dve.reciprocal(small[:, 17, 2:4], small[:, 17, 0:2]).then_inc(rden_done, 1)
                        wait(dve, rden_done, h(1, H1 + 1))
                        dve.tensor_tensor(probs2, probs2, col(small[:, 17, 2:4]), ALU.mult).then_inc(probs_done, 1)

            def memory(slot, b):
                h, half = b.halved(), b.c % 2
                if slot == 3 and half == 0:
                    wait(dve, scores_done, h(1, HEADS + 1))
                    dve.tensor_reduce(small[:, 21, 0:2], bank_s[:, :, :], AX.X, ALU.max).then_inc(max_done, 1)
                    dve.tensor_copy(m_probs, bank_s[:, :, :])
                    wait(dve, max_done, h(1, HEADS + 1))
                    dve.tensor_scalar(small[:, 20, 0:2], small[:, 21, 0:2], -M_SCALE, None, ALU.mult).then_inc(nmax_done, 1)
                if slot == 5 and half == 0:
                    wait(dve, exp_done, h(1, HEADS + 1))
                    dve.reciprocal(small[:, 17, 2:4], small[:, 19, 0:2]).then_inc(rden_done, 1)
                    wait(dve, rden_done, h(1, HEADS + 1))
                    dve.tensor_tensor(m_probs, m_probs, col(small[:, 17, 2:4]), ALU.mult).then_inc(probs_done, 1)

            def gates(g, n, slot, b):
                if slot == 3:
                    o = taken(g, b, 3)
                    dve.tensor_tensor(gate_space, o, row(rms[:, 0, :]), ALU.mult).then_inc(evac[0], 1)
                    wait(dve, evac[0], b(1, g.first + 1))
                    dve.tensor_tensor(gate_space, gate_space, col(vec("b_gate", b(2, 16 * n), 2)), ALU.add).then_inc(gate_biased, 1)
                if slot == 7:
                    o = taken(g, b, 7)
                    wait(dve, gate_sig, b(1, 8 * n + 1))
                    m = merged[:, ix(b(2), 2), :]
                    if n == 0:
                        dve.tensor_tensor(m, gate_space, o, ALU.mult).then_inc(evac[1], 1)
                        return
                    dve.tensor_tensor(gate_space, gate_space, o, ALU.mult).then_inc(evac[1], 1)
                    wait(dve, evac[1], b(1, g.first + 1))
                    ins = dve.tensor_tensor(m, m, gate_space, ALU.add)
                    ins.then_inc(merged_done, 1)

            def branch_events(n):
                def f(slot, b):
                    if n == 0:
                        local(slot, b)
                    if n == 1:
                        memory(slot, b)
                    gates(branches[n], n, slot, b)
                return f

            def operand(n, src, hi, lo):
                def f():
                    for c in range(4):
                        dve.wait_ge(op_hi, 4 * n + c + 1)
                        t = slice(4 * c, 4 * c + 4)
                        dve.tensor_tensor(lo[:, t, :], src[:, t, :], hi[:, t, :].bitcast(f32), ALU.subtract).then_inc(op_lo, 1)
                return f

            def out2_events(slot, b):
                if slot in (3, 7):
                    o, p = taken(out2, b, slot), slot // 4
                    dve.tensor_copy(qm[:, ix(b(4, 2 * p), 2), :], o).then_inc(evac[p], 1)

            def mixed():
                dve.wait_ge(stat_root, 6)
                link(dve.reciprocal(rms[:, 0, :], rms[:, 1, :]))
                for c in range(4):
                    for k in range(4 * c, 4 * c + 4):
                        ins = dve.scalar_tensor_tensor(qm[:, k, :], qm[:, k, :], vec("mix_post", k, 1), rms[:, 0, :], ALU.mult, ALU.mult)
                    link(ins)
                    t = slice(4 * c, 4 * c + 4)
                    dve.tensor_tensor(H[:, t, :], H[:, t, :], qm[:, t, :], ALU.add).then_inc(post_added, 1)
                    dve.wait_ge(pre_hi, c + 1)
                    for k in range(4 * c, 4 * c + 4):
                        ins = dve.scalar_tensor_tensor(XL[:, k, :], H[:, k, :], vec("mlp_pre", k, 1), XH[:, k, :].bitcast(f32),
                                                       ALU.mult, ALU.subtract)
                    ins.then_inc(pre_lo, 1)

            def up2_events(g, first):
                def f(slot, b):
                    if slot in (3, 7):
                        p = slot // 4
                        o = taken(g, b, slot)
                        if slot == 3 and first == 0 and isinstance(b(), int) and b() == 0:
                            dve.wait_ge(stat_root, 7)
                            link(dve.reciprocal(rms[:, 0, :], rms[:, 1, :]))
                        wait(dve, up_lo, b(2, first + p))
                        dve.tensor_tensor(up_space, o, row(rms[:, 0, :]), ALU.mult).then_inc(evac[p], 1)
                        wait(dve, evac[p], b(1, g.first + 1))
                        dve.scalar_tensor_tensor(up_space, up_space, 0.0, up_space, ALU.max, ALU.mult).then_inc(up_sq, 1)
                        wait(dve, up_hi, b(2, first + p + 1))
                        t = ix(b(4, 2 * p), 2)
                        dve.tensor_tensor(UL[:, t, :], up_space, UH[:, t, :].bitcast(f32), ALU.subtract).then_inc(up_lo, 1)
                return f

            def down2_events(g, n):
                def f(slot, b):
                    if slot in (3, 7):
                        o, p = taken(g, b, slot), slot // 4
                        y = qm[:, ix(b(4, 2 * p), 2), :]
                        if n == 0:
                            dve.tensor_copy(y, o).then_inc(evac[p], 1)
                        else:
                            dve.tensor_tensor(y, y, o, ALU.add).then_inc(evac[p], 1)
                return f

            late = stream(dve, lru_in, lower, late, lru_in_events, tail=block_norms)
            late = stream(dve, lru_gate, lower, late, lru_gate_events)
            late = stream(dve, in_q2, lower, late, q2_events)
            late = stream(dve, in_k2, lower, late, k2_events, tail=last_lru)
            late = stream(dve, in_v2, lower, late, v2_events)
            late = stream(dve, in_qm, lower, late, qm_events)
            dve.wait_ge(mask2_in, 16)
            late = stream(dve, branches[0], lower, late, branch_events(0))
            late = stream(dve, branches[1], lower, late, branch_events(1), tail=operand(0, q_late, UH, UL))
            late = stream(dve, branches[2], lower, late, branch_events(2), tail=operand(1, qm, UH, UL))
            late = stream(dve, out2, lower, late, out2_events, tail=operand(2, merged, XH, XL))
            for n, (up, down) in enumerate(ffn2):
                late = stream(dve, up, lower, late, up2_events(up, 8 * n), tail=mixed if n == 0 else None)
                late = stream(dve, down, lower, late, down2_events(down, n))
            late[0](6, late[1])
            late[0](7, late[1])
            dve.wait_ge(stat_root, 8)
            link(dve.reciprocal(rms[:, 0, :], rms[:, 1, :]))
            for c in range(4):
                for k in range(4 * c, 4 * c + 4):
                    ins = dve.scalar_tensor_tensor(qm[:, k, :], qm[:, k, :], vec("mlp_post", k, 1), rms[:, 0, :], ALU.mult, ALU.mult)
                link(ins)
                t = slice(4 * c, 4 * c + 4)
                dve.tensor_tensor(H[:, t, :], H[:, t, :], qm[:, t, :], ALU.add).then_inc(dve_step, 1)

        @block.gpsimd
        def _(pool):
            links = [0]

            def link(ins):
                links[0] += 1
                ins.then_inc(pool_link, 1)
                pool.wait_ge(pool_link, links[0])

            def sum_chunk(src, dst, zeroed):
                link(pool.tensor_tensor(squares, src, src, ALU.mult))
                for k in range(4):
                    if not zeroed and k == 0:
                        link(pool.tensor_copy(dst, squares[:, 0, :]))
                    else:
                        link(pool.tensor_tensor(dst, dst, squares[:, k, :], ALU.add))

            pool.dma_start(c_stage[:, :, :], A["c_re_im"][0]).then_inc(cs_in, 16)
            pool.memset(consts[:, 2:3], MAGIC)
            link(pool.memset(ones[:, :], 1.0))
            for n in range(4):
                pool.wait_ge(x_in[n], 16)
                sum_chunk(H[:, 4 * n:4 * n + 4, :], acc[:, 0, :], n > 0)
            pool.memset(small[:, 23, 0:1], 0.0).then_inc(stat_in, 1)
            for n in range(4):
                if n >= 2:
                    pool.wait_ge(ml_done, n - 1)
                    pool.dma_start(mem_raw[n % 2], A["mem"][:, 4 * n:4 * n + 4, :]).then_inc(mem_in[n], 16)
                pool.wait_ge(mem_in[n], 16)
                link(pool.tensor_tensor(squares, mem_raw[n % 2], mem_raw[n % 2], ALU.mult))
                pool.memset(small[:, 23, 1:2], 0.0).then_inc(mem_squared, 1)
                for k in range(4):
                    if n + k == 0:
                        link(pool.tensor_copy(acc[:, 1, :], squares[:, 0, :]))
                    else:
                        link(pool.tensor_tensor(acc[:, 1, :], acc[:, 1, :], squares[:, k, :], ALU.add))
            pool.memset(small[:, 23, 2:3], 0.0).then_inc(stat_in, 1)

            def cycles(s):
                pool.tensor_tensor(fcyc, steps[:, :], small[:, 6, ix(s())].to_broadcast([P, T]), ALU.mult).then_inc(cyc_half, 1)
                wait(pool, cyc_half, s(1, 1))
                pool.tensor_tensor(kcyc, fcyc, consts[:, 2:3].to_broadcast([P, T]), ALU.add).then_inc(cyc_done, 1)

            def pair(q, i, last=False):
                s = q.times(4).plus(i)
                wait(pool, pq_done, s(1, 1))
                pool.tensor_tensor(state_g[:, 0, :], prod_c[:, 0, :], prod_s[:, 1, :], ALU.add)
                pool.tensor_tensor(state_g[:, 1, :], prod_s[:, 0, :], prod_c[:, 1, :], ALU.subtract).then_inc(gin_done, 1)
                if i == 0 and not (isinstance(q(), int) and q() == 0):
                    wait(pool, y_done, q(4))
                    pool.dma_start(c_stage[:, :, :], A["c_re_im"][ix(q())].rearrange("a p k n -> p (a k) n")).then_inc(cs_in, 16)
                if not last:
                    cycles(s.plus(1))
                wait(pool, pq2_done, s(1, 1))
                wait(pool, y_done, s())
                pool.tensor_tensor(state_h[:, 0, :], prod_c[:, 0, :], prod_s[:, 1, :], ALU.add)
                pool.tensor_tensor(state_h[:, 1, :], prod_c[:, 1, :], prod_s[:, 0, :], ALU.subtract).then_inc(h_done, 1)
                if i == 3 and not last:
                    pool.dma_start(b_stage[:, :, :], bt_scratch[ix(q(1, 1))].rearrange("a p k n -> p (a k) n")).then_inc(bs_in, 16)

            pool.wait_ge(bt_out, 16)
            pool.dma_start(b_stage[:, :, :], bt_scratch[0]).then_inc(bs_in, 16)
            cycles(At(None, 0, 0))
            for i in range(4):
                pair(At(None, 0, 0), i)
            with pool.Fori(1, UT - 1) as r:
                for i in range(4):
                    pair(At(r, 1, 0), i)
            for i in range(4):
                pair(At(None, 0, UT - 1), i, last=i == 3)

            h_flat = H[:, :, :].rearrange("p k t -> p (k t)")

            def sum_two(r, p, dst, value, gained=False):
                pool.wait_ge(sq_step, value)
                t = h_flat[:, bass.ds(r * (4 * T) + 2 * T * p, 2 * T)] if gained else H[:, bass.ds(r * 4 + 2 * p, 2), :]
                o = squares[:, 0:2, :]
                pool.tensor_tensor(o.rearrange("p k t -> p (k t)") if gained else o, t, t, ALU.mult).then_inc(sq_step, 1)
                pool.wait_ge(sq_step, value + 1)
                pool.tensor_tensor(dst, dst, squares[:, 0, :], ALU.add).then_inc(sq_step, 1)
                pool.wait_ge(sq_step, value + 2)
                pool.tensor_tensor(dst, dst, squares[:, 1, :], ALU.add).then_inc(sq_step, 1)

            for n in range(2):
                pool.wait_ge(memkv_out[n], 16 * 8)
            pool.wait_ge(stat_mm, 2)
            pool.memset(acc[:, :, :], 0.0).then_inc(sq_step, 1)
            with pool.Fori(0, out_ssm.bodies) as r:
                for p in range(2):
                    pool.wait_ge(evac[p], r + (out_ssm.first + 1))
                    sum_two(r, p, acc[:, 0, :], r * 6 + (3 * p + 1))
            pool.memset(small[:, 23, 3:4], 0.0).then_inc(stat_in, 1)
            pool.wait_ge(stat_mm, 3)
            link(pool.memset(acc[:, :, :], 0.0))
            down = ffn1[2][1]
            with pool.Fori(0, down.bodies) as r:
                for p in range(2):
                    v = 1 + 3 * 2 * out_ssm.bodies + 6 * p
                    pool.wait_ge(evac[p], r + (down.first + 1))
                    sum_two(r, p, acc[:, 0, :], r * 12 + v)
                    pool.memset(small[:, 23, 4:5], 0.0).then_inc(res_sq, 1)
                    pool.wait_ge(res_done, r * 2 + (p + 1))
                    sum_two(r, p, acc[:, 1, :], r * 12 + (v + 3), gained=True)
            pool.memset(small[:, 23, 5:6], 0.0).then_inc(stat_in, 1)

            pool.wait_ge(lru_consts, 1)
            for n in range(2):
                pool.dma_start(lru_weights[n], A["w_lru_gates"][n]).then_inc(lw_in[n], 16)
            with pool.Fori(1, 8) as r:
                for n in range(2):
                    pool.wait_ge(lru_mm, r * 2 + (n - 1))
                    pool.dma_start(lru_weights[n], A["w_lru_gates"][bass.ds(r * 2 + n, 1)].rearrange("a p m n -> p (a m) n"))\
                        .then_inc(lw_in[n], 16)
            pool.wait_ge(lru_mm, 16)
            pool.dma_start(masks[:, 0, :], A["mask2"]).then_inc(mask2_in, 16)
            pool.wait_ge(oh_done, H1 + 16)
            with pool.Fori(0, 4) as r:
                pool.wait_ge(pv_done, r + HEADS)
                for n in range(2):
                    pool.dma_start(mk[:, 2 * n:2 * n + 2, :], memk_scratch[bass.ds(r * 2 + n, 1)].rearrange("a p k t -> p (a k) t"))\
                        .then_inc(mkv_in, 16)
                    pool.dma_start(mv[:, 2 * n:2 * n + 2, :], memv_scratch[bass.ds(r * 2 + n, 1)].rearrange("a p k t -> p (a k) t"))\
                        .then_inc(mkv_in, 16)

            def sum_tiles(src, g, v0):
                link(pool.memset(acc[:, 0, :], 0.0))
                with pool.Fori(0, g.bodies) as r:
                    for p in range(2):
                        pool.wait_ge(evac[p], r + (g.first + 1))
                        v = v0 + 3 * p
                        pool.wait_ge(sq_step, r * 6 + v)
                        t = src[:, bass.ds(r * 4 + 2 * p, 2), :]
                        pool.tensor_tensor(squares[:, 0:2, :], t, t, ALU.mult).then_inc(sq_step, 1)
                        pool.wait_ge(sq_step, r * 6 + (v + 1))
                        pool.tensor_tensor(acc[:, 0, :], acc[:, 0, :], squares[:, 0, :], ALU.add).then_inc(sq_step, 1)
                        pool.wait_ge(sq_step, r * 6 + (v + 2))
                        pool.tensor_tensor(acc[:, 0, :], acc[:, 0, :], squares[:, 1, :], ALU.add).then_inc(sq_step, 1)
                pool.memset(small[:, 23, 6:7], 0.0).then_inc(stat_in, 1)
                return v0 + 6 * g.bodies

            pool.wait_ge(oh_done, HEADS + 4)
            steps_done = sum_tiles(qm, out2, 1 + 18 * out_ssm.bodies)
            pool.wait_ge(stat_mm, 6)
            for c in range(4):
                pool.wait_ge(post_added, c + 1)
                sum_chunk(H[:, 4 * c:4 * c + 4, :], acc[:, 0, :], c > 0)
            pool.memset(small[:, 23, 7:8], 0.0).then_inc(stat_in, 1)
            pool.wait_ge(stat_mm, 7)
            sum_tiles(qm, ffn2[3][1], steps_done)


def tiled(w):
    k, n = w.shape
    kt = k // P // UNITS
    return np.ascontiguousarray(w.reshape(UNITS, kt, P, n // GC, GC).transpose(3, 0, 2, 1, 4)
                                .reshape(n // GC, UNITS, P, kt * GC))


def paired(a, b):
    a, b = tiled(a), tiled(b)
    return np.ascontiguousarray(np.stack([a, b], 1).reshape(2 * a.shape[0], *a.shape[1:]))


def by_partition(v, n=None):
    return v.reshape(-1, P).T


def laid_out(i):
    A = {}
    A["x"] = i["x"][0].T.reshape(KT, P, T).transpose(1, 0, 2)
    A["mem"] = i["mem_2"][0].T.reshape(KT, P, T).transpose(1, 0, 2)
    w = i["w_in"][0]
    A["w_in_u"], A["w_in_qk"], A["w_in_v"] = tiled(w[:, 3 * AW:]), tiled(w[:, :2 * AW]), tiled(w[:, 2 * AW:3 * AW])
    A["w_mem_k"], A["w_mem_v"] = tiled(i["w_mem_kv_2"][0][:, :D]), tiled(i["w_mem_kv_2"][0][:, D:])
    A["w_out_attn"], A["w_out_ssm"] = tiled(i["w_out"][0][:AW]), tiled(i["w_out"][0][AW:])
    A["w_glu"] = tiled(i["w_glu"][0])
    for c, (a, b) in enumerate(((0, 2048), (2048, 4096), (4096, FF1))):
        A[f"w_gu{c}"] = paired(i["w_gate"][0][:, a:b], i["w_up"][0][:, a:b])
        A[f"w_dn{c}"] = tiled(i["w_down"][0][a:b])
    at = {}
    start = 0
    for name, n in (("xr", D), ("gr", D), ("q", D), ("k", 512), ("v", 512), ("qm", D), ("g0", D), ("g1", D), ("g2", D)):
        at[name] = i["w_in_2"][0][:, start:start + n]
        start += n
    A["w_lru_in"], A["w_lru_gate"], A["w_in_q2"] = tiled(at["xr"]), tiled(at["gr"]), tiled(at["q"])
    A["w_in_k2"], A["w_in_v2"], A["w_in_qm"] = tiled(at["k"]), tiled(at["v"]), tiled(at["qm"])
    for n, name in enumerate(("w_br_lru_2", "w_br_attn_2", "w_br_mem_2")):
        A[f"w_branch{n}"] = paired(at[f"g{n}"], i[name][0])
    A["w_out2"] = tiled(i["w_out_2"][0])
    for c in range(4):
        A[f"w_up{c}"] = tiled(i["w_up_2"][0][:, D * c:D * c + D])
        A[f"w_down{c}"] = tiled(i["w_down_2"][0][D * c:D * c + D])
    A["w_lru_gates"] = np.stack([i[n][0] for n in ("wr_f_2", "wr_b_2", "wi_f_2", "wi_b_2")], 2)
    A["positions"] = np.broadcast_to(i["positions_2"].astype(np.int32).reshape(1, T), (P, T))
    v = {"norm1": i["norm1_g"][0], "norm2": i["norm2_g"][0], "final": i["final_g"], "mem": i["norm_mem_2"][0],
         "mix_pre": i["norm_mix_pre_2"][0], "mix_post": i["norm_mix_post_2"][0], "mlp_pre": i["norm_mlp_pre_2"][0],
         "mlp_post": i["norm_mlp_post_2"][0], "b_glu": i["b_glu"][0], "d_skip": i["d_skip"][0].reshape(-1),
         "a_re": i["a_re"][0].reshape(-1), "a_im": i["a_im"][0].reshape(-1), "log_dt": np.repeat(i["log_dt"][0], 64),
         "b_gate": i["b_gate_2"][0], "conv_w": i["conv_w_2"][0].reshape(-1), "conv_b": i["conv_b_2"][0],
         "br": np.concatenate([i["br_f_2"][0].reshape(-1), i["br_b_2"][0].reshape(-1)]),
         "bi": np.concatenate([i["bi_f_2"][0].reshape(-1), i["bi_b_2"][0].reshape(-1)]),
         "lam": np.concatenate([i["lam_f_2"][0], i["lam_b_2"][0]])}
    cols = []
    for name, (_, n) in VEC.items():
        if name == "sink":
            cols.append(np.broadcast_to(i["attn_sink_2"][0][None, :], (P, n)))
        elif name == "freq":
            half = HD // 2
            f = (10000.0 ** (-np.arange(half, dtype=np.float32) / np.float32(half))).astype(np.float32)
            cols.append(np.concatenate([f, f])[:, None])
        else:
            cols.append(by_partition(v[name]))
    A["vecs"] = np.concatenate(cols, 1)
    A["ident"] = np.eye(P, dtype=np.float32)
    rot = np.zeros((P, P), np.float32)
    for a in range(16):
        rot[a + 16, a], rot[a, a + 16] = -1.0, 1.0
    A["rotate1"] = rot
    rot2 = np.zeros((P, P), np.float32)
    for a in range(64):
        rot2[a + 64, a], rot2[a, a + 64] = -1.0, 1.0
    A["rotate2"] = rot2
    near = np.abs(np.arange(T)[:, None] - np.arange(T)[None, :]) <= 128
    A["mask2"] = np.where(near, 0.0, NEG).astype(np.float32).reshape(2, P, T).transpose(1, 0, 2).reshape(P, 2 * T)
    A["steps"] = np.broadcast_to(np.arange(T, dtype=np.float32)[None, :], (P, T))
    inv = (500000.0 ** (-np.arange(0, 32, 2) / 32)).astype(np.float32)
    ang = (np.arange(T, dtype=np.float32)[:, None] * inv[None, :]).astype(np.float64)
    cs = np.zeros((P, 2, T), np.float32)
    cs[:, 0] = 1.0
    for a in (0, 16):
        cs[a:a + 16, 0], cs[a:a + 16, 1] = np.cos(ang).T, np.sin(ang).T
    A["cos_sin"] = cs
    q = np.arange(T)[:, None]
    k = np.arange(T)[None, :]
    count = sum(((k <= q) & ((q - k) % d == 0) & (q - k <= w)).astype(np.float32) for w, d in ((128, 1), (512, 4), (2048, 16)))
    both = np.stack([np.where(count > 0, 0.0, NEG).astype(np.float32), count])
    A["masks1"] = both.reshape(2, 2, P, T).transpose(2, 0, 1, 3).reshape(P, 2, 2 * T)
    for name, b in (("b_re", i["b_re"][0]), ("b_im", i["b_im"][0])):
        m = np.zeros((2, 64, PAIRS, 2, 16), np.float32)
        for g in range(2):
            m[g, :, :, g, :] = b.reshape(PAIRS, 2, 64, 16)[:, g].transpose(1, 0, 2)
        A[name] = m.reshape(P, PAIRS, 32)
    cc = np.zeros((UT, 2, 64, 2, 4, 2, 16), np.float32)
    for r, c in enumerate((i["c_re"][0], i["c_im"][0])):
        for g in range(2):
            cc[:, g, :, r, :, g, :] = c.reshape(UT, 4, 2, 16, 64)[:, :, g].transpose(0, 3, 1, 2)
    A["c_re_im"] = cc.reshape(UT, P, 2, P)
    return {k: np.ascontiguousarray(v, dtype=np.float32) if v.dtype.kind == "f" else np.ascontiguousarray(v)
            for k, v in A.items()}


def kernel(**inputs):
    import concourse.bacc as bacc
    from concourse.bass_utils import run_bass_kernel_spmd

    nc = bacc.Bacc("TRN2", target_bir_lowering=False, num_devices=1, dynamic_dma_scratch_size=4096)
    arrays = laid_out({k: np.asarray(v) for k, v in inputs.items()})
    aps = {k: nc.dram_tensor("in_" + k, v.shape, mybir.dt.from_np(v.dtype), kind="ExternalInput").ap()
           for k, v in arrays.items()}
    out = nc.dram_tensor("out_x", (P, KT, T), mybir.dt.float32, kind="ExternalOutput").ap()
    program(nc, aps, out)
    got = run_bass_kernel_spmd(nc, [{"in_" + k: v for k, v in arrays.items()}], core_ids=[0]).results[0]["out_x"]
    return np.ascontiguousarray(got.transpose(1, 0, 2).reshape(D, T).T[None])
```

```python
import math
from contextlib import ExitStack

import numpy as np
import concourse.bass as bass
from concourse import mybir

D = 2048
T = 256
P = 128
KT = D // P
AW = 1024
HD = 128
H1 = AW // HD
HEADS = H1 + D // HD
STATES = 64 * 64
PAIRS = STATES // P
UT = AW // P
FF1, FF2 = 5632, 8192
GC = 256
UNITS = 4
SLOTS = 8
RING = 4
LAG = 3
M_SCALE = 512 ** -0.5
EPS = 1e-6
SCALE = float(HD) ** -0.5
MAGIC = 12582912.0
TWO_PI = 6.283185
NEG = -1e30

VEC = {}
for _name, _n in (("norm1", 16), ("norm2", 16), ("final", 16), ("mem", 16), ("mix_pre", 16), ("mix_post", 16),
                  ("mlp_pre", 16), ("mlp_post", 16), ("b_glu", 8), ("d_skip", 8), ("a_re", 32), ("a_im", 32),
                  ("log_dt", 32), ("b_gate", 48), ("conv_w", 64), ("conv_b", 16), ("br", 32), ("bi", 32),
                  ("lam", 32), ("sink", 16), ("freq", 1)):
    VEC[_name] = (sum(n for _, n in VEC.values()), _n)
NVEC = sum(n for _, n in VEC.values())


class At:

    def __init__(self, reg, k, c):
        self.reg, self.k, self.c = reg, k, c

    def __call__(self, mul=1, add=0):
        c = mul * self.c + add
        if self.reg is None:
            return c
        e = self.reg if mul * self.k == 1 else self.reg * (mul * self.k)
        return e + c if c > 0 else e - (-c) if c < 0 else e

    def plus(self, n):
        return At(self.reg, self.k, self.c + n)

    def before(self):
        return self.plus(-1)

    def times(self, n):
        return At(self.reg, self.k * n, self.c * n)

    def halved(self):
        return At(self.reg, self.k // 2, self.c // 2)


def wait(eng, sem, value):
    if not isinstance(value, int) or value > 0:
        eng.wait_ge(sem, value)


def ix(value, n=1):
    return slice(value, value + n) if isinstance(value, int) else bass.ds(value, n)


class Gemm:

    bodies_before = 0

    def __init__(self, w, bodies, unroll=1):
        self.w, self.bodies, self.unroll = w, bodies, unroll
        self.kt = w.shape[3] // GC
        self.first = Gemm.bodies_before
        Gemm.bodies_before += bodies

    def stretches(self, eng, peel):
        u = self.unroll
        for c in range(u if peel else 0):
            yield At(None, 0, c), c
        rest = self.bodies // u - (1 if peel else 0)
        start = 1 if peel else 0
        if rest == 1:
            for c in range(u):
                yield At(None, 0, start * u + c), c
        elif rest > 1:
            with eng.Fori(start, self.bodies // u) as r:
                for c in range(u):
                    yield At(r, u, c), c


def program(nc, A, out):
    f32, f32r, i32 = mybir.dt.float32, mybir.dt.float32r, mybir.dt.int32
    ACT, ALU, AX = mybir.ActivationFunctionType, mybir.AluOpType, mybir.AxisListType
    Gemm.bodies_before = 0

    in_u = Gemm(A["w_in_u"], 2, unroll=2)
    in_qk = Gemm(A["w_in_qk"], 4, unroll=2)
    in_v = Gemm(A["w_in_v"], 2, unroll=2)
    mem_k = Gemm(A["w_mem_k"], 4, unroll=2)
    mem_v = Gemm(A["w_mem_v"], 4, unroll=2)
    out_attn = Gemm(A["w_out_attn"], 4, unroll=4)
    glu = Gemm(A["w_glu"], 2, unroll=2)
    out_ssm = Gemm(A["w_out_ssm"], 4)
    ffn1 = []
    for c in range(3):
        up, down = A[f"w_gu{c}"], A[f"w_dn{c}"]
        ffn1.append((Gemm(up, up.shape[0] // 2), Gemm(down, down.shape[0] // 2)))
    lru_in, lru_gate = Gemm(A["w_lru_in"], 4), Gemm(A["w_lru_gate"], 4)
    in_q2 = Gemm(A["w_in_q2"], 4)
    in_k2, in_v2 = Gemm(A["w_in_k2"], 1), Gemm(A["w_in_v2"], 1)
    in_qm = Gemm(A["w_in_qm"], 4)
    branches = [Gemm(A[f"w_branch{n}"], 8, unroll=2 if n < 2 else 1) for n in range(3)]
    out2 = Gemm(A["w_out2"], 4)
    ffn2 = [(Gemm(A[f"w_up{c}"], 4), Gemm(A[f"w_down{c}"], 4)) for c in range(4)]
    stages = [in_u, in_qk, in_v, mem_k, mem_v, out_attn, glu, out_ssm] + [g for pair in ffn1 for g in pair]
    stages += [lru_in, lru_gate, in_q2, in_k2, in_v2, in_qm] + branches + [out2] + [g for pair in ffn2 for g in pair]

    ctx = ExitStack()
    with ctx:
        def sb(name, shape, dt=f32):
            return ctx.enter_context(nc.sbuf_tensor(name, shape, dt))

        def sem(name):
            return ctx.enter_context(nc.semaphore(name))

        RAW = sb("weights", [P, RING, UNITS * GC])
        HI = sb("weights_hi", [P, RING, UNITS * GC], f32r)
        LO = sb("weights_lo", [P, RING, UNITS * GC], f32r)
        XH = sb("x_hi", [P, KT, T], f32r)
        XL = sb("x_lo", [P, KT, T], f32r)
        UH = sb("u_hi", [P, KT, T], f32r)
        UL = sb("u_lo", [P, KT, T], f32r)
        H = sb("residual", [P, KT, T])
        ZP = sb("projections", [P, 2 * KT, T])
        Q2 = sb("late", [P, 4096])
        WK = sb("work", [P, 4096])
        vecs = sb("vecs", [P, NVEC])
        ident = sb("ident", [P, P])
        ones = sb("ones", [P, P])
        rotate = sb("rotate", [P, P])
        steps = sb("steps", [P, T])
        cos_sin = sb("cos_sin", [P, 2, T])
        masks = sb("masks", [P, 2, 2 * T])
        rms = sb("rms", [P, 2, T])
        rms_col = sb("rms_col", [P, 2, 2])
        acc = sb("squares", [P, 2, T])
        small = sb("small", [P, 24, 32])
        consts = sb("consts", [P, 4])

        def vec(name, a=0, n=None):
            start, size = VEC[name]
            n = size - a if n is None else n
            return vecs[:, start + a:start + a + n] if isinstance(a, int) else vecs[:, bass.ds(a + start, n)]

        def view(buf, at, shape):
            n = int(np.prod(shape))
            v = buf[:, at:at + n]
            return v if len(shape) == 1 else v.rearrange("p (a b) -> p a b", b=shape[1])
        q2, wk = Q2, WK
        fcyc, kcyc, acyc = view(q2, 0, [T]), view(q2, 256, [T]), view(q2, 512, [T])
        sin_t = [view(q2, 768 + 512 * n, [T]) for n in range(2)]
        cos_t = [view(q2, 1024 + 512 * n, [T]) for n in range(2)]
        prod_c, prod_s = view(q2, 1792, [2, T]), view(q2, 2304, [2, T])
        state_g, state_h = view(q2, 2816, [2, T]), view(q2, 3328, [2, T])
        b_stage, c_stage = view(q2, 3840, [2, P]), view(wk, 2816, [2, P])
        qk_rot, rot_tmp = view(wk, 0, [2, T]), view(wk, 512, [2, T])
        probs, probs_t = view(wk, 1024, [2, T]), view(wk, 1536, [2, T])
        v_stage = view(wk, 2048, [2, P])
        u_stage = view(wk, 2304, [T])
        mem_raw = [view(wk, 0, [4, T]), view(wk, 1024, [4, T]), ZP[:, 24:28, :], ZP[:, 28:32, :]]
        b_raw = [view(q2, 0, [PAIRS, 32]), view(q2, 1024, [PAIRS, 32])]
        b_bar = [view(q2, 2048, [PAIRS, 32]), view(q2, 3072, [PAIRS, 32])]
        squares = view(wk, 3072, [4, T])
        mem_stage = [view(wk, 3072, [2, T]), view(wk, 3584, [2, T])]
        b_flat = Q2[:, 0:2048]
        block_sum = [ZP[:, 8 + 2 * n:10 + 2 * n, :] for n in range(2)]
        gate_space = masks[:, 1, :].rearrange("p (a t) -> p a t", a=2)
        up_space = view(wk, 0, [2, T])
        xr, gr = ZP[:, 0:KT, :], ZP[:, KT:2 * KT, :]
        qm, merged = ZP[:, 0:KT, :], ZP[:, KT:2 * KT, :]
        q_late = Q2[:, :].rearrange("p (a t) -> p a t", t=T)
        lru_xc = [view(wk, 1792 * n, [T]) for n in range(2)]
        lru_a = [view(wk, 1792 * n + 256, [2, T]) for n in range(2)]
        lru_w = [view(wk, 1792 * n + 768, [2, T]) for n in range(2)]
        lru_i = [view(wk, 1792 * n + 1280, [2, T]) for n in range(2)]
        lru_tmp = [view(wk, 3584, [2, T]), acc[:, :, :]]
        lru_weights = [masks[:, n, :].rearrange("p (m n) -> p m n", m=4) for n in range(2)]
        pos_raw, ang, ang_tmp = wk[:, 0:T], wk[:, 256:512], wk[:, 512:768]
        k2, v2 = view(wk, 0, [4, T]), view(wk, 1024, [2, 4 * P])
        q_rot, scores2 = view(wk, 2048, [T]), view(wk, 2304, [2, T])
        probs2_t, v2_stage = view(wk, 2816, [2, T]), view(wk, 3328, [2, P])
        probs2 = view(wk, 3584, [2, T])
        qm_stage, mk, mv = view(wk, 0, [4, T]), view(wk, 1024, [4, T]), view(wk, 2048, [4, GC])
        m_probs, m_probs_t = view(wk, 3072, [2, T]), view(wk, 3584, [2, T])
        values = ZP[:, 3 * UT:4 * UT, :].rearrange("p a t -> p (a t)").rearrange("p (k c) -> p k c", k=2)
        by_head = ZP[:, :, :].rearrange("p (a b) t -> p b a t", b=H1)

        def heads(h, first, n):
            v = by_head[:, ix(h()), first:first + n, :]
            return v.rearrange("p b a t -> p (b a) t") if n > 1 else v.rearrange("p b a t -> p (b a t)")

        def v_head(h):
            return values[:, :, ix(h(HD), HD)]
        bt_scratch = nc.dram_tensor("b_scratch", [UT, P, 2, P], f32).ap()
        memk_scratch = nc.dram_tensor("memk_scratch", [8, P, 2, T], f32).ap()
        memv_scratch = nc.dram_tensor("memv_scratch", [8, P, 2, T], f32).ap()

        GP = ctx.enter_context(nc.psum_tensor("gemm_psum", [P, 4, 512], f32))
        bank_a = ctx.enter_context(nc.psum_tensor("bank_a", [P, 2, T], f32))
        bank_s = ctx.enter_context(nc.psum_tensor("bank_s", [P, 2, T], f32))
        bank_b = ctx.enter_context(nc.psum_tensor("bank_b", [P, 2, T], f32))
        bank_y = ctx.enter_context(nc.psum_tensor("bank_y", [P, 2, T], f32))

        raw_in = [sem(f"raw_in{n}") for n in range(RING)]
        evac = [sem(f"evac{n}") for n in range(2)]
        x_in = [sem(f"x_in{n}") for n in range(4)]
        mem_in = [sem(f"mem_in{n}") for n in range(4)]
        memkv_out = [sem("memkv_out0"), sem("memkv_out1")]
        lw_in = [sem("lru_weights_in0"), sem("lru_weights_in1")]
        stored = [sem(f"stored{n}") for n in range(4)]
        vecs_in, tabs_in, b_in, xh_done = sem("vecs_in"), sem("tabs_in"), sem("b_in"), sem("xh_done")
        xl_done, mh_done, ml_done = sem("xl_done"), sem("mh_done"), sem("ml_done")
        stat_in, stat_mm, stat_root, norm_part = sem("stat_in"), sem("stat_mm"), sem("stat_root"), sem("norm_part")
        pool_link, dve_link, act_link, sq_step = sem("pool_link"), sem("dve_link"), sem("act_link"), sem("sq_step")
        hi_done, lo_done, mm_done = sem("hi_done"), sem("lo_done"), sem("mm_done")
        angle_in, theta_done, angle_done, bbar_done = sem("angle_in"), sem("theta_done"), sem("angle_done"), sem("bbar_done")
        bt_done, bt_copied, bt_out, cyc_half = sem("bt_done"), sem("bt_copied"), sem("bt_out"), sem("cyc_half")
        cyc_done, frac_done, abs_done, trig_done = sem("cyc_done"), sem("frac_done"), sem("abs_done"), sem("trig_done")
        bu_done, pq_done, gin_done, scan_done = sem("bu_done"), sem("pq_done"), sem("gin_done"), sem("scan_done")
        pq2_done, h_done, y_done, yt_done = sem("pq2_done"), sem("h_done"), sem("y_done"), sem("yt_done")
        bs_in, cs_in, us_done = sem("bs_in"), sem("cs_in"), sem("us_done")
        rot_done, qk_sin, rope_done, scores_done = sem("rot_done"), sem("qk_sin"), sem("rope_done"), sem("scores_done")
        masked, max_done, nmax_done, exp_done = sem("masked"), sem("max_done"), sem("nmax_done"), sem("exp_done")
        counted, den_done, rden_done, probs_done = sem("counted"), sem("den_done"), sem("rden_done"), sem("probs_done")
        pt_done, pt_copied, vs_done, pv_done = sem("pt_done"), sem("pt_copied"), sem("vs_done"), sem("pv_done")
        oh_done, ol_done, mask2_in, k_rot = sem("oh_done"), sem("ol_done"), sem("mask2_in"), sem("k_rot")
        k_cos, k_roped, mkv_in, qm_staged = sem("k_cos"), sem("k_roped"), sem("mkv_in"), sem("qm_staged")
        lam_exp, lru_consts, gated_in, conv_step = sem("lam_exp"), sem("lru_consts"), sem("gated_in"), sem("conv_step")
        conv_done, lru_mm, sig_gates, gap_done = sem("conv_done"), sem("lru_mm"), sem("sig_gates"), sem("gap_done")
        decays, a_squared, w_done, root_done = sem("decays"), sem("a_squared"), sem("w_done"), sem("root_done")
        u_done, scans_done, dirs_summed, lru_y = sem("u_done"), sem("scans_done"), sem("dirs_summed"), sem("lru_y")
        lru_hi, lru_lo, gr_done = sem("lru_hi"), sem("lru_lo"), sem("gr_done")
        x_final, yh_done, yl_done, gated = sem("x_final"), sem("yh_done"), sem("yl_done"), sem("gated")
        gh_done, gl_done, res_done, res_g = sem("gh_done"), sem("gl_done"), sem("res_done"), sem("res_g")
        res_hi, res_lo, res_sq, silu_done = sem("res_hi"), sem("res_lo"), sem("res_sq"), sem("silu_done")
        act_gated, act_hi, act_lo, pos_in = sem("act_gated"), sem("act_hi"), sem("act_lo"), sem("pos_in")
        rotate2_in, turn_done, op_hi, op_lo = sem("rotate2_in"), sem("turn_done"), sem("op_hi"), sem("op_lo")
        gate_sig, merged_done, gate_biased, post_added = sem("gate_sig"), sem("merged_done"), sem("gate_biased"), sem("post_added")
        pre_hi, pre_lo, up_sq, up_hi = sem("pre_hi"), sem("pre_lo"), sem("up_sq"), sem("up_hi")
        up_lo = sem("up_lo")

        block = ctx.enter_context(nc.Block())

        @block.sync
        def _(sp):
            sp.dma_start(vecs[:, :], A["vecs"]).then_inc(vecs_in, 16)
            for n in range(4):
                sp.dma_start(H[:, 4 * n:4 * n + 4, :], A["x"][:, 4 * n:4 * n + 4, :]).then_inc(x_in[n], 16)
            for g in stages:
                for b, _ in g.stretches(sp, peel=g is in_u):
                    for j in range(SLOTS):
                        wait(sp, lo_done, b(SLOTS, SLOTS * g.first + j - RING + 1))
                        sp.dma_start(RAW[:, j % RING:j % RING + 1, 0:g.kt * GC],
                                     g.w[ix(b(2, j // UNITS)), j % UNITS].rearrange("a p n -> p a n"))\
                          .then_inc(raw_in[j % RING], 16)
            for n in range(4):
                sp.wait_ge(x_final, n + 1)
                sp.dma_start(out[:, 4 * n:4 * n + 4, :], H[:, 4 * n:4 * n + 4, :]).then_inc(stored[n], 16)
            for n in range(4):
                sp.wait_ge(stored[n], 16)

        @block.tensor
        def _(pe):
            def units(g, b, j, operands, tokens_out=False):
                p = j // UNITS
                wait(pe, lo_done, b(SLOTS, SLOTS * g.first + j + 1))
                if j % UNITS == 0:
                    wait(pe, evac[p], b(1, g.first))
                xh, xl, off = operands
                for n in range(2):
                    for k in range(g.kt):
                        kk = off + (j % UNITS) * g.kt + k
                        first, end = j % UNITS == 0 and k == 0, j % UNITS == UNITS - 1 and k == g.kt - 1
                        o = GP[:, 2 * p + n, 0:T]
                        if tokens_out:
                            cols = slice(k * GC, (k + 1) * GC)
                            wh, wl = HI[:, j % RING, cols], LO[:, j % RING, cols]
                            ah, al = xh[:, kk, n * P:(n + 1) * P], xl[:, kk, n * P:(n + 1) * P]
                            pe.matmul(o, ah, wh, start=first, stop=False)
                            pe.matmul(o, al, wh, start=False, stop=False)
                            mm = pe.matmul(o, ah, wl, start=False, stop=end)
                        else:
                            cols = slice(k * GC + n * P, k * GC + (n + 1) * P)
                            wh, wl = HI[:, j % RING, cols], LO[:, j % RING, cols]
                            pe.matmul(o, wh, xh[:, kk, :], start=first, stop=False)
                            pe.matmul(o, wh, xl[:, kk, :], start=False, stop=False)
                            mm = pe.matmul(o, wl, xh[:, kk, :], start=False, stop=end)
                mm.then_inc(mm_done, 1)

            def ssm_in(q, i):
                wait(pe, pq_done, q(4, i))
                wait(pe, bs_in, q(16, 16))
                wait(pe, us_done, q(1, 1))
                rows = slice(32 * i, 32 * i + 32)
                for n in range(2):
                    mm = pe.matmul(bank_b[:, n, :], b_stage[rows, n, :], u_stage[rows, :],
                                   start=True, stop=True)
                mm.then_inc(bu_done, 1)

            def ssm_out(q, i):
                wait(pe, h_done, q(4, i + 1))
                if i == 0:
                    wait(pe, cs_in, q(16, 16))
                    wait(pe, yt_done, q())
                o = bank_y[32 * i:32 * i + 32, 0, :]
                pe.matmul(o, c_stage[:, 0, 32 * i:32 * i + 32], state_h[:, 0, :], start=True, stop=False)
                pe.matmul(o, c_stage[:, 1, 32 * i:32 * i + 32], state_h[:, 1, :], start=False, stop=True)\
                  .then_inc(y_done, 1)

            def ssm(slot, b, q0):
                q, half = b.halved().plus(q0), b.c % 2
                if slot == 0:
                    ssm_in(q, 2 * half)
                if slot == 2:
                    if half:
                        ssm_out(q, 1)
                    elif not (isinstance(q(), int) and q() == 0):
                        ssm_out(q.before(), 3)
                if slot == 4:
                    ssm_in(q, 2 * half + 1)
                if slot == 6:
                    ssm_out(q, 2 * half)

            def attention(slot, h):
                first = isinstance(h(), int) and h() == 0
                if slot == 0 and not first:
                    turned(h.before())
                if slot == 1 and not first:
                    pv(h.before())
                if slot == 2:
                    wait(pe, ol_done, h())
                    if isinstance(h(), int) and h() == 0:
                        pe.wait_ge(evac[1], in_v.first + in_v.bodies)
                    pe.matmul(bank_a[:, 0, :], rotate[:, :], heads(h, 1, 1), start=True, stop=True)
                    pe.matmul(bank_a[:, 1, :], rotate[:, :], heads(h, 2, 1), start=True, stop=True).then_inc(rot_done, 1)
                if slot == 4:
                    wait(pe, rope_done, h(1, 1))
                    wait(pe, pt_copied, h())
                    for n in range(2):
                        mm = pe.matmul(bank_s[:, n, :], qk_rot[:, 0, n * P:(n + 1) * P], qk_rot[:, 1, :],
                                       start=True, stop=True)
                    mm.then_inc(scores_done, 1)

            def turned(h):
                wait(pe, probs_done, h(1, 1))
                for kt in range(2):
                    for n in range(2):
                        mm = pe.transpose(bank_s[:, kt, n * P:(n + 1) * P], probs[:, n, kt * P:(kt + 1) * P],
                                          ident[:, :])
                mm.then_inc(pt_done, 1)

            def pv(h):
                wait(pe, vs_done, h(1, 1))
                for kt in range(2):
                    mm = pe.matmul(bank_a[:, 0, :], v_stage[:, kt, :], probs_t[:, kt, :], start=kt == 0, stop=kt == 1)
                mm.then_inc(pv_done, 1)

            def statistics(ready, columns, sums=1):
                pe.wait_ge(*ready)
                for s in range(sums):
                    mm = pe.matmul(bank_y[:, s, :], ones[:, :], acc[:, s, :], start=True, stop=True)
                if columns:
                    for tt in range(2):
                        mm = pe.matmul(bank_a[:, 0, tt:tt + 1], acc[:, 0, tt * P:(tt + 1) * P], ones[:, 0:1],
                                       start=True, stop=True)
                mm.then_inc(stat_mm, 1)

            def input_weights_turned():
                pe.wait_ge(tabs_in, 80)
                pe.wait_ge(bbar_done, 1)
                pe.wait_ge(stat_root, 1)
                for q in range(UT):
                    bank = (bank_a, bank_s, bank_b, bank_y)[q // 2]
                    for n in range(2):
                        mm = pe.transpose(bank[:, q % 2, n * P:(n + 1) * P], b_bar[n][:, 4 * q:4 * q + 4, :], ident[:, :])
                mm.then_inc(bt_done, 1)

            x, u = (XH, XL, 0), (UH, UL, 0)
            for b, _ in in_u.stretches(pe, peel=True):
                for j in range(SLOTS):
                    if b() == 0 and j < 4:
                        pe.wait_ge(xl_done, j + 1)
                    if b() == 0 and j == 4:
                        statistics((stat_in, 1), True)
                    if b() == 1 and j == 3:
                        input_weights_turned()
                    units(in_u, b, j, x)
            for b, _ in in_qk.stretches(pe, peel=True):
                for j in range(SLOTS):
                    ssm(j, b, 0)
                    units(in_qk, b, j, x)
            for b, _ in in_v.stretches(pe, peel=False):
                for j in range(SLOTS):
                    ssm(j, b, 2)
                    units(in_v, b, j, x, tokens_out=True)
            pe.wait_ge(ml_done, 4)
            pe.wait_ge(stat_in, 2)
            for b, _ in mem_k.stretches(pe, peel=True):
                for j in range(SLOTS):
                    ssm(j, b, 3)
                    attention(j, b)
                    if b() == 0 and isinstance(b(), int) and j == 1:
                        for tt in range(2):
                            mm = pe.matmul(bank_a[:, 0, tt:tt + 1], acc[:, 1, tt * P:(tt + 1) * P], ones[:, 0:1],
                                           start=True, stop=True)
                        mm = pe.matmul(bank_s[:, 0, :], ones[:, :], acc[:, 1, :], start=True, stop=True)
                        mm.then_inc(stat_mm, 1)
                        pe.wait_ge(stat_root, 2)
                    units(mem_k, b, j, u)
            for b, _ in mem_v.stretches(pe, peel=False):
                for j in range(SLOTS):
                    ssm(j, b, 5)
                    attention(j, b.plus(4))
                    units(mem_v, b, j, u, tokens_out=True)
            q7 = At(None, 0, 7)
            for b, c in out_attn.stretches(pe, peel=True):
                for j in range(SLOTS):
                    if j == 0:
                        ssm_in(q7, c)
                    if c == 0 and j == 0:
                        turned(q7)
                        pe.wait_ge(ol_done, H1 - 1)
                    if c == 0 and j == 1:
                        pv(q7)
                    if c == 0 and j == 3:
                        pe.wait_ge(ol_done, H1)
                    if j == 2:
                        ssm_out(q7, c - 1) if c else ssm_out(q7.before(), 3)
                    units(out_attn, b, j, x)
            ssm_out(q7, 3)
            for b, _ in glu.stretches(pe, peel=True):
                for j in range(SLOTS):
                    if b() == 0 and j in (0, 2, 3):
                        pe.wait_ge(yl_done, (1, 2, 2, 3)[j])
                    units(glu, b, j, (XH, XL, UT))
            for b, _ in out_ssm.stretches(pe, peel=True):
                for j in range(SLOTS):
                    if isinstance(b(), int) and b() == 0 and j in (0, 2):
                        pe.wait_ge(gl_done, j // 2 + 1)
                    units(out_ssm, b, j, u)

            def first_of(b):
                return isinstance(b(), int) and b() == 0

            act_parts = 0
            for n, (up, down) in enumerate(ffn1):
                for b, _ in up.stretches(pe, peel=n == 0):
                    for j in range(SLOTS):
                        if n == 0 and first_of(b):
                            if j < 4:
                                pe.wait_ge(res_lo, 2 * j + 2)
                            if j == 4:
                                statistics((stat_in, 3), False)
                        units(up, b, j, x)
                for b, _ in down.stretches(pe, peel=True):
                    for j in range(SLOTS):
                        if first_of(b) and j < 4:
                            pe.wait_ge(act_lo, act_parts + ((j + 1) * down.kt + 1) // 2)
                        units(down, b, j, u)
                act_parts += up.bodies

            def lru(slot, b, before):
                if slot == 3:
                    c = b.plus(before)
                    for n in range(2):
                        wait(pe, conv_done, c(2, n + 1))
                        wait(pe, lw_in[n], c(16, 16))
                        banks = ((bank_a, bank_s), (bank_b, bank_y))[n]
                        for m in range(4):
                            mm = pe.matmul(banks[m // 2][:, m % 2, :], lru_weights[n][:, m, :], lru_xc[n],
                                           start=True, stop=True)
                        mm.then_inc(lru_mm, 1)

            for b, _ in lru_in.stretches(pe, peel=True):
                for j in range(SLOTS):
                    if first_of(b) and j < 4:
                        pe.wait_ge(res_lo, 8 + 2 * j + 2)
                    if first_of(b) and j == 4:
                        statistics((stat_in, 4), False, sums=2)
                        for s in range(2):
                            for tt in range(2):
                                mm = pe.matmul(bank_a[:, 0, 2 * s + tt:2 * s + tt + 1], acc[:, s, tt * P:(tt + 1) * P],
                                               ones[:, 0:1], start=True, stop=True)
                        mm.then_inc(stat_mm, 1)
                    units(lru_in, b, j, x)
            pe.wait_ge(stat_root, 5)
            for b, _ in lru_gate.stretches(pe, peel=False):
                for j in range(SLOTS):
                    lru(j, b, 0)
                    units(lru_gate, b, j, x)
            for b, _ in in_q2.stretches(pe, peel=False):
                for j in range(SLOTS):
                    lru(j, b, 4)
                    units(in_q2, b, j, x)
            for g in (in_k2, in_v2):
                for b, _ in g.stretches(pe, peel=True):
                    for j in range(SLOTS):
                        units(g, b, j, x, tokens_out=g is in_v2)
            pe.wait_ge(rotate2_in, 16)
            for b, _ in in_qm.stretches(pe, peel=True):
                for j in range(SLOTS):
                    if j == 2:
                        wait(pe, k_roped, b())
                        pe.matmul(bank_a[:, 0, :], rotate[:, :], k2[:, ix(b()), :].rearrange("p a t -> p (a t)"),
                                  start=True, stop=True).then_inc(k_rot, 1)
                    units(in_qm, b, j, x)

            def local(slot, b):
                for n in range(2):
                    h = b.times(2).plus(n)
                    if slot == 4 * n:
                        pe.matmul(bank_a[:, 0, :], rotate[:, :], q_late[:, ix(h()), :].rearrange("p a t -> p (a t)"),
                                  start=True, stop=True).then_inc(rot_done, 1)
                    if slot == 4 * n + 2:
                        wait(pe, rope_done, h(1, H1 + 1))
                        wait(pe, masked, h(1, H1))
                        kv = k2[:, ix(b.halved()()), :].rearrange("p a t -> p (a t)")
                        for t in range(2):
                            mm = pe.matmul(bank_s[:, t, :], q_rot[:, t * P:(t + 1) * P], kv, start=True, stop=True)
                        mm.then_inc(scores_done, 1)
                local_end(slot, b)

            def local_end(slot, b):
                for n in range(2):
                    h = b.times(2).plus(-n)
                    if isinstance(h(), int) and not 0 <= h() < 16:
                        continue
                    if slot == 6 - 4 * n:
                        wait(pe, probs_done, h(1, H1 + 1))
                        wait(pe, pt_copied, h(1, H1))
                        for kt in range(2):
                            for t in range(2):
                                mm = pe.transpose(bank_y[:, kt, t * P:(t + 1) * P], probs2[:, t, kt * P:(kt + 1) * P],
                                                  ident[:, :])
                        mm.then_inc(pt_done, 1)
                    if slot == 7 - 4 * n:
                        wait(pe, pt_copied, h(1, H1 + 1))
                        wait(pe, oh_done, h(1, H1))
                        for kt in range(2):
                            mm = pe.matmul(bank_b[:, 0, :], v2_stage[:, kt, :], probs2_t[:, kt, :], start=kt == 0, stop=kt == 1)
                        mm.then_inc(pv_done, 1)

            def memory(slot, b):
                h, half = b.halved(), b.c % 2
                if slot == 6 and half == 0:
                    wait(pe, qm_staged, h(1, 1))
                    wait(pe, mkv_in, h(64, 64))
                    for t in range(2):
                        for d in range(4):
                            mm = pe.matmul(bank_s[:, t, :], qm_stage[:, d, t * P:(t + 1) * P], mk[:, d, :],
                                           start=d == 0, stop=d == 3)
                    mm.then_inc(scores_done, 1)
                if slot == 3 and half == 1:
                    wait(pe, probs_done, h(1, HEADS + 1))
                    for kt in range(2):
                        for t in range(2):
                            mm = pe.transpose(bank_a[:, kt, t * P:(t + 1) * P], m_probs[:, t, kt * P:(kt + 1) * P],
                                              ident[:, :])
                    mm.then_inc(pt_done, 1)
                if slot == 5 and half == 1:
                    wait(pe, pt_copied, h(1, HEADS + 1))
                    for d in range(4):
                        bank = (bank_b, bank_y)[d // 2]
                        for kt in range(2):
                            mm = pe.matmul(bank[:, d % 2, :], mv[:, 2 * (d // 2) + kt, (d % 2) * P:(d % 2 + 1) * P],
                                           m_probs_t[:, kt, :], start=kt == 0, stop=kt == 1)
                    mm.then_inc(pv_done, 1)

            for n, g in enumerate(branches):
                for b, _ in g.stretches(pe, peel=True):
                    for j in range(SLOTS):
                        if n == 0 and j == 0 and isinstance(b(), int) and b() == 0:
                            pe.wait_ge(k_roped, 4)
                        if n == 0:
                            local(j, b)
                        if n == 1:
                            if isinstance(b(), int) and b() == 0:
                                local_end(j, At(None, 0, 8))
                            memory(j, b)
                        if j >= 4 and isinstance(b(), int) and b() == 0:
                            pe.wait_ge(lru_lo, 4) if n == 0 else pe.wait_ge(op_lo, 4 * (n - 1) + j - 3)
                        units(g, b, j, x if j < 4 else u)
            for b, _ in out2.stretches(pe, peel=True):
                for j in range(SLOTS):
                    if isinstance(b(), int) and b() == 0 and j < 4:
                        pe.wait_ge(op_lo, 8 + j + 1)
                    units(out2, b, j, x)
            statistics((stat_in, 5), False)
            for n, (up, down) in enumerate(ffn2):
                for b, _ in up.stretches(pe, peel=n == 0):
                    for j in range(SLOTS):
                        if n == 0 and first_of(b):
                            if j < 4:
                                pe.wait_ge(pre_lo, j + 1)
                            if j == 6:
                                statistics((stat_in, 6), False)
                        units(up, b, j, x)
                for b, _ in down.stretches(pe, peel=True):
                    for j in range(SLOTS):
                        if first_of(b) and j < 4:
                            pe.wait_ge(up_lo, 8 * n + 2 * j + 2)
                        units(down, b, j, u)
            statistics((stat_in, 7), False)

        def stream(eng, g, split, late, events, tail=None):
            for b, _ in g.stretches(eng, peel=True):
                for j in range(SLOTS):
                    split(g, b, j)
                    if j >= LAG:
                        events(j - LAG, b)
                    elif isinstance(b(), int) and b() == 0:
                        if late:
                            late[0](SLOTS - LAG + j, late[1])
                        if j == LAG - 1 and tail:
                            tail()
                    else:
                        events(SLOTS - LAG + j, b.before())
            return events, At(None, 0, g.bodies - 1)

        @block.scalar
        def _(act):
            links = [0]

            def link(ins):
                links[0] += 1
                ins.then_inc(act_link, 1)
                act.wait_ge(act_link, links[0])

            def upper(g, b, j):
                wait(act, raw_in[j % RING], b(32, 32 * g.first + 16 * (j // RING) + 16))
                wait(act, mm_done, b(SLOTS, SLOTS * g.first + j - RING + 1))
                act.activation(HI[:, j % RING, 0:g.kt * GC], RAW[:, j % RING, 0:g.kt * GC], ACT.Copy)\
                   .then_inc(hi_done, 1)

            def root(n, src, dst, src_col=None, dst_col=None):
                act.wait_ge(stat_mm, n + 1)
                ins = act.activation(dst, src, ACT.Sqrt, scale=1.0 / D, bias=consts[:, 0:1])
                if src_col is not None:
                    ins = act.activation(dst_col, src_col, ACT.Sqrt, scale=1.0 / D, bias=consts[:, 0:1])
                ins.then_inc(stat_root, 1)

            def nothing(slot, b):
                pass

            act.wait_ge(vecs_in, 16)
            for n in range(4):
                act.wait_ge(x_in[n], 16)
                for k in range(4 * n, 4 * n + 4):
                    ins = act.activation(XH[:, k, :], H[:, k, :], ACT.Copy, scale=vec("norm1", k, 1))
                ins.then_inc(xh_done, 1)
            act.dma_start(ident[:, :], A["ident"]).then_inc(tabs_in, 16)
            act.dma_start(rotate[:, :], A["rotate1"]).then_inc(tabs_in, 16)
            act.dma_start(steps[:, :], A["steps"]).then_inc(tabs_in, 16)
            act.dma_start(cos_sin[:, :, :], A["cos_sin"]).then_inc(tabs_in, 16)
            act.dma_start(masks[:, :, :], A["masks1"]).then_inc(tabs_in, 16)
            for n in range(2):
                act.dma_start(b_raw[n], A[("b_re", "b_im")[n]]).then_inc(b_in, 16)
            for n in range(4):
                act.dma_start(mem_raw[n], A["mem"][:, 4 * n:4 * n + 4, :]).then_inc(mem_in[n], 16)

            def in_u_events(slot, b):
                if slot == 0 and b() == 0:
                    act.wait_ge(vecs_in, 16)
                    act.activation(small[:, 0, :], vec("log_dt"), ACT.Exp).then_inc(angle_in, 1)
                if slot == 1 and b() == 0:
                    act.wait_ge(theta_done, 1)
                    act.activation(small[:, 3, :], small[:, 1, :], ACT.Exp)
                    link(act.activation(small[:, 7, :], small[:, 6, :], ACT.Abs))
                    act.activation(small[:, 8, :], small[:, 6, :], ACT.Sin, scale=TWO_PI)
                    act.activation(small[:, 9, :], small[:, 7, :], ACT.Sin, scale=-TWO_PI, bias=consts[:, 1:2])\
                       .then_inc(angle_done, 1)
                if slot == 3 and b() == 1:
                    act.wait_ge(bt_done, 1)
                    for n, bank in enumerate((bank_a, bank_s, bank_b, bank_y)):
                        ins = act.activation(b_flat[:, 512 * n:512 * n + 512], bank[:, :, :], ACT.Copy)
                    ins.then_inc(bt_copied, 1)
                    act.wait_ge(bt_copied, 1)
                    act.dma_start(bt_scratch.rearrange("q p a n -> p q (a n)"),
                                  b_flat.rearrange("p (q n) -> p q n", n=2 * P)).then_inc(bt_out, 16)
                if slot == 3 and b() == 0:
                    root(0, bank_y[:, 0, :], rms[:, 1, :], bank_a[:, 0, 0:2], rms_col[:, 1, :])

            def tables(s, par):
                wait(act, frac_done, s(1, 1))
                act.activation(acyc, kcyc, ACT.Abs).then_inc(abs_done, 1)
                act.activation(sin_t[par], kcyc, ACT.Sin, scale=-TWO_PI)
                wait(act, abs_done, s(1, 1))
                act.activation(cos_t[par], acyc, ACT.Sin, scale=-TWO_PI, bias=consts[:, 1:2]).then_inc(trig_done, 1)

            def input_staged(q):
                wait(act, bu_done, q(4))
                act.activation(u_stage, ZP[:, ix(q()), :].rearrange("p a t -> p (a t)"), ACT.Copy).then_inc(us_done, 1)

            def ssm(slot, b, q0):
                if slot == 5 and b.c % 2:
                    input_staged(b.halved().plus(q0 + 1))
                if slot in (2, 6):
                    tables(b.times(2).plus(4 * q0 + slot // 4 + 1), (slot // 4 + 1) % 2)

            def attention(slot, h):
                first = isinstance(h(), int) and h() == 0
                if slot == 0 and not first:
                    turned(h.before())
                if slot == 1 and not first:
                    upper_out(h.before())
                if slot == 6:
                    wait(act, nmax_done, h(1, 1))
                    for n in range(2):
                        ins = act.activation(probs[:, n, :], rot_tmp[:, n, :], ACT.Exp, scale=SCALE, bias=small[:, 20, n:n + 1])
                    ins.then_inc(exp_done, 1)

            def turned(h):
                wait(act, pt_done, h(1, 1))
                act.activation(probs_t[:, :, :], bank_s[:, :, :], ACT.Copy).then_inc(pt_copied, 1)
                act.activation(v_stage[:, :, :], v_head(h), ACT.Copy).then_inc(vs_done, 1)

            def upper_out(h):
                wait(act, pv_done, h(1, 1))
                act.activation(XH[:, ix(h()), :], bank_a[:, 0:1, :], ACT.Copy).then_inc(oh_done, 1)

            def qk_events(slot, b):
                ssm(slot, b, 0)
                if slot == 7:
                    act.wait_ge(mem_in[b()], 16)
                    for k in range(4 * b(), 4 * b() + 4):
                        ins = act.activation(UH[:, k, :], mem_raw[b()][:, k % 4, :], ACT.Copy, scale=vec("mem", k, 1))
                    ins.then_inc(mh_done, 1)

            def v_events(slot, b):
                ssm(slot, b, 2)

            def mem_out(scratch, g, slot, b):
                p = slot // 4
                wait(act, evac[p], b(1, g.first + 1))
                act.dma_start(scratch[ix(b(2, p))].rearrange("a p k t -> p (a k) t"), mem_stage[p]).then_inc(memkv_out[p], 16)

            def mem_k_events(slot, b):
                attention(slot, b)
                ssm(slot, b, 3)
                if slot in (3, 7):
                    mem_out(memk_scratch, mem_k, slot, b)

            def mem_v_events(slot, b):
                attention(slot, b.plus(4))
                ssm(slot, b, 5)
                if slot in (3, 7):
                    mem_out(memv_scratch, mem_v, slot, b)

            def gelu_part(start, stop):
                act.wait_ge(yt_done, stop)
                link(act.activation(ZP[:, start:stop, :], ZP[:, start:stop, :], ACT.Gelu_apprx_tanh))
                act.activation(XH[:, UT + start:UT + stop, :], ZP[:, start:stop, :], ACT.Copy).then_inc(yh_done, 1)

            def out_attn_events(slot, b):
                if slot == 5 and b() in (1, 2):
                    gelu_part(*((0, 4), (4, 7))[b() - 1])
                if slot == 0 and b() == 0:
                    turned(At(None, 0, 7))
                if slot == 1 and b() == 0:
                    upper_out(At(None, 0, 7))
                if slot == 2 and b() < 3:
                    tables(At(None, 0, 29 + b()), (29 + b()) % 2)

            def qk_tail():
                act.wait_ge(bt_out, 16)
                tables(At(None, 0, 0), 0)
                act.wait_ge(evac[1], in_u.first + in_u.bodies)
                input_staged(At(None, 0, 0))

            def mem_stats():
                root(1, bank_s[:, 0, :], rms[:, 1, :], bank_a[:, 0, 0:2], rms_col[:, 1, :])

            late = stream(act, in_u, upper, None, in_u_events)
            late = stream(act, in_qk, upper, late, qk_events, tail=qk_tail)
            late = stream(act, in_v, upper, late, v_events)
            late = stream(act, mem_k, upper, late, mem_k_events, tail=mem_stats)
            late = stream(act, mem_v, upper, late, mem_v_events)
            late = stream(act, out_attn, upper, late, out_attn_events)

            def gelu_y():
                gelu_part(7, 8)

            def glu_events(slot, b):
                if slot in (3, 7):
                    gidx = 2 * b() + slot // 4
                    act.wait_ge(mm_done, SLOTS * (glu.first + b()) + slot + 1)
                    for n in range(2):
                        ins = act.activation(ZP[:, UT + 2 * gidx + n, :], GP[:, 2 * (slot // 4) + n, 0:T], ACT.Sigmoid,
                                             bias=vec("b_glu", 2 * gidx + n, 1))
                    ins.then_inc(evac[slot // 4], 1)
                if slot == 7:
                    act.wait_ge(gated, b() + 1)
                    act.activation(UH[:, 4 * b():4 * b() + 4, :], ZP[:, UT + 4 * b():UT + 4 * b() + 4, :], ACT.Copy)\
                       .then_inc(gh_done, 1)

            late = stream(act, glu, upper, late, glu_events, tail=gelu_y)

            def out_ssm_events(slot, b):
                if slot in (3, 7):
                    tiles = b(4, 2 * (slot // 4))
                    wait(act, res_g, b(2, slot // 4 + 1))
                    act.activation(XH[:, ix(tiles, 2), :], ZP[:, 0:2, :], ACT.Copy).then_inc(res_hi, 1)

            late = stream(act, out_ssm, upper, late, out_ssm_events)
            act.wait_ge(ol_done, H1)
            act.dma_start(rotate[:, :], A["rotate2"]).then_inc(rotate2_in, 16)
            act.dma_start(pos_raw.bitcast(i32), A["positions"]).then_inc(pos_in, 16)

            def up_events(g, first):
                def f(slot, b):
                    if slot == 3 and first == 0 and isinstance(b(), int) and b() == 0:
                        root(2, bank_y[:, 0, :], rms[:, 1, :])
                    if slot == 7:
                        tiles = b(2)
                        wait(act, evac[0], b(1, g.first + 1))
                        act.activation(ZP[:, 4:6, :], ZP[:, 2:4, :], ACT.Silu).then_inc(silu_done, 1)
                        wait(act, act_gated, b(1, first + 1))
                        act.activation(UH[:, ix(tiles, 2), :], ZP[:, 6:8, :], ACT.Copy).then_inc(act_hi, 1)
                return f

            def last_down_events(slot, b):
                if slot in (3, 7):
                    tiles = b(4, 2 * (slot // 4))
                    wait(act, res_g, b(2, 8 + slot // 4 + 1))
                    act.activation(XH[:, ix(tiles, 2), :], ZP[:, 0:2, :], ACT.Copy).then_inc(res_hi, 1)

            def second_constants():
                act.wait_ge(turn_done, 1)
                link(act.activation(ang_tmp, ang, ACT.Abs))
                act.activation(cos_sin[:, 1, :], ang, ACT.Sin, scale=TWO_PI)
                act.activation(cos_sin[:, 0, :], ang_tmp, ACT.Sin, scale=-TWO_PI, bias=consts[:, 1:2])

            def lru_constants():
                link(act.activation(small[:, 0, :], vec("lam"), ACT.Abs))
                act.activation(small[:, 1, :], small[:, 0, :], ACT.Exp, scale=-1.0).then_inc(lam_exp, 1)

            done = 0
            for n, (up, down) in enumerate(ffn1):
                late = stream(act, up, upper, late, up_events(up, done))
                done += up.bodies
                late = stream(act, down, upper, late, last_down_events if n == 2 else nothing,
                              tail=(second_constants, lru_constants, None)[n])

            def block_roots():
                act.wait_ge(stat_mm, 5)
                act.activation(rms[:, 1, :], bank_y[:, 0, :], ACT.Sqrt, scale=1.0 / D, bias=consts[:, 0:1])
                act.activation(rms_col[:, 1, :], bank_a[:, 0, 0:2], ACT.Sqrt, scale=1.0 / D, bias=consts[:, 0:1])\
                   .then_inc(stat_root, 1)
                act.wait_ge(norm_part, 1)
                act.activation(rms[:, 0, :], rms[:, 0, :], ACT.Sqrt, scale=1.0 / D, bias=consts[:, 0:1])
                act.activation(rms_col[:, 0, :], rms_col[:, 0, :], ACT.Sqrt, scale=1.0 / D, bias=consts[:, 0:1])\
                   .then_inc(stat_root, 1)

            def gelu_gate(b):
                wait(act, evac[0], b(1, lru_gate.first))
                wait(act, evac[1], b(1, lru_gate.first))
                t = gr[:, ix(b(4, -4), 4), :]
                act.activation(t, t, ACT.Gelu_apprx_tanh).then_inc(gr_done, 1)

            def lru(slot, b, before):
                c = b.plus(before)
                if slot == 3:
                    for n in range(2):
                        wait(act, lru_mm, c(2, n + 1))
                        wait(act, scans_done, c(2, n - 1))
                        banks = ((bank_a, bank_s), (bank_b, bank_y))[n]
                        for d in range(2):
                            act.activation(lru_a[n][:, d, :], banks[0][:, d, :], ACT.Sigmoid, bias=vec("br", c(2, 16 * d + n), 1))
                            ins = act.activation(lru_i[n][:, d, :], banks[1][:, d, :], ACT.Sigmoid, bias=vec("bi", c(2, 16 * d + n), 1))
                        ins.then_inc(sig_gates, 1)
                if slot == 4:
                    wait(act, lru_y, c(2))
                    for n in range(2):
                        wait(act, sig_gates, c(2, n + 1))
                        for d in range(2):
                            ins = act.activation(lru_w[n][:, d, :], lru_a[n][:, d, :], ACT.Tanh, scale=small[:, 15, ix(c(2, 16 * d + n))])
                    ins.then_inc(gap_done, 1)
                    wait(act, gap_done, c(1, 1))
                    for n in range(2):
                        for d in range(2):
                            ins = act.activation(lru_a[n][:, d, :], lru_a[n][:, d, :], ACT.Exp, scale=small[:, 16, ix(c(2, 16 * d + n))])
                        ins.then_inc(decays, 1)
                if slot == 7:
                    for n in range(2):
                        wait(act, w_done, c(2, n + 1))
                        act.activation(lru_w[n], lru_w[n], ACT.Sqrt).then_inc(root_done, 1)

            def lru_gate_events(slot, b):
                if slot == 1 and not (isinstance(b(), int) and b() == 0):
                    gelu_gate(b)
                lru(slot, b, 0)

            def q2_events(slot, b):
                if slot == 1 and isinstance(b(), int) and b() == 0:
                    gelu_gate(At(None, 0, 4))
                lru(slot, b, 4)

            def qm_events(slot, b):
                if slot == 5:
                    wait(act, lru_y, 16)
                    t = ix(b(4), 4)
                    act.activation(UH[:, t, :], gr[:, t, :], ACT.Copy).then_inc(lru_hi, 1)

            def lru_in_events(slot, b):
                if slot == 3 and isinstance(b(), int) and b() == 0:
                    block_roots()

            late = stream(act, lru_in, upper, late, lru_in_events)
            late = stream(act, lru_gate, upper, late, lru_gate_events)
            late = stream(act, in_q2, upper, late, q2_events)
            late = stream(act, in_k2, upper, late, nothing)
            late = stream(act, in_v2, upper, late, nothing)
            late = stream(act, in_qm, upper, late, qm_events)

            def local(slot, b):
                for n in range(2):
                    h = b.times(2).plus(-n)
                    if isinstance(h(), int) and not 0 <= h() < 16:
                        continue
                    if slot == 4 - 4 * n:
                        wait(act, nmax_done, h(1, H1 + 1))
                        for t in range(2):
                            act.activation(probs2[:, t, :], scores2[:, t, :], ACT.Exp, scale=SCALE, bias=small[:, 20, t:t + 1],
                                           accum_out=small[:, 19, t:t + 1])
                        act.activation(small[:, 19, 2:4], small[:, 20, 0:2], ACT.Exp, bias=vec("sink", h(), 1)).then_inc(exp_done, 1)
                    if slot == 6 - 4 * n:
                        wait(act, pt_done, h(1, H1 + 1))
                        act.activation(probs2_t[:, :, :], bank_y[:, :, :], ACT.Copy)
                        act.activation(v2_stage[:, :, :], v2_head(b, n), ACT.Copy).then_inc(pt_copied, 1)
                    if slot == 7 - 4 * n:
                        wait(act, pv_done, h(1, H1 + 1))
                        act.activation(q_late[:, ix(h()), :], bank_b[:, 0:1, :], ACT.Copy).then_inc(oh_done, 1)

            def v2_head(b, n):
                kv = b.halved() if n == 0 or b.c % 2 else b.plus(-2).halved()
                return v2[:, :, ix(kv(HD), HD)]

            def gates(g, n, slot, b):
                if slot == 3:
                    wait(act, gate_biased, b(1, 8 * n + 1))
                    act.activation(gate_space, gate_space, ACT.Sigmoid).then_inc(gate_sig, 1)

            def memory(slot, b):
                h, half = b.halved(), b.c % 2
                if slot == 4 and half == 0:
                    wait(act, scores_done, h(1, HEADS))
                    act.activation(qm_stage[:, :, :], qm[:, ix(h(4), 4), :], ACT.Copy).then_inc(qm_staged, 1)
                if slot == 0 and half == 1:
                    wait(act, nmax_done, h(1, HEADS + 1))
                    for t in range(2):
                        ins = act.activation(m_probs[:, t, :], m_probs[:, t, :], ACT.Exp, scale=M_SCALE, bias=small[:, 20, t:t + 1],
                                             accum_out=small[:, 19, t:t + 1])
                    ins.then_inc(exp_done, 1)
                if slot == 3 and half == 1:
                    wait(act, pt_done, h(1, HEADS + 1))
                    act.activation(m_probs_t[:, :, :], bank_a[:, :, :], ACT.Copy).then_inc(pt_copied, 1)
                if slot == 5 and half == 1:
                    wait(act, pv_done, h(1, HEADS + 1))
                    act.activation(qm[:, ix(h(4, 2), 2), :], bank_y[:, :, :], ACT.Copy)
                    act.activation(qm[:, ix(h(4), 2), :], bank_b[:, :, :], ACT.Copy).then_inc(oh_done, 1)

            def upper_chunk(src, hi, c):
                act.activation(hi[:, 4 * c:4 * c + 4, :], src[:, 4 * c:4 * c + 4, :], ACT.Copy).then_inc(op_hi, 1)

            def operand(n, src, hi):
                def f():
                    if n == 0:
                        act.wait_ge(oh_done, H1 + 15)
                    if n == 1:
                        act.wait_ge(oh_done, HEADS + 4)
                    if n == 2:
                        act.wait_ge(merged_done, 16)
                    act.wait_ge(mm_done, SLOTS * (branches[n].first + 8))
                    for c in range(3 if n == 0 else 4):
                        upper_chunk(src, hi, c)
                return f

            def branch_events(n):
                def f(slot, b):
                    if n == 0:
                        local(slot, b)
                    if n == 1:
                        if isinstance(b(), int) and b() == 0:
                            local(slot, At(None, 0, 8))
                            if slot == 3:
                                act.wait_ge(oh_done, HEADS)
                                upper_chunk(q_late, UH, 3)
                        memory(slot, b)
                    gates(branches[n], n, slot, b)
                return f

            late = stream(act, branches[0], upper, late, branch_events(0))
            late = stream(act, branches[1], upper, late, branch_events(1), tail=operand(0, q_late, UH))
            late = stream(act, branches[2], upper, late, branch_events(2), tail=operand(1, qm, UH))
            late = stream(act, out2, upper, late, nothing, tail=operand(2, merged, XH))

            def mixed():
                root(5, bank_y[:, 0, :], rms[:, 1, :])
                for k in range(KT):
                    if k % 4 == 0:
                        act.wait_ge(post_added, k // 4 + 1)
                    ins = act.activation(XH[:, k, :], H[:, k, :], ACT.Copy, scale=vec("mlp_pre", k, 1))
                    if k % 4 == 3:
                        ins.then_inc(pre_hi, 1)

            def up2_events(first):
                def f(slot, b):
                    if slot in (3, 7):
                        if slot == 3 and first == 0 and isinstance(b(), int) and b() == 0:
                            root(6, bank_y[:, 0, :], rms[:, 1, :])
                        wait(act, up_sq, b(2, first + slot // 4 + 1))
                        act.activation(UH[:, ix(b(4, 2 * (slot // 4)), 2), :], up_space, ACT.Copy).then_inc(up_hi, 1)
                return f

            for n, (up, down) in enumerate(ffn2):
                late = stream(act, up, upper, late, up2_events(8 * n), tail=mixed if n == 0 else None)
                late = stream(act, down, upper, late, nothing)
            root(7, bank_y[:, 0, :], rms[:, 1, :])

        @block.vector
        def _(dve):
            links = [0]

            def link(ins):
                links[0] += 1
                ins.then_inc(dve_link, 1)
                dve.wait_ge(dve_link, links[0])

            def lower(g, b, j):
                wait(dve, hi_done, b(SLOTS, SLOTS * g.first + j + 1))
                cols = slice(0, g.kt * GC)
                dve.tensor_tensor(LO[:, j % RING, cols], RAW[:, j % RING, cols], HI[:, j % RING, cols].bitcast(f32),
                                  ALU.subtract).then_inc(lo_done, 1)

            def taken(g, b, slot):
                wait(dve, mm_done, b(SLOTS, SLOTS * g.first + slot + 1))
                return GP[:, 2 * (slot // 4):2 * (slot // 4) + 2, 0:T]

            def row(v):
                return v.unsqueeze(1).to_broadcast([P, 2, T])

            def col(v, n=T):
                return v.unsqueeze(2).to_broadcast([P, v.shape[1], n])

            dve.memset(consts[:, 0:1], EPS)
            link(dve.memset(consts[:, 1:2], math.pi / 2))
            dve.wait_ge(vecs_in, 16)
            for n in range(4):
                dve.wait_ge(x_in[n], 16)
                dve.wait_ge(xh_done, n + 1)
                for k in range(4 * n, 4 * n + 4):
                    ins = dve.scalar_tensor_tensor(XL[:, k, :], H[:, k, :], vec("norm1", k, 1), XH[:, k, :].bitcast(f32),
                                                   ALU.mult, ALU.subtract)
                ins.then_inc(xl_done, 1)

            def reduced(dst, src, tmp):
                link(dve.tensor_scalar(tmp, src, 1.0 / (2 * math.pi), MAGIC, ALU.mult, ALU.add))
                link(dve.tensor_scalar(tmp, tmp, -MAGIC, None, ALU.add))
                for part in (-6.28125, -0.0019350051879882812, -3.019916e-07):
                    link(dve.scalar_tensor_tensor(src, tmp, part, src, ALU.mult, ALU.add))
                link(dve.tensor_scalar(dst, src, 1.0 / (2 * math.pi), None, ALU.mult))
                return dve.tensor_scalar(dst, dst, 0.5, -0.5, ALU.min, ALU.max)

            def s_(n):
                return small[:, n, :]

            def tt(o, a, b, op):
                link(dve.tensor_tensor(o, a, b, op))

            def ssm_params():
                dve.wait_ge(angle_in, 1)
                tt(s_(1), vec("a_re"), s_(0), ALU.mult)
                tt(s_(2), vec("a_im"), s_(0), ALU.mult)
                reduced(s_(6), s_(2), s_(4)).then_inc(theta_done, 1)
                tt(s_(4), vec("a_re"), vec("a_re"), ALU.mult)
                tt(s_(5), vec("a_im"), vec("a_im"), ALU.mult)
                tt(s_(4), s_(4), s_(5), ALU.add)
                link(dve.reciprocal(s_(12), s_(4)))

            def ssm_input():
                dve.wait_ge(angle_done, 1)
                tt(s_(11), s_(3), s_(8), ALU.mult)
                tt(s_(10), s_(3), s_(9), ALU.mult)
                link(dve.tensor_scalar(s_(10), s_(10), -1.0, None, ALU.add))
                tt(s_(4), s_(10), vec("a_re"), ALU.mult)
                tt(s_(5), s_(11), vec("a_im"), ALU.mult)
                tt(s_(4), s_(4), s_(5), ALU.add)
                tt(s_(13), s_(4), s_(12), ALU.mult)
                tt(s_(4), s_(11), vec("a_re"), ALU.mult)
                tt(s_(5), s_(10), vec("a_im"), ALU.mult)
                tt(s_(4), s_(4), s_(5), ALU.subtract)
                tt(s_(14), s_(4), s_(12), ALU.mult)

            def ssm_input_weights():
                dve.wait_ge(b_in, 32)
                re, im = col(s_(13), 32), col(s_(14), 32)
                tt(b_bar[0], b_raw[0], re, ALU.mult)
                tt(b_bar[1], b_raw[1], im, ALU.mult)
                tt(b_bar[0], b_bar[0], b_bar[1], ALU.subtract)
                tt(b_bar[1], b_raw[1], re, ALU.mult)
                tt(b_raw[0], b_raw[0], im, ALU.mult)
                dve.tensor_tensor(b_bar[1], b_bar[1], b_raw[0], ALU.add).then_inc(bbar_done, 1)

            def scaled_out(g, b, slot, dst):
                o = taken(g, b, slot)
                dve.tensor_tensor(dst, o, row(rms[:, 0, :]), ALU.mult).then_inc(evac[slot // 4], 1)

            def in_u_events(slot, b):
                if slot == 0 and b() == 0:
                    ssm_params()
                if slot == 4 and b() == 0:
                    ssm_input()
                if slot == 5 and b() == 0:
                    ssm_input_weights()
                if slot in (3, 7):
                    if slot == 3 and b() == 0:
                        dve.wait_ge(stat_root, 1)
                        link(dve.reciprocal(rms[:, 0, :], rms[:, 1, :]))
                        link(dve.reciprocal(rms_col[:, 0, :], rms_col[:, 1, :]))
                    tile0 = 4 * b() + 2 * (slot // 4)
                    scaled_out(in_u, b, slot, ZP[:, tile0:tile0 + 2, :])

            def fractions(s):
                wait(dve, cyc_done, s(1, 1))
                dve.scalar_tensor_tensor(kcyc, kcyc, MAGIC, fcyc, ALU.subtract, ALU.subtract).then_inc(frac_done, 1)

            def rotate_in(s, par):
                wait(dve, bu_done, s(1, 1))
                wait(dve, trig_done, s(1, 1))
                wait(dve, h_done, s())
                dve.tensor_tensor(prod_c, bank_b[:, :, :], row(cos_t[par]), ALU.mult)
                dve.tensor_tensor(prod_s, bank_b[:, :, :], row(sin_t[par]), ALU.mult).then_inc(pq_done, 1)

            def scan_and_rotate_out(s, par):
                wait(dve, gin_done, s(1, 1))
                decay = small[:, 3, ix(s())].to_broadcast([P, T])
                for n in range(2):
                    ins = dve.tensor_tensor_scan(state_g[:, n, :], decay, state_g[:, n, :], 0.0, ALU.mult, ALU.add)
                ins.then_inc(scan_done, 1)
                wait(dve, scan_done, s(1, 1))
                dve.tensor_tensor(prod_c, state_g, row(cos_t[par]), ALU.mult)
                dve.tensor_tensor(prod_s, state_g, row(sin_t[par]), ALU.mult).then_inc(pq2_done, 1)

            def skip_added(q):
                wait(dve, y_done, q(4, 4))
                tile = ZP[:, ix(q()), :].rearrange("p a t -> p (a t)")
                dve.scalar_tensor_tensor(tile, tile, vec("d_skip", q(), 1), bank_y[:, 0, :], ALU.mult, ALU.add)\
                   .then_inc(yt_done, 1)

            def ssm(slot, b, q0):
                s = b.times(2).plus(4 * q0)
                if slot in (0, 4):
                    rotate_in(s.plus(slot // 4), slot // 4)
                if slot in (2, 6):
                    scan_and_rotate_out(s.plus(slot // 4), slot // 4)
                if slot in (1, 5):
                    fractions(s.plus(slot // 4 + 1))
                if slot == 3 and b.c % 2 == 0:
                    q = b.halved().plus(q0 - 1)
                    if not (isinstance(q(), int) and q() < 0):
                        skip_added(q)

            def attention(slot, h):
                if slot == 1 and not (isinstance(h(), int) and h() == 0):
                    lower_out(h.before())
                if slot == 2:
                    wait(dve, rot_done, h(1, 1))
                    dve.tensor_tensor(qk_rot, heads(h, 1, 2), row(cos_sin[:, 0, :]), ALU.mult)
                    dve.tensor_tensor(rot_tmp, bank_a[:, :, :], row(cos_sin[:, 1, :]), ALU.mult).then_inc(qk_sin, 1)
                    wait(dve, qk_sin, h(1, 1))
                    dve.tensor_tensor(qk_rot, qk_rot, rot_tmp, ALU.add).then_inc(rope_done, 1)
                if slot == 4:
                    wait(dve, scores_done, h(1, 1))
                    dve.tensor_tensor(rot_tmp, bank_s[:, :, :], masks[:, 0, :].rearrange("p (a t) -> p a t", a=2), ALU.add)\
                       .then_inc(masked, 1)
                    wait(dve, masked, h(1, 1))
                    dve.tensor_reduce(small[:, 21, 0:2], rot_tmp, AX.X, ALU.max).then_inc(max_done, 1)
                    wait(dve, max_done, h(1, 1))
                    dve.tensor_scalar(small[:, 20, 0:2], small[:, 21, 0:2], -SCALE, None, ALU.mult).then_inc(nmax_done, 1)
                if slot == 6:
                    wait(dve, exp_done, h(1, 1))
                    dve.tensor_tensor(probs, probs, masks[:, 1, :].rearrange("p (a t) -> p a t", a=2), ALU.mult).then_inc(counted, 1)
                    wait(dve, counted, h(1, 1))
                    dve.tensor_reduce(small[:, 19, 0:2], probs, AX.X, ALU.add).then_inc(den_done, 1)
                    wait(dve, den_done, h(1, 1))
                    dve.reciprocal(small[:, 18, 0:2], small[:, 19, 0:2]).then_inc(rden_done, 1)
                    wait(dve, rden_done, h(1, 1))
                    dve.tensor_tensor(probs, probs, col(small[:, 18, 0:2]), ALU.mult).then_inc(probs_done, 1)

            def lower_out(h):
                wait(dve, oh_done, h(1, 1))
                dve.tensor_tensor(XL[:, ix(h()), :], bank_a[:, 0:1, :], XH[:, ix(h()), :].bitcast(f32), ALU.subtract)\
                   .then_inc(ol_done, 1)

            def qk_events(slot, b):
                ssm(slot, b, 0)
                if slot == 7:
                    dve.wait_ge(mh_done, b() + 1)
                    for k in range(4 * b(), 4 * b() + 4):
                        ins = dve.scalar_tensor_tensor(UL[:, k, :], mem_raw[b()][:, k % 4, :], vec("mem", k, 1),
                                                       UH[:, k, :].bitcast(f32), ALU.mult, ALU.subtract)
                    ins.then_inc(ml_done, 1)
                if slot in (3, 7):
                    scaled_out(in_qk, b, slot, ZP[:, ix(b(4, 8 + 2 * (slot // 4)), 2), :])

            def v_events(slot, b):
                ssm(slot, b, 2)
                if slot in (3, 7):
                    o = taken(in_v, b, slot)
                    dve.tensor_tensor(values[:, :, ix(b(2 * GC, GC * (slot // 4)), GC)], o, col(rms_col[:, 0, :]), ALU.mult)\
                       .then_inc(evac[slot // 4], 1)

            def mem_out(g, slot, b, factor):
                p = slot // 4
                o = taken(g, b, slot)
                wait(dve, memkv_out[p], b(16, 16 * (g.first - mem_k.first)))
                dve.tensor_tensor(mem_stage[p], o, factor, ALU.mult).then_inc(evac[p], 1)

            def mem_k_events(slot, b):
                ssm(slot, b, 3)
                attention(slot, b)
                if slot in (3, 7):
                    mem_out(mem_k, slot, b, row(rms[:, 0, :]))

            def mem_v_events(slot, b):
                ssm(slot, b, 5)
                attention(slot, b.plus(4))
                if slot in (3, 7):
                    mem_out(mem_v, slot, b, col(rms_col[:, 0, :]))

            def lower_part(n, start, stop):
                dve.wait_ge(yh_done, n)
                dve.tensor_tensor(XL[:, UT + start:UT + stop, :], ZP[:, start:stop, :], XH[:, UT + start:UT + stop, :].bitcast(f32),
                                  ALU.subtract).then_inc(yl_done, 1)

            def out_attn_events(slot, b):
                s = At(None, 0, 28 + b())
                if slot == 5 and b() in (1, 2):
                    lower_part(b(), *((0, 4), (4, 7))[b() - 1])
                if slot == 0:
                    rotate_in(s, b() % 2)
                if slot == 3 and b() == 0:
                    skip_added(At(None, 0, 6))
                if slot == 1:
                    if b() == 0:
                        lower_out(At(None, 0, 7))
                    if b() < 3:
                        fractions(s.plus(1))
                if slot == 2:
                    scan_and_rotate_out(s, b() % 2)
                if slot in (3, 7):
                    o = taken(out_attn, b, slot)
                    tiles = slice(4 * b() + 2 * (slot // 4), 4 * b() + 2 * (slot // 4) + 2)
                    dve.tensor_tensor(H[:, tiles, :], H[:, tiles, :], o, ALU.add).then_inc(evac[slot // 4], 1)

            def qk_tail():
                fractions(At(None, 0, 0))

            def mem_stats():
                dve.wait_ge(stat_root, 2)
                link(dve.reciprocal(rms[:, 0, :], rms[:, 1, :]))
                link(dve.reciprocal(rms_col[:, 0, :], rms_col[:, 1, :]))

            def y_lower():
                skip_added(At(None, 0, 7))
                lower_part(3, 7, 8)

            def glu_events(slot, b):
                if slot == 7:
                    dve.wait_ge(evac[1], glu.first + b() + 1)
                    t, y = slice(UT + 4 * b(), UT + 4 * b() + 4), slice(4 * b(), 4 * b() + 4)
                    dve.tensor_tensor(ZP[:, t, :], ZP[:, t, :], ZP[:, y, :], ALU.mult).then_inc(gated, 1)
                    dve.wait_ge(gh_done, b() + 1)
                    dve.tensor_tensor(UL[:, y, :], ZP[:, t, :], UH[:, y, :].bitcast(f32), ALU.subtract).then_inc(gl_done, 1)

            def residual(g, b, slot, gain, before):
                p = slot // 4
                o = taken(g, b, slot)
                tiles = ix(b(4, 2 * p), 2)
                wait(dve, res_lo, b(2, before + p))
                if before:
                    wait(dve, res_sq, b(2, p))
                    dve.tensor_tensor(block_sum[p], H[:, tiles, :], o, ALU.add).then_inc(evac[p], 1)
                    wait(dve, evac[p], b(1, g.first + 1))
                    dve.tensor_tensor(H[:, tiles, :], block_sum[p], col(vec("final", b(4, 2 * p), 2)), ALU.mult).then_inc(res_done, 1)
                    wait(dve, res_done, b(2, p + 1))
                else:
                    dve.tensor_tensor(H[:, tiles, :], H[:, tiles, :], o, ALU.add).then_inc(evac[p], 1)
                    wait(dve, evac[p], b(1, g.first + 1))
                dve.tensor_tensor(ZP[:, 0:2, :], H[:, tiles, :], col(vec(gain, b(4, 2 * p), 2)), ALU.mult).then_inc(res_g, 1)
                wait(dve, res_hi, b(2, before + p + 1))
                dve.tensor_tensor(XL[:, tiles, :], ZP[:, 0:2, :], XH[:, tiles, :].bitcast(f32), ALU.subtract).then_inc(res_lo, 1)

            def out_ssm_events(slot, b):
                if slot in (3, 7):
                    residual(out_ssm, b, slot, "norm2", 0)

            def up_events(g, first):
                def f(slot, b):
                    if slot == 3:
                        if first == 0 and isinstance(b(), int) and b() == 0:
                            dve.wait_ge(stat_root, 3)
                            link(dve.reciprocal(rms[:, 0, :], rms[:, 1, :]))
                        o = taken(g, b, 3)
                        dve.tensor_tensor(ZP[:, 2:4, :], o, row(rms[:, 0, :]), ALU.mult).then_inc(evac[0], 1)
                    if slot == 7:
                        o = taken(g, b, 7)
                        dve.tensor_tensor(ZP[:, 6:8, :], o, row(rms[:, 0, :]), ALU.mult).then_inc(evac[1], 1)
                        wait(dve, silu_done, b(1, first + 1))
                        wait(dve, evac[1], b(1, g.first + 1))
                        dve.tensor_tensor(ZP[:, 6:8, :], ZP[:, 6:8, :], ZP[:, 4:6, :], ALU.mult).then_inc(act_gated, 1)
                        wait(dve, act_hi, b(1, first + 1))
                        dve.tensor_tensor(UL[:, ix(b(2), 2), :], ZP[:, 6:8, :], UH[:, ix(b(2), 2), :].bitcast(f32),
                                          ALU.subtract).then_inc(act_lo, 1)
                return f

            def down_events(g):
                def f(slot, b):
                    if slot in (3, 7):
                        o = taken(g, b, slot)
                        tiles = ix(b(4, 2 * (slot // 4)), 2)
                        dve.tensor_tensor(H[:, tiles, :], H[:, tiles, :], o, ALU.add).then_inc(evac[slot // 4], 1)
                return f

            def last_down_events(slot, b):
                if slot in (3, 7):
                    residual(ffn1[2][1], b, slot, "mix_pre", 8)

            late = stream(dve, in_u, lower, None, in_u_events)
            late = stream(dve, in_qk, lower, late, qk_events, tail=qk_tail)
            late = stream(dve, in_v, lower, late, v_events)
            late = stream(dve, mem_k, lower, late, mem_k_events, tail=mem_stats)
            late = stream(dve, mem_v, lower, late, mem_v_events)
            late = stream(dve, out_attn, lower, late, out_attn_events)
            late = stream(dve, glu, lower, late, glu_events, tail=y_lower)
            late = stream(dve, out_ssm, lower, late, out_ssm_events)
            def second_constants():
                dve.wait_ge(pos_in, 16)
                link(dve.tensor_copy(ang, pos_raw.bitcast(i32)))
                link(dve.tensor_scalar(ang, ang, vec("freq"), None, ALU.mult))
                link(reduced(ang, ang, ang_tmp))
                dve.wait_ge(ol_done, H1)
                dve.tensor_copy(small[:, 14, 0:1], small[:, 14, 1:2]).then_inc(turn_done, 1)

            def lru_constants():
                dve.wait_ge(lam_exp, 1)
                link(dve.tensor_scalar(s_(2), s_(1), 2.0, None, ALU.add))
                link(dve.reciprocal(s_(2), s_(2)))
                tt(s_(2), s_(2), s_(1), ALU.mult)
                tt(s_(3), s_(2), s_(2), ALU.mult)
                link(dve.tensor_scalar(s_(4), s_(3), 1.0 / 19, 1.0 / 17, ALU.mult, ALU.add))
                for k in range(15, 0, -2):
                    tt(s_(4), s_(4), s_(3), ALU.mult)
                    link(dve.tensor_scalar(s_(4), s_(4), 1.0 / k, None, ALU.add))
                tt(s_(4), s_(4), s_(2), ALU.mult)
                link(dve.tensor_scalar(s_(5), vec("lam"), -1.0, 0.0, ALU.mult, ALU.max))
                link(dve.scalar_tensor_tensor(s_(5), s_(4), 2.0, s_(5), ALU.mult, ALU.add))
                dve.tensor_scalar(s_(15), s_(5), 8.0, None, ALU.mult)
                dve.tensor_scalar(s_(16), s_(5), -8.0, None, ALU.mult).then_inc(lru_consts, 1)

            done = 0
            for n, (up, down) in enumerate(ffn1):
                late = stream(dve, up, lower, late, up_events(up, done))
                done += up.bodies
                late = stream(dve, down, lower, late, last_down_events if n == 2 else down_events(down),
                              tail=(second_constants, lru_constants, None)[n])

            def block_norms():
                dve.wait_ge(stat_root, 4)
                link(dve.reciprocal(rms[:, 1, :], rms[:, 1, :]))
                link(dve.reciprocal(rms_col[:, 1, :], rms_col[:, 1, :]))
                tt(rms[:, 0, :], rms[:, 1, :], rms[:, 1, :], ALU.mult)
                tt(rms_col[:, 0, :], rms_col[:, 1, :], rms_col[:, 1, :], ALU.mult)
                dve.tensor_tensor(rms[:, 0, :], rms[:, 0, :], bank_y[:, 1, :], ALU.mult)
                dve.tensor_tensor(rms_col[:, 0, :], rms_col[:, 0, :], bank_a[:, 0, 2:4], ALU.mult).then_inc(norm_part, 1)
                dve.wait_ge(stat_root, 5)
                link(dve.reciprocal(rms[:, 0, :], rms[:, 0, :]))
                link(dve.reciprocal(rms_col[:, 0, :], rms_col[:, 0, :]))
                tt(rms[:, 0, :], rms[:, 0, :], rms[:, 1, :], ALU.mult)
                tt(rms_col[:, 0, :], rms_col[:, 0, :], rms_col[:, 1, :], ALU.mult)

            def lru_in_events(slot, b):
                if slot == 3 and isinstance(b(), int) and b() == 0:
                    block_norms()
                if slot in (3, 7):
                    p = slot // 4
                    tiles = ix(b(4, 2 * p), 2)
                    scaled_out(lru_in, b, slot, xr[:, tiles, :])
                    dve.tensor_tensor(H[:, tiles, :], H[:, tiles, :], row(rms[:, 1, :]), ALU.mult)

            def lru(slot, b, before):
                c = b.plus(before)
                if slot == 0:
                    for n in range(2):
                        src = xr[:, ix(c(2, n)), :].rearrange("p a t -> p (a t)")

                        def tap(k):
                            return vec("conv_w", c(2, 16 * k + n), 1)
                        v = lru_xc[n]
                        wait(dve, gated_in, c(2, n - 1))
                        dve.tensor_scalar(v, src, tap(1), vec("conv_b", c(2, n), 1), ALU.mult, ALU.add).then_inc(conv_step, 1)
                        wait(dve, conv_step, c(6, 3 * n + 1))
                        dve.scalar_tensor_tensor(v[:, 1:T], src[:, 0:T - 1], tap(0), v[:, 1:T], ALU.mult, ALU.add).then_inc(conv_step, 1)
                        wait(dve, conv_step, c(6, 3 * n + 2))
                        dve.scalar_tensor_tensor(v[:, 0:T - 1], src[:, 1:T], tap(2), v[:, 0:T - 1], ALU.mult, ALU.add).then_inc(conv_step, 1)
                        wait(dve, conv_step, c(6, 3 * n + 3))
                        dve.scalar_tensor_tensor(v[:, 0:T - 2], src[:, 2:T], tap(3), v[:, 0:T - 2], ALU.mult, ALU.add).then_inc(conv_done, 1)
                    if not (isinstance(c(), int) and c() == 0):
                        scans(c.before())
                if slot == 6:
                    for n in range(2):
                        wait(dve, a_squared, c(2, n + 1))
                        dve.scalar_tensor_tensor(lru_w[n], lru_tmp[n], 1.0, lru_w[n], ALU.add, ALU.mult).then_inc(w_done, 1)

            def scans(c):
                for n in range(2):
                    wait(dve, root_done, c(2, n + 1))
                    dve.tensor_tensor(lru_i[n], lru_w[n], lru_i[n], ALU.mult).then_inc(u_done, 1)
                for n in range(2):
                    wait(dve, u_done, c(2, n + 1))
                    dve.tensor_tensor_scan(lru_w[n][:, 0, :], lru_a[n][:, 0, :], lru_i[n][:, 0, :], 0.0, ALU.mult, ALU.add)
                    dve.tensor_tensor_scan(lru_w[n][:, 1, ::-1], lru_a[n][:, 1, ::-1], lru_i[n][:, 1, ::-1], 0.0, ALU.mult, ALU.add)\
                       .then_inc(scans_done, 1)

            def lru_gate_events(slot, b):
                lru(slot, b, 0)
                if slot in (3, 7):
                    scaled_out(lru_gate, b, slot, gr[:, ix(b(4, 2 * (slot // 4)), 2), :])

            def q2_events(slot, b):
                lru(slot, b, 4)
                if slot in (3, 7):
                    scaled_out(in_q2, b, slot, q_late[:, ix(b(4, 2 * (slot // 4)), 2), :])

            def k2_events(slot, b):
                if slot == 0:
                    scans(At(None, 0, 7))
                if slot == 3:
                    dve.wait_ge(lru_y, 16)
                if slot in (3, 7):
                    scaled_out(in_k2, b, slot, k2[:, 2 * (slot // 4):2 * (slot // 4) + 2, :])

            def v2_events(slot, b):
                if slot in (3, 7):
                    o, p = taken(in_v2, b, slot), slot // 4
                    dve.tensor_tensor(v2[:, :, GC * p:GC * p + GC], o, col(rms_col[:, 0, :]), ALU.mult).then_inc(evac[p], 1)

            def qm_events(slot, b):
                if slot == 5:
                    wait(dve, lru_hi, b(1, 1))
                    t = ix(b(4), 4)
                    dve.tensor_tensor(UL[:, t, :], gr[:, t, :], UH[:, t, :].bitcast(f32), ALU.subtract).then_inc(lru_lo, 1)
                if slot == 2:
                    wait(dve, k_rot, b(1, 1))
                    k = k2[:, ix(b()), :].rearrange("p a t -> p (a t)")
                    dve.tensor_tensor(k, k, cos_sin[:, 0, :], ALU.mult)
                    dve.tensor_tensor(scores2[:, 0, :], bank_a[:, 0, :], cos_sin[:, 1, :], ALU.mult).then_inc(k_cos, 1)
                    wait(dve, k_cos, b(1, 1))
                    dve.tensor_tensor(k, k, scores2[:, 0, :], ALU.add).then_inc(k_roped, 1)
                if slot in (3, 7):
                    scaled_out(in_qm, b, slot, qm[:, ix(b(4, 2 * (slot // 4)), 2), :])

            def local(slot, b):
                for n in range(2):
                    h = b.times(2).plus(n)
                    if slot == 4 * n:
                        wait(dve, rot_done, h(1, H1 + 1))
                        dve.tensor_tensor(q_rot, q_late[:, ix(h()), :].rearrange("p a t -> p (a t)"), cos_sin[:, 0, :], ALU.mult)
                        dve.tensor_tensor(acc[:, 0, :], bank_a[:, 0, :], cos_sin[:, 1, :], ALU.mult).then_inc(qk_sin, 1)
                        wait(dve, qk_sin, h(1, H1 + 1))
                        dve.tensor_tensor(q_rot, q_rot, acc[:, 0, :], ALU.add).then_inc(rope_done, 1)
                    if slot == 4 * n + 2:
                        wait(dve, scores_done, h(1, H1 + 1))
                        dve.tensor_tensor(scores2, bank_s[:, :, :], masks[:, 0, :].rearrange("p (a t) -> p a t", a=2), ALU.add)\
                           .then_inc(masked, 1)
                        wait(dve, masked, h(1, H1 + 1))
                        dve.tensor_reduce(small[:, 21, 0:2], scores2, AX.X, ALU.max).then_inc(max_done, 1)
                        wait(dve, max_done, h(1, H1 + 1))
                        dve.scalar_tensor_tensor(small[:, 18, 0:2], small[:, 21, 0:2], SCALE, vec("sink", h(), 1).to_broadcast([P, 2]),
                                                 ALU.mult, ALU.max).then_inc(counted, 1)
                        wait(dve, counted, h(1, H1 + 1))
                        dve.tensor_scalar(small[:, 20, 0:2], small[:, 18, 0:2], -1.0, None, ALU.mult).then_inc(nmax_done, 1)
                local_end(slot, b)

            def local_end(slot, b):
                for n in range(2):
                    h = b.times(2).plus(-n)
                    if isinstance(h(), int) and not 0 <= h() < 16:
                        continue
                    if slot == 4 - 4 * n:
                        wait(dve, exp_done, h(1, H1 + 1))
                        dve.tensor_tensor(small[:, 17, 0:2], small[:, 19, 0:2], small[:, 19, 2:4], ALU.add).then_inc(den_done, 1)
                        wait(dve, den_done, h(1, H1 + 1))
                        dve.reciprocal(small[:, 17, 2:4], small[:, 17, 0:2]).then_inc(rden_done, 1)
                        wait(dve, rden_done, h(1, H1 + 1))
                        dve.tensor_tensor(probs2, probs2, col(small[:, 17, 2:4]), ALU.mult).then_inc(probs_done, 1)

            def memory(slot, b):
                h, half = b.halved(), b.c % 2
                if slot == 6 and half == 0:
                    wait(dve, scores_done, h(1, HEADS + 1))
                    dve.tensor_reduce(small[:, 21, 0:2], bank_s[:, :, :], AX.X, ALU.max).then_inc(max_done, 1)
                    dve.tensor_copy(m_probs, bank_s[:, :, :])
                    wait(dve, max_done, h(1, HEADS + 1))
                    dve.tensor_scalar(small[:, 20, 0:2], small[:, 21, 0:2], -M_SCALE, None, ALU.mult).then_inc(nmax_done, 1)
                if slot == 1 and half == 1:
                    wait(dve, exp_done, h(1, HEADS + 1))
                    dve.reciprocal(small[:, 17, 2:4], small[:, 19, 0:2]).then_inc(rden_done, 1)
                    wait(dve, rden_done, h(1, HEADS + 1))
                    dve.tensor_tensor(m_probs, m_probs, col(small[:, 17, 2:4]), ALU.mult).then_inc(probs_done, 1)

            def gates(g, n, slot, b):
                if slot == 3:
                    o = taken(g, b, 3)
                    dve.tensor_tensor(gate_space, o, row(rms[:, 0, :]), ALU.mult).then_inc(evac[0], 1)
                    wait(dve, evac[0], b(1, g.first + 1))
                    dve.tensor_tensor(gate_space, gate_space, col(vec("b_gate", b(2, 16 * n), 2)), ALU.add).then_inc(gate_biased, 1)
                if slot == 7:
                    o = taken(g, b, 7)
                    wait(dve, gate_sig, b(1, 8 * n + 1))
                    m = merged[:, ix(b(2), 2), :]
                    if n == 0:
                        dve.tensor_tensor(m, gate_space, o, ALU.mult).then_inc(evac[1], 1)
                        return
                    dve.tensor_tensor(gate_space, gate_space, o, ALU.mult).then_inc(evac[1], 1)
                    wait(dve, evac[1], b(1, g.first + 1))
                    ins = dve.tensor_tensor(m, m, gate_space, ALU.add)
                    ins.then_inc(merged_done, 1)

            def branch_events(n):
                def f(slot, b):
                    if n == 0:
                        local(slot, b)
                    if n == 1:
                        if isinstance(b(), int) and b() == 0:
                            local_end(slot, At(None, 0, 8))
                            if slot == 3:
                                lower_chunk(0, q_late, UH, UL, 3)
                        memory(slot, b)
                    gates(branches[n], n, slot, b)
                return f

            def lower_chunk(n, src, hi, lo, c):
                dve.wait_ge(op_hi, 4 * n + c + 1)
                t = slice(4 * c, 4 * c + 4)
                dve.tensor_tensor(lo[:, t, :], src[:, t, :], hi[:, t, :].bitcast(f32), ALU.subtract).then_inc(op_lo, 1)

            def operand(n, src, hi, lo):
                def f():
                    for c in range(3 if n == 0 else 4):
                        lower_chunk(n, src, hi, lo, c)
                return f

            def out2_events(slot, b):
                if slot in (3, 7):
                    o, p = taken(out2, b, slot), slot // 4
                    dve.tensor_copy(qm[:, ix(b(4, 2 * p), 2), :], o).then_inc(evac[p], 1)

            def mixed():
                dve.wait_ge(stat_root, 6)
                link(dve.reciprocal(rms[:, 0, :], rms[:, 1, :]))
                for c in range(5):
                    if c < 4:
                        for k in range(4 * c, 4 * c + 4):
                            ins = dve.scalar_tensor_tensor(qm[:, k, :], qm[:, k, :], vec("mix_post", k, 1), rms[:, 0, :],
                                                           ALU.mult, ALU.mult)
                        link(ins)
                        t = slice(4 * c, 4 * c + 4)
                        dve.tensor_tensor(H[:, t, :], H[:, t, :], qm[:, t, :], ALU.add).then_inc(post_added, 1)
                    if c > 0:
                        gained_lower(c - 1)

            def gained_lower(c):
                dve.wait_ge(pre_hi, c + 1)
                for k in range(4 * c, 4 * c + 4):
                    ins = dve.scalar_tensor_tensor(XL[:, k, :], H[:, k, :], vec("mlp_pre", k, 1), XH[:, k, :].bitcast(f32),
                                                   ALU.mult, ALU.subtract)
                ins.then_inc(pre_lo, 1)

            def up2_events(g, first):
                def f(slot, b):
                    if slot in (3, 7):
                        p = slot // 4
                        o = taken(g, b, slot)
                        if slot == 3 and first == 0 and isinstance(b(), int) and b() == 0:
                            dve.wait_ge(stat_root, 7)
                            link(dve.reciprocal(rms[:, 0, :], rms[:, 1, :]))
                        wait(dve, up_lo, b(2, first + p))
                        dve.tensor_tensor(up_space, o, row(rms[:, 0, :]), ALU.mult).then_inc(evac[p], 1)
                        wait(dve, evac[p], b(1, g.first + 1))
                        dve.scalar_tensor_tensor(up_space, up_space, 0.0, up_space, ALU.max, ALU.mult).then_inc(up_sq, 1)
                        wait(dve, up_hi, b(2, first + p + 1))
                        t = ix(b(4, 2 * p), 2)
                        dve.tensor_tensor(UL[:, t, :], up_space, UH[:, t, :].bitcast(f32), ALU.subtract).then_inc(up_lo, 1)
                return f

            def down2_events(g, n):
                def f(slot, b):
                    if slot in (3, 7):
                        o, p = taken(g, b, slot), slot // 4
                        y = qm[:, ix(b(4, 2 * p), 2), :]
                        if n == 0:
                            dve.tensor_copy(y, o).then_inc(evac[p], 1)
                        else:
                            dve.tensor_tensor(y, y, o, ALU.add).then_inc(evac[p], 1)
                return f

            late = stream(dve, lru_in, lower, late, lru_in_events)
            late = stream(dve, lru_gate, lower, late, lru_gate_events)
            late = stream(dve, in_q2, lower, late, q2_events)
            late = stream(dve, in_k2, lower, late, k2_events)
            late = stream(dve, in_v2, lower, late, v2_events)
            late = stream(dve, in_qm, lower, late, qm_events)
            dve.wait_ge(mask2_in, 16)
            late = stream(dve, branches[0], lower, late, branch_events(0))
            late = stream(dve, branches[1], lower, late, branch_events(1), tail=operand(0, q_late, UH, UL))
            late = stream(dve, branches[2], lower, late, branch_events(2), tail=operand(1, qm, UH, UL))
            late = stream(dve, out2, lower, late, out2_events, tail=operand(2, merged, XH, XL))
            for n, (up, down) in enumerate(ffn2):
                late = stream(dve, up, lower, late, up2_events(up, 8 * n), tail=mixed if n == 0 else None)
                late = stream(dve, down, lower, late, down2_events(down, n))
            for slot in range(SLOTS - LAG, SLOTS):
                late[0](slot, late[1])
            dve.wait_ge(stat_root, 8)
            link(dve.reciprocal(rms[:, 0, :], rms[:, 1, :]))
            for c in range(4):
                for k in range(4 * c, 4 * c + 4):
                    ins = dve.scalar_tensor_tensor(qm[:, k, :], qm[:, k, :], vec("mlp_post", k, 1), rms[:, 0, :], ALU.mult, ALU.mult)
                link(ins)
                t = slice(4 * c, 4 * c + 4)
                dve.tensor_tensor(H[:, t, :], H[:, t, :], qm[:, t, :], ALU.add).then_inc(x_final, 1)

        @block.gpsimd
        def _(pool):
            links = [0]

            def link(ins):
                links[0] += 1
                ins.then_inc(pool_link, 1)
                pool.wait_ge(pool_link, links[0])

            def sum_chunk(src, dst, zeroed):
                link(pool.tensor_tensor(squares, src, src, ALU.mult))
                for k in range(4):
                    if not zeroed and k == 0:
                        link(pool.tensor_copy(dst, squares[:, 0, :]))
                    else:
                        link(pool.tensor_tensor(dst, dst, squares[:, k, :], ALU.add))

            pool.dma_start(c_stage[:, :, :], A["c_re_im"][0]).then_inc(cs_in, 16)
            pool.memset(consts[:, 2:3], MAGIC)
            link(pool.memset(ones[:, :], 1.0))
            for n in range(4):
                pool.wait_ge(x_in[n], 16)
                sum_chunk(H[:, 4 * n:4 * n + 4, :], acc[:, 0, :], n > 0)
            pool.memset(small[:, 23, 0:1], 0.0).then_inc(stat_in, 1)
            for n in range(4):
                pool.wait_ge(mem_in[n], 16)
                link(pool.tensor_tensor(squares, mem_raw[n], mem_raw[n], ALU.mult))
                for k in range(4):
                    if n + k == 0:
                        link(pool.tensor_copy(acc[:, 1, :], squares[:, 0, :]))
                    else:
                        link(pool.tensor_tensor(acc[:, 1, :], acc[:, 1, :], squares[:, k, :], ALU.add))
            pool.memset(small[:, 23, 2:3], 0.0).then_inc(stat_in, 1)

            def cycles(s):
                pool.tensor_tensor(fcyc, steps[:, :], small[:, 6, ix(s())].to_broadcast([P, T]), ALU.mult).then_inc(cyc_half, 1)
                wait(pool, cyc_half, s(1, 1))
                pool.tensor_tensor(kcyc, fcyc, consts[:, 2:3].to_broadcast([P, T]), ALU.add).then_inc(cyc_done, 1)

            def pair(q, i, last=False, last_but_one=False):
                s = q.times(4).plus(i)
                wait(pool, pq_done, s(1, 1))
                pool.tensor_tensor(state_g[:, 0, :], prod_c[:, 0, :], prod_s[:, 1, :], ALU.add)
                pool.tensor_tensor(state_g[:, 1, :], prod_s[:, 0, :], prod_c[:, 1, :], ALU.subtract).then_inc(gin_done, 1)
                if i == 3 and not last:
                    pool.dma_start(b_stage[:, :, :], bt_scratch[ix(q(1, 1))].rearrange("a p k n -> p (a k) n")).then_inc(bs_in, 16)
                wait(pool, y_done, s())
                if i == 0 and not (isinstance(q(), int) and q() == 0):
                    pool.dma_start(c_stage[:, :, :], A["c_re_im"][ix(q())].rearrange("a p k n -> p (a k) n")).then_inc(cs_in, 16)
                wait(pool, pq2_done, s(1, 1))
                pool.tensor_tensor(state_h[:, 0, :], prod_c[:, 0, :], prod_s[:, 1, :], ALU.add)
                pool.tensor_tensor(state_h[:, 1, :], prod_c[:, 1, :], prod_s[:, 0, :], ALU.subtract).then_inc(h_done, 1)
                if not (last or last_but_one):
                    wait(pool, trig_done, s(1, 2))
                    cycles(s.plus(2))

            pool.wait_ge(bt_out, 16)
            pool.dma_start(b_stage[:, :, :], bt_scratch[0]).then_inc(bs_in, 16)
            cycles(At(None, 0, 0))
            pool.wait_ge(trig_done, 1)
            cycles(At(None, 0, 1))
            for i in range(4):
                pair(At(None, 0, 0), i)
            with pool.Fori(1, UT - 1) as r:
                for i in range(4):
                    pair(At(r, 1, 0), i)
            for i in range(4):
                pair(At(None, 0, UT - 1), i, last=i == 3, last_but_one=i == 2)

            def sum_two(src, dst, value):
                pool.wait_ge(sq_step, value)
                t = src()
                pool.tensor_tensor(squares[:, 0:2, :], t, t, ALU.mult).then_inc(sq_step, 1)
                pool.wait_ge(sq_step, value + 1)
                pool.tensor_tensor(dst, dst, squares[:, 0, :], ALU.add).then_inc(sq_step, 1)
                pool.wait_ge(sq_step, value + 2)
                pool.tensor_tensor(dst, dst, squares[:, 1, :], ALU.add).then_inc(sq_step, 1)

            for n in range(2):
                pool.wait_ge(memkv_out[n], 16 * 8)
            pool.wait_ge(stat_mm, 2)
            pool.memset(acc[:, :, :], 0.0).then_inc(sq_step, 1)
            with pool.Fori(0, out_ssm.bodies) as r:
                for p in range(2):
                    pool.wait_ge(evac[p], r + (out_ssm.first + 1))
                    sum_two(lambda: H[:, bass.ds(r * 4 + 2 * p, 2), :], acc[:, 0, :], r * 6 + (3 * p + 1))
            pool.memset(small[:, 23, 3:4], 0.0).then_inc(stat_in, 1)
            pool.wait_ge(stat_mm, 3)
            link(pool.memset(acc[:, :, :], 0.0))
            pool.memset(small[:, 23, 4:5], 0.0).then_inc(res_sq, 1)
            down = ffn1[2][1]
            with pool.Fori(0, down.bodies) as r:
                for p in range(2):
                    v = 1 + 3 * 2 * out_ssm.bodies + 6 * p
                    pool.wait_ge(evac[p], r + (down.first + 1))
                    sum_two(lambda: block_sum[p], acc[:, 0, :], r * 12 + v)
                    pool.memset(small[:, 23, 4:5], 0.0).then_inc(res_sq, 1)
                    pool.wait_ge(res_done, r * 2 + (p + 1))
                    sum_two(lambda: H[:, bass.ds(r * 4 + 2 * p, 2), :], acc[:, 1, :], r * 12 + (v + 3))
            pool.memset(small[:, 23, 5:6], 0.0).then_inc(stat_in, 1)

            pool.wait_ge(lru_consts, 1)
            for n in range(2):
                pool.dma_start(lru_weights[n], A["w_lru_gates"][n]).then_inc(lw_in[n], 16)

            def lru(c, gelus, last=False):
                for n in range(2):
                    wait(pool, sig_gates, c(2, n + 1))
                    pool.tensor_tensor(lru_i[n], lru_i[n], lru_xc[n].unsqueeze(1).to_broadcast([P, 2, T]), ALU.mult).then_inc(gated_in, 1)
                if not last:
                    for n in range(2):
                        wait(pool, lru_mm, c(2, n + 1))
                        pool.dma_start(lru_weights[n], A["w_lru_gates"][ix(c(2, 2 + n))].rearrange("a p m n -> p (a m) n"))\
                            .then_inc(lw_in[n], 16)
                for n in range(2):
                    wait(pool, decays, c(2, n + 1))
                    pool.tensor_tensor(lru_tmp[n], lru_a[n], lru_a[n], ALU.mult).then_inc(a_squared, 1)
                for n in range(2):
                    wait(pool, scans_done, c(2, n + 1))
                    pool.tensor_tensor(lru_w[n][:, 0, :], lru_w[n][:, 0, :], lru_w[n][:, 1, :], ALU.add).then_inc(dirs_summed, 1)
                for n in range(2):
                    wait(pool, dirs_summed, c(2, n + 1))
                    wait(pool, gr_done, gelus)
                    y = gr[:, ix(c(2, n)), :].rearrange("p a t -> p (a t)")
                    pool.tensor_tensor(y, lru_w[n][:, 0, :], y, ALU.mult).then_inc(lru_y, 1)

            lru(At(None, 0, 0), 1)
            with pool.Fori(1, 4) as r:
                lru(At(r, 1, 0), r + 1)
            with pool.Fori(4, 7) as r:
                lru(At(r, 1, 0), 4)
            lru(At(None, 0, 7), 4, last=True)
            pool.wait_ge(lru_mm, 16)
            pool.dma_start(masks[:, 0, :], A["mask2"]).then_inc(mask2_in, 16)
            pool.wait_ge(oh_done, HEADS)
            with pool.Fori(0, 4) as r:
                pool.wait_ge(pv_done, r + HEADS)
                for n in range(2):
                    pool.dma_start(mk[:, 2 * n:2 * n + 2, :], memk_scratch[bass.ds(r * 2 + n, 1)].rearrange("a p k t -> p (a k) t"))\
                        .then_inc(mkv_in, 16)
                    pool.dma_start(mv[:, 2 * n:2 * n + 2, :], memv_scratch[bass.ds(r * 2 + n, 1)].rearrange("a p k t -> p (a k) t"))\
                        .then_inc(mkv_in, 16)

            def sum_tiles(src, g, v0):
                link(pool.memset(acc[:, 0, :], 0.0))
                with pool.Fori(0, g.bodies) as r:
                    for p in range(2):
                        pool.wait_ge(evac[p], r + (g.first + 1))
                        v = v0 + 3 * p
                        pool.wait_ge(sq_step, r * 6 + v)
                        t = src[:, bass.ds(r * 4 + 2 * p, 2), :]
                        pool.tensor_tensor(squares[:, 0:2, :], t, t, ALU.mult).then_inc(sq_step, 1)
                        pool.wait_ge(sq_step, r * 6 + (v + 1))
                        pool.tensor_tensor(acc[:, 0, :], acc[:, 0, :], squares[:, 0, :], ALU.add).then_inc(sq_step, 1)
                        pool.wait_ge(sq_step, r * 6 + (v + 2))
                        pool.tensor_tensor(acc[:, 0, :], acc[:, 0, :], squares[:, 1, :], ALU.add).then_inc(sq_step, 1)
                pool.memset(small[:, 23, 6:7], 0.0).then_inc(stat_in, 1)
                return v0 + 6 * g.bodies

            pool.wait_ge(oh_done, HEADS + 4)
            steps_done = sum_tiles(qm, out2, 1 + 18 * out_ssm.bodies)
            pool.wait_ge(stat_mm, 6)
            for c in range(4):
                pool.wait_ge(post_added, c + 1)
                sum_chunk(H[:, 4 * c:4 * c + 4, :], acc[:, 0, :], c > 0)
            pool.memset(small[:, 23, 7:8], 0.0).then_inc(stat_in, 1)
            pool.wait_ge(stat_mm, 7)
            sum_tiles(qm, ffn2[3][1], steps_done)


def tiled(w):
    k, n = w.shape
    kt = k // P // UNITS
    return np.ascontiguousarray(w.reshape(UNITS, kt, P, n // GC, GC).transpose(3, 0, 2, 1, 4)
                                .reshape(n // GC, UNITS, P, kt * GC))


def paired(a, b):
    a, b = tiled(a), tiled(b)
    return np.ascontiguousarray(np.stack([a, b], 1).reshape(2 * a.shape[0], *a.shape[1:]))


def by_partition(v, n=None):
    return v.reshape(-1, P).T


def laid_out(i):
    A = {}
    A["x"] = i["x"][0].T.reshape(KT, P, T).transpose(1, 0, 2)
    A["mem"] = i["mem_2"][0].T.reshape(KT, P, T).transpose(1, 0, 2)
    w = i["w_in"][0]
    A["w_in_u"], A["w_in_qk"], A["w_in_v"] = tiled(w[:, 3 * AW:]), tiled(w[:, :2 * AW]), tiled(w[:, 2 * AW:3 * AW])
    A["w_mem_k"], A["w_mem_v"] = tiled(i["w_mem_kv_2"][0][:, :D]), tiled(i["w_mem_kv_2"][0][:, D:])
    A["w_out_attn"], A["w_out_ssm"] = tiled(i["w_out"][0][:AW]), tiled(i["w_out"][0][AW:])
    A["w_glu"] = tiled(i["w_glu"][0])
    for c, (a, b) in enumerate(((0, 2048), (2048, 4096), (4096, FF1))):
        A[f"w_gu{c}"] = paired(i["w_gate"][0][:, a:b], i["w_up"][0][:, a:b])
        A[f"w_dn{c}"] = tiled(i["w_down"][0][a:b])
    at = {}
    start = 0
    for name, n in (("xr", D), ("gr", D), ("q", D), ("k", 512), ("v", 512), ("qm", D), ("g0", D), ("g1", D), ("g2", D)):
        at[name] = i["w_in_2"][0][:, start:start + n]
        start += n
    A["w_lru_in"], A["w_lru_gate"], A["w_in_q2"] = tiled(at["xr"]), tiled(at["gr"]), tiled(at["q"])
    A["w_in_k2"], A["w_in_v2"], A["w_in_qm"] = tiled(at["k"]), tiled(at["v"]), tiled(at["qm"])
    for n, name in enumerate(("w_br_lru_2", "w_br_attn_2", "w_br_mem_2")):
        A[f"w_branch{n}"] = paired(at[f"g{n}"], i[name][0])
    A["w_out2"] = tiled(i["w_out_2"][0])
    for c in range(4):
        A[f"w_up{c}"] = tiled(i["w_up_2"][0][:, D * c:D * c + D])
        A[f"w_down{c}"] = tiled(i["w_down_2"][0][D * c:D * c + D])
    A["w_lru_gates"] = np.stack([i[n][0] for n in ("wr_f_2", "wr_b_2", "wi_f_2", "wi_b_2")], 2)
    A["positions"] = np.broadcast_to(i["positions_2"].astype(np.int32).reshape(1, T), (P, T))
    v = {"norm1": i["norm1_g"][0], "norm2": i["norm2_g"][0], "final": i["final_g"], "mem": i["norm_mem_2"][0],
         "mix_pre": i["norm_mix_pre_2"][0], "mix_post": i["norm_mix_post_2"][0], "mlp_pre": i["norm_mlp_pre_2"][0],
         "mlp_post": i["norm_mlp_post_2"][0], "b_glu": i["b_glu"][0], "d_skip": i["d_skip"][0].reshape(-1),
         "a_re": i["a_re"][0].reshape(-1), "a_im": i["a_im"][0].reshape(-1), "log_dt": np.repeat(i["log_dt"][0], 64),
         "b_gate": i["b_gate_2"][0], "conv_w": i["conv_w_2"][0].reshape(-1), "conv_b": i["conv_b_2"][0],
         "br": np.concatenate([i["br_f_2"][0].reshape(-1), i["br_b_2"][0].reshape(-1)]),
         "bi": np.concatenate([i["bi_f_2"][0].reshape(-1), i["bi_b_2"][0].reshape(-1)]),
         "lam": np.concatenate([i["lam_f_2"][0], i["lam_b_2"][0]])}
    cols = []
    for name, (_, n) in VEC.items():
        if name == "sink":
            cols.append(np.broadcast_to(i["attn_sink_2"][0][None, :], (P, n)))
        elif name == "freq":
            half = HD // 2
            f = (10000.0 ** (-np.arange(half, dtype=np.float32) / np.float32(half))).astype(np.float32)
            cols.append(np.concatenate([f, f])[:, None])
        else:
            cols.append(by_partition(v[name]))
    A["vecs"] = np.concatenate(cols, 1)
    A["ident"] = np.eye(P, dtype=np.float32)
    rot = np.zeros((P, P), np.float32)
    for a in range(16):
        rot[a + 16, a], rot[a, a + 16] = -1.0, 1.0
    A["rotate1"] = rot
    rot2 = np.zeros((P, P), np.float32)
    for a in range(64):
        rot2[a + 64, a], rot2[a, a + 64] = -1.0, 1.0
    A["rotate2"] = rot2
    near = np.abs(np.arange(T)[:, None] - np.arange(T)[None, :]) <= 128
    A["mask2"] = np.where(near, 0.0, NEG).astype(np.float32).reshape(2, P, T).transpose(1, 0, 2).reshape(P, 2 * T)
    A["steps"] = np.broadcast_to(np.arange(T, dtype=np.float32)[None, :], (P, T))
    inv = (500000.0 ** (-np.arange(0, 32, 2) / 32)).astype(np.float32)
    ang = (np.arange(T, dtype=np.float32)[:, None] * inv[None, :]).astype(np.float64)
    cs = np.zeros((P, 2, T), np.float32)
    cs[:, 0] = 1.0
    for a in (0, 16):
        cs[a:a + 16, 0], cs[a:a + 16, 1] = np.cos(ang).T, np.sin(ang).T
    A["cos_sin"] = cs
    q = np.arange(T)[:, None]
    k = np.arange(T)[None, :]
    count = sum(((k <= q) & ((q - k) % d == 0) & (q - k <= w)).astype(np.float32) for w, d in ((128, 1), (512, 4), (2048, 16)))
    both = np.stack([np.where(count > 0, 0.0, NEG).astype(np.float32), count])
    A["masks1"] = both.reshape(2, 2, P, T).transpose(2, 0, 1, 3).reshape(P, 2, 2 * T)
    for name, b in (("b_re", i["b_re"][0]), ("b_im", i["b_im"][0])):
        m = np.zeros((2, 64, PAIRS, 2, 16), np.float32)
        for g in range(2):
            m[g, :, :, g, :] = b.reshape(PAIRS, 2, 64, 16)[:, g].transpose(1, 0, 2)
        A[name] = m.reshape(P, PAIRS, 32)
    cc = np.zeros((UT, 2, 64, 2, 4, 2, 16), np.float32)
    for r, c in enumerate((i["c_re"][0], i["c_im"][0])):
        for g in range(2):
            cc[:, g, :, r, :, g, :] = c.reshape(UT, 4, 2, 16, 64)[:, :, g].transpose(0, 3, 1, 2)
    A["c_re_im"] = cc.reshape(UT, P, 2, P)
    return {k: np.ascontiguousarray(v, dtype=np.float32) if v.dtype.kind == "f" else np.ascontiguousarray(v)
            for k, v in A.items()}


def kernel(**inputs):
    import concourse.bacc as bacc
    from concourse.bass_utils import run_bass_kernel_spmd

    nc = bacc.Bacc("TRN2", target_bir_lowering=False, num_devices=1, dynamic_dma_scratch_size=4096)
    arrays = laid_out({k: np.asarray(v) for k, v in inputs.items()})
    aps = {k: nc.dram_tensor("in_" + k, v.shape, mybir.dt.from_np(v.dtype), kind="ExternalInput").ap()
           for k, v in arrays.items()}
    out = nc.dram_tensor("out_x", (P, KT, T), mybir.dt.float32, kind="ExternalOutput").ap()
    program(nc, aps, out)
    got = run_bass_kernel_spmd(nc, [{"in_" + k: v for k, v in arrays.items()}], core_ids=[0]).results[0]["out_x"]
    return np.ascontiguousarray(got.transpose(1, 0, 2).reshape(D, T).T[None])
```
